# Optimizing a Trainium2 kernel written in Bass

```python
import math
import jax, jax.numpy as jnp
from jax import lax
import numpy as np

D_MODEL = 1024
BATCH = 1
SEQ = 256
DEPTH = 2

N_A = DEPTH // 2
N_B = DEPTH - N_A
N_DENSE = (DEPTH + 1) // 2
N_MOE = DEPTH // 2

MEM_LEN = 256
HEAD_DIM = 64
MEM_HEADS = 4
MEM_DIM = MEM_HEADS * HEAD_DIM
MIX_DIM = D_MODEL - MEM_DIM

GLA_HEADS = 4
GLA_DV = MIX_DIM // GLA_HEADS
GLA_DK = GLA_DV // 2
GLA_KDIM = GLA_HEADS * GLA_DK
GLA_GATE_RANK = 16
GLA_GATE_NORM = 16.0
GLA_CHUNK = 64

DIFF_HEADS = MIX_DIM // (2 * HEAD_DIM)
DIFF_VDIM = 2 * HEAD_DIM
Q_BLOCK = 128
ROPE_THETA = 10000.0

FFN_DENSE = 2816
N_EXPERTS = 8
TOP_K = 2
FFN_EXPERT = 3584
MOE_BLOCK = 256
EPS = 1e-6

A_SPLITS = (GLA_KDIM, 2 * GLA_KDIM, 2 * GLA_KDIM + MIX_DIM, 2 * GLA_KDIM + 2 * MIX_DIM,
            2 * GLA_KDIM + 2 * MIX_DIM + GLA_GATE_RANK)
W_IN_A = 2 * GLA_KDIM + 2 * MIX_DIM + GLA_GATE_RANK + MEM_DIM
W_IN_B = MIX_DIM + MEM_DIM

kernel_name = "yoco_gla_diffattn_moe_memory"

def rmsnorm(x, g):
    xf = x.astype(jnp.float32)
    y = xf * lax.rsqrt(jnp.mean(xf * xf, axis=-1, keepdims=True) + EPS)
    return (y * g.astype(jnp.float32)).astype(x.dtype)

def rope(x, pos):
    half = x.shape[-1] // 2
    inv = ROPE_THETA ** (-jnp.arange(half, dtype=jnp.float32) / half)
    ang = pos.astype(jnp.float32)[:, None] * inv[None, :]
    cos = jnp.cos(ang)[None, :, None, :]
    sin = jnp.sin(ang)[None, :, None, :]
    x1 = x[..., :half].astype(jnp.float32)
    x2 = x[..., half:].astype(jnp.float32)
    out = jnp.concatenate([x1 * cos - x2 * sin, x1 * sin + x2 * cos], axis=-1)
    return out.astype(x.dtype)

def gla_chunked(q, k, v, gk):
    B, S, H, dk = q.shape
    dv = v.shape[-1]
    N = S // GLA_CHUNK

    def chunks(t):
        return t.astype(jnp.float32).reshape(B, N, GLA_CHUNK, H, t.shape[-1]).transpose(0, 3, 1, 2, 4)

    q = chunks(q) * GLA_DK ** -0.5
    k = chunks(k)
    v = chunks(v)
    b = jnp.cumsum(chunks(gk), axis=3)
    b_last = b[:, :, :, -1:, :]
    b_ref = b[:, :, :, GLA_CHUNK // 2 - 1:GLA_CHUNK // 2, :]
    mask = jnp.tril(jnp.ones((GLA_CHUNK, GLA_CHUNK), dtype=bool))
    scores = jnp.einsum('bhnid,bhnjd->bhnij', q * jnp.exp(b - b_ref), k * jnp.exp(b_ref - b))
    scores = jnp.where(mask, scores, 0.0)
    o_intra = jnp.einsum('bhnij,bhnjv->bhniv', scores, v)
    kv = jnp.einsum('bhncd,bhncv->nbhdv', k * jnp.exp(b_last - b), v)
    decay = jnp.exp(b_last[:, :, :, 0, :]).transpose(2, 0, 1, 3)

    def step(state, inp):
        kv_n, dec_n = inp
        return dec_n[..., None] * state + kv_n, state

    _, states = lax.scan(step, jnp.zeros((B, H, dk, dv), jnp.float32), (kv, decay))
    o_inter = jnp.einsum('bhnid,nbhdv->bhniv', q * jnp.exp(b), states)
    o = o_intra + o_inter
    return o.transpose(0, 2, 3, 1, 4).reshape(B, S, H, dv)

def memory_attention(q_mem, mem, w_mem_kv):
    B, S = q_mem.shape[:2]
    kv = mem.astype(q_mem.dtype) @ w_mem_kv
    M = kv.shape[1]
    k = kv[..., :MEM_DIM].reshape(B, M, MEM_HEADS, HEAD_DIM)
    v = kv[..., MEM_DIM:].reshape(B, M, MEM_HEADS, HEAD_DIM)
    s = jnp.einsum('bshd,bmhd->bhsm', q_mem, k).astype(jnp.float32) * HEAD_DIM ** -0.5
    p = jax.nn.softmax(s, axis=-1).astype(v.dtype)
    return jnp.einsum('bhsm,bmhd->bshd', p, v).reshape(B, S, MEM_DIM)

def diff_attention(q, k, v, lam, lambda_init, g_subln):
    B, S, H2, d = q.shape
    H = H2 // 2
    n_blk = S // Q_BLOCK
    qb = q.reshape(B, n_blk, Q_BLOCK, H2, d).transpose(1, 0, 2, 3, 4)
    kpos = jnp.arange(S)

    def block(args):
        qi, i = args
        s = jnp.einsum('bqhd,bkhd->bhqk', qi, k).astype(jnp.float32) * d ** -0.5
        qpos = i * Q_BLOCK + jnp.arange(Q_BLOCK)
        s = jnp.where(kpos[None, :] <= qpos[:, None], s, -jnp.inf)
        p = jax.nn.softmax(s, axis=-1).reshape(B, H, 2, Q_BLOCK, S)
        a = p[:, :, 0] - lam * p[:, :, 1]
        return jnp.einsum('bhqk,bkhe->bqhe', a.astype(v.dtype), v)

    o = lax.map(block, (qb, jnp.arange(n_blk)))
    o = o.transpose(1, 0, 2, 3, 4).reshape(B, S, H, 2 * d)
    o = rmsnorm(o, g_subln) * (1.0 - lambda_init)
    return o.reshape(B, S, H * 2 * d)

def gla_group(h, mem, w_in, w_gk_up, b_gk, g_gla, w_mem_kv):
    B, S, _ = h.shape
    q, k, v, g_out, gk_low, q_mem = jnp.split(h @ w_in, A_SPLITS, axis=-1)
    gk = jax.nn.log_sigmoid((gk_low @ w_gk_up + b_gk).astype(jnp.float32)) / GLA_GATE_NORM
    o = gla_chunked(q.reshape(B, S, GLA_HEADS, GLA_DK), k.reshape(B, S, GLA_HEADS, GLA_DK),
                    v.reshape(B, S, GLA_HEADS, GLA_DV), gk.reshape(B, S, GLA_HEADS, GLA_DK))
    o = rmsnorm(o.astype(h.dtype), g_gla) * jax.nn.silu(g_out.reshape(B, S, GLA_HEADS, GLA_DV))
    m = memory_attention(q_mem.reshape(B, S, MEM_HEADS, HEAD_DIM), mem, w_mem_kv)
    return jnp.concatenate([o.reshape(B, S, MIX_DIM), m], axis=-1)

def diff_group(h, mem, k_shared, v_shared, w_in, lq1, lk1, lq2, lk2, g_subln, w_mem_kv,
               lambda_init, pos):
    B, S, _ = h.shape
    proj = h @ w_in
    q = rope(proj[..., :MIX_DIM].reshape(B, S, 2 * DIFF_HEADS, HEAD_DIM), pos)
    q_mem = proj[..., MIX_DIM:].reshape(B, S, MEM_HEADS, HEAD_DIM)
    lam = (jnp.exp(jnp.sum(lq1.astype(jnp.float32) * lk1.astype(jnp.float32)))
           - jnp.exp(jnp.sum(lq2.astype(jnp.float32) * lk2.astype(jnp.float32))) + lambda_init)
    o = diff_attention(q, k_shared, v_shared, lam, lambda_init, g_subln)
    m = memory_attention(q_mem, mem, w_mem_kv)
    return jnp.concatenate([o, m], axis=-1)

def swiglu(h, w_gate, w_up, w_down):
    return (jax.nn.silu(h @ w_gate) * (h @ w_up)) @ w_down

def moe_swiglu(h, w_router, w_gate, w_up, w_down):
    B, S, D = h.shape
    T = B * S
    A = T * TOP_K
    x = h.reshape(T, D)
    logits = (x @ w_router).astype(jnp.float32)
    top_logit, top_idx = lax.top_k(logits, TOP_K)
    gates = jax.nn.softmax(top_logit, axis=-1)
    expert = top_idx.reshape(A)
    token = jnp.repeat(jnp.arange(T, dtype=jnp.int32), TOP_K)
    gate = gates.reshape(A).astype(h.dtype)
    order = jnp.argsort(expert)
    e_sorted, t_sorted, g_sorted = expert[order], token[order], gate[order]
    counts = jnp.bincount(expert, length=N_EXPERTS)
    padded = (counts + MOE_BLOCK - 1) // MOE_BLOCK * MOE_BLOCK
    start = jnp.cumsum(counts) - counts
    pend = jnp.cumsum(padded)
    pstart = pend - padded
    dest = pstart[e_sorted] + jnp.arange(A, dtype=jnp.int32) - start[e_sorted]
    n_blocks = (A + MOE_BLOCK - 1) // MOE_BLOCK + N_EXPERTS
    L = n_blocks * MOE_BLOCK
    rows_token = jnp.zeros((L,), jnp.int32).at[dest].set(t_sorted)
    rows_gate = jnp.zeros((L,), h.dtype).at[dest].set(g_sorted)
    xs = x[rows_token].reshape(n_blocks, MOE_BLOCK, D)
    block_expert = jnp.clip(jnp.searchsorted(pend, jnp.arange(n_blocks) * MOE_BLOCK, side='right'),
                            0, N_EXPERTS - 1)

    def run(args):
        xb, e = args
        return swiglu(xb, w_gate[e], w_up[e], w_down[e])

    ys = lax.map(run, (xs, block_expert)).reshape(L, D)
    out = jnp.zeros((T, D), h.dtype).at[rows_token].add(ys * rows_gate[:, None])
    return out.reshape(B, S, D)

def setup_inputs(seed: int = 0) -> dict:
    key = jax.random.key(seed)
    ks = list(jax.random.split(key, 32))
    it = iter(ks)

    def normal(shape, scale):
        return jax.random.normal(next(it), shape, jnp.float32) * scale

    def w(shape, fan_in):
        return normal(shape, fan_in ** -0.5)

    def gain(shape):
        return 1.0 + normal(shape, 0.02)

    return {
        "x": normal((BATCH, SEQ, D_MODEL), 1.0),
        "mem": normal((BATCH, MEM_LEN, D_MODEL), 1.0),
        "g_mix": gain((DEPTH, D_MODEL)),
        "g_ffn": gain((DEPTH, D_MODEL)),
        "w_mem_kv": w((DEPTH, D_MODEL, 2 * MEM_DIM), D_MODEL),
        "w_out": w((DEPTH, D_MODEL, D_MODEL), D_MODEL),
        "w_in_a": w((N_A, D_MODEL, W_IN_A), D_MODEL),
        "w_gk_up": w((N_A, GLA_GATE_RANK, GLA_KDIM), GLA_GATE_RANK),
        "b_gk": normal((N_A, GLA_KDIM), 0.01),
        "g_gla": gain((N_A, GLA_DV)),
        "g_kv": gain((D_MODEL,)),
        "w_kv": w((D_MODEL, 2 * MIX_DIM), D_MODEL),
        "w_in_b": w((N_B, D_MODEL, W_IN_B), D_MODEL),
        "lambda_q1": normal((N_B, HEAD_DIM), 0.1),
        "lambda_k1": normal((N_B, HEAD_DIM), 0.1),
        "lambda_q2": normal((N_B, HEAD_DIM), 0.1),
        "lambda_k2": normal((N_B, HEAD_DIM), 0.1),
        "g_subln": gain((N_B, DIFF_VDIM)),
        "w_dense_gate": w((N_DENSE, D_MODEL, FFN_DENSE), D_MODEL),
        "w_dense_up": w((N_DENSE, D_MODEL, FFN_DENSE), D_MODEL),
        "w_dense_down": w((N_DENSE, FFN_DENSE, D_MODEL), FFN_DENSE),
        "w_router": w((N_MOE, D_MODEL, N_EXPERTS), D_MODEL),
        "w_exp_gate": w((N_MOE, N_EXPERTS, D_MODEL, FFN_EXPERT), D_MODEL),
        "w_exp_up": w((N_MOE, N_EXPERTS, D_MODEL, FFN_EXPERT), D_MODEL),
        "w_exp_down": w((N_MOE, N_EXPERTS, FFN_EXPERT, D_MODEL), FFN_EXPERT),
        "g_final": gain((D_MODEL,)),
    }

def reference(x, mem, g_mix, g_ffn, w_mem_kv, w_out, w_in_a, w_gk_up, b_gk, g_gla, g_kv, w_kv,
              w_in_b, lambda_q1, lambda_k1, lambda_q2, lambda_k2, g_subln, w_dense_gate,
              w_dense_up, w_dense_down, w_router, w_exp_gate, w_exp_up, w_exp_down, g_final):
    B, S, _ = x.shape
    pos = jnp.arange(S)
    k_shared = None
    v_shared = None
    for l in range(DEPTH):
        h = rmsnorm(x, g_mix[l])
        if l < N_A:
            mixed = gla_group(h, mem, w_in_a[l], w_gk_up[l], b_gk[l], g_gla[l], w_mem_kv[l])
        else:
            j = l - N_A
            lambda_init = 0.8 - 0.6 * math.exp(-0.3 * l)
            mixed = diff_group(h, mem, k_shared, v_shared, w_in_b[j], lambda_q1[j], lambda_k1[j],
                               lambda_q2[j], lambda_k2[j], g_subln[j], w_mem_kv[l], lambda_init, pos)
        x = x + mixed @ w_out[l]
        h = rmsnorm(x, g_ffn[l])
        if l % 2 == 0:
            i = l // 2
            x = x + swiglu(h, w_dense_gate[i], w_dense_up[i], w_dense_down[i])
        else:
            i = l // 2
            x = x + moe_swiglu(h, w_router[i], w_exp_gate[i], w_exp_up[i], w_exp_down[i])
        if l == N_A - 1:
            kv = rmsnorm(x, g_kv) @ w_kv
            k_shared = rope(kv[..., :MIX_DIM].reshape(B, S, 2 * DIFF_HEADS, HEAD_DIM), pos)
            v_shared = kv[..., MIX_DIM:].reshape(B, S, DIFF_HEADS, DIFF_VDIM)
    return rmsnorm(x, g_final)


_drawn_inputs = setup_inputs


def setup_inputs(seed=0):
    import zlib

    import numpy as np

    out = dict(_drawn_inputs(seed))
    spreads = {}
    factors = {'b_gk': 8.0, 'g_kv': 3.203, 'g_subln': 2.723, 'g_final': 2.809}
    for name, (base, spread) in spreads.items():
        noise = np.random.default_rng([zlib.crc32(name.encode()), seed]).standard_normal(out[name].shape)
        drawn = base * np.exp(spread * noise) if base else spread * noise
        out[name] = __import__('jax').numpy.asarray(drawn.astype(out[name].dtype))
    for name, factor in factors.items():
        out[name] = (out[name] * factor).astype(out[name].dtype)
    return out
```

```python
import math
from contextlib import ExitStack

import concourse.bass as bass
from concourse import mybir

F32 = mybir.dt.float32
F32R = mybir.dt.float32r
U32 = mybir.dt.uint32
I32 = mybir.dt.int32
ALU = mybir.AluOpType
ACT = mybir.ActivationFunctionType
AX = mybir.AxisListType

P = 128
D = 1024
S = 256
KT = D // P
TT = S // P
MEM_HEADS, HEAD_DIM = 4, 64
MEM_DIM = MEM_HEADS * HEAD_DIM
MIX = D - MEM_DIM
GH, GDV, GDK, RANK, CHUNK = 4, 192, 96, 16, 64
NCH = S // CHUNK
DH, DV = 6, 128
F_DENSE, F_EXP, NE = 2816, 3584, 8
EPS = 1e-6
LAMBDA_INIT = 0.8 - 0.6 * math.exp(-0.3)
NEG = -3.0e38

SLOT = 2048
RAW = 7
SPLIT = 3
E_SPLIT = 6

C_ID, C_IOTA, C_STRICT, C_CAUSAL, C_GLA, C_ROPE, C_EPS = 0, 128, 384, 512, 768, 832, 960
C_N = 961


def prefill_slots(w):
    slots, first = [], {}

    def add(stage, src, k0, kt, n0, n):
        first.setdefault(stage, len(slots))
        slots.append((src, k0, kt, n0, n))

    for l in range(2):
        add("mem_kv", w["w_mem_kv"][l], 0, 8, 0, 256)
        add("mem_kv", w["w_mem_kv"][l], 0, 8, 256, 256)
    add("in_a", w["w_in_a"][0], 0, 8, 2 * GH * GDK + 2 * MIX, RANK)
    add("in_a", w["w_in_a"][0], 0, 8, W_QMEM, MEM_DIM)
    for i in range(4):
        add("in_a", w["w_in_a"][0], 0, 8, 192 * i, 192)
    for base in (768, 1536):
        add("in_a", w["w_in_a"][0], 0, 4, base, 512)
        add("in_a", w["w_in_a"][0], 4, 4, base, 512)
        add("in_a", w["w_in_a"][0], 0, 8, base + 512, 256)

    def blocks(stage, src, nb):
        for b in range(nb):
            add(stage, src, 0, 4, 512 * b, 512)
            add(stage, src, 4, 4, 512 * b, 512)

    blocks("out_a", w["w_out"][0], 2)
    n = F_DENSE // 256
    for i in range(n + 1):
        if i < n:
            add("dense", w["w_dense_gate"][0], 0, 8, 256 * i, 256)
            add("dense", w["w_dense_up"][0], 0, 8, 256 * i, 256)
        if i > 0:
            add("dense", w["w_dense_down"][0], 2 * (i - 1), 2, 0, D)
    blocks("kv", w["w_kv"], 3)
    blocks("in_b", w["w_in_b"][0], 2)
    blocks("out_b", w["w_out"][1], 2)
    add("router", w["w_router"][0], 0, 8, 0, NE)
    first["experts"] = len(slots)
    return slots, first


W_QMEM = 2 * GH * GDK + 2 * MIX + RANK
STEPS = F_EXP // 512
PER_EXPERT = 6 * STEPS


def trunk(nc, x, mem, g_mix, g_ffn, w_mem_kv, w_out, w_in_a, w_gk_up, b_gk, g_gla, g_kv, w_kv, w_in_b,
          lambda_q1, lambda_k1, lambda_q2, lambda_k2, g_subln, w_dense_gate, w_dense_up, w_dense_down,
          w_router, w_exp_gate, w_exp_up, w_exp_down, g_final, consts, out):
    W = dict(w_mem_kv=w_mem_kv, w_out=w_out, w_in_a=w_in_a, w_kv=w_kv, w_in_b=w_in_b,
             w_dense_gate=w_dense_gate, w_dense_up=w_dense_up, w_dense_down=w_dense_down, w_router=w_router)
    slots, first = prefill_slots(W)
    NPRE = first["experts"]

    with ExitStack() as ctx:
        def sb(name, shape, dt=F32):
            return ctx.enter_context(nc.sbuf_tensor(name, shape, dt))

        def sem(name):
            return ctx.enter_context(nc.semaphore(name))

        raw = sb("raw", [P, RAW, SLOT])
        act_hi = sb("act_hi", [P, KT, S], F32R)
        act_lo = sb("act_lo", [P, KT, S], F32R)
        xres = sb("xres", [P, TT, D])
        H = sb("H", [P, TT, D])
        gain = sb("gain", [P, D])
        cst = sb("cst", [P, C_N])
        ones = sb("ones", [P, P])
        small = sb("small", [P, 128])
        rsc = sb("rsc", [P, 4, TT, NE])
        bgk = sb("bgk", [GDK, GH])
        idx8 = sb("idx8", [P, TT, 8], U32)
        route_gate = sb("route_gate", [P, TT, NE + 1])
        route_rank = sb("route_rank", [P, TT, NE + 1])
        flag = sb("flag", [1, 8], I32)

        ps = ctx.enter_context(nc.psum_tensor("ps", [P, 8, 512], F32))

        with ExitStack() as prefill:
            def sbp(name, shape, dt=F32):
                return prefill.enter_context(nc.sbuf_tensor(name, shape, dt))

            w_hi = sbp("w_hi", [P, SPLIT, SLOT], F32R)
            w_lo = sbp("w_lo", [P, SPLIT, SLOT], F32R)
            T = sbp("T", [P, 8, D])
            v_tok = sbp("v_tok", [P, TT, MIX])
            kmT = sbp("kmT", [P, 2, 2, S])
            vm = sbp("vm", [P, 2, TT, MEM_DIM])
            qmT = sbp("qmT", [P, 2, S])
            sc = sbp("sc", [P, 3, 512])
            pT = sbp("pT", [P, 2, S])
            f_hi = sbp("f_hi", [P, 2, S], F32R)
            f_lo = sbp("f_lo", [P, 2, S], F32R)
            ggla = sbp("ggla", [P, GDV])
            gsub = sbp("gsub", [P, DV])

        e_whi = sb("e_whi", [P, E_SPLIT, SLOT], F32R)
        e_wlo = sb("e_wlo", [P, E_SPLIT, SLOT], F32R)
        oh = sb("oh", [P, TT, P])
        ohT = sb("ohT", [P, S])
        e_h = sb("e_h", [P, 512])
        y_e = sb("y_e", [P, D])
        xg_hi, xg_lo = act_hi[:, :, 0:P], act_lo[:, :, 0:P]
        h_hi, h_lo = act_hi[:, 0:4, P:S], act_lo[:, 0:4, P:S]

        ident = cst[:, C_ID:C_ID + P]
        cos_sin = cst[:, C_ROPE:C_ROPE + 128].rearrange("p (t c d) -> p t c d", t=TT, c=2)
        eps = cst[:, C_EPS:C_EPS + 1]
        ss, rms, rs = small[:, 0:2], small[:, 2:4], small[:, 4:6]
        nmax, nbias, rsum = small[:, 8:14], small[:, 14:20], small[:, 20:26]
        rinv = small[:, 26:32]
        lamc = small[:, 32:40]
        hss, hrms, hrs = small[:, 40:52], small[:, 52:64], small[:, 64:76]
        cur_rank, cur_gate = small[:, 76:78], small[:, 78:80]
        rt = small[:, 80:120]

        gq, gk_, gb, gd = (T[0:GDK, i, :] for i in range(4))
        ge, gf, qi, ki = (T[0:GDK, i, :] for i in range(4, 8))
        gla_o = T[:, 3:5, 0:MIX]
        state = T[0:GDK, 2, 0:3 * GDV].rearrange("p (n v) -> p n v", n=3)
        kdT = T[:, 2, 576:768].rearrange("p (t n) -> p t n", t=TT)
        sT = T[:, 2, 768:1024].rearrange("p (t n) -> p t n", t=TT)
        lam4 = sc[:, 0, 0:4 * HEAD_DIM].rearrange("p (i n) -> p i n", i=4)
        wgk = sc[0:RANK, 1, 0:GH * GDK]
        f_gate, f_h = T[:, 0, 0:512], T[:, 1, 0:512]
        flatT = T[:, :, :].rearrange("p a b -> p (a b)")
        k_raw = flatT[:, 0:1536].rearrange("p (t n) -> p t n", t=TT)
        q_raw = flatT[:, 1536:3072].rearrange("p (t n) -> p t n", t=TT)
        rot = flatT[:, 3072:4608].rearrange("p (t n) -> p t n", t=TT)
        kT = flatT[:, 4608:6144].rearrange("p (h s) -> p h s", h=DH)
        qT = flatT[:, 6144:7680].rearrange("p (h s) -> p h s", h=DH)
        qm_tok = flatT[:, 7680:8192].rearrange("p (t n) -> p t n", t=TT)
        rope_t = sc[:, :, :].rearrange("p a b -> p (a b)")[:, 0:1536].rearrange("p (a n) -> p a n", a=4)
        diff_o = flatT[:, 0:1536].rearrange("p (t n) -> p t n", t=TT)
        diff_sq = flatT[:, 1536:3072].rearrange("p (t n) -> p t n", t=TT)
        top8, fidx, msk, tmp8 = (rsc[:, i, :, :] for i in range(4))

        const_in = sem("const_in")
        small_in = sem("small_in")
        mem_in = sem("mem_in")
        x_in = sem("x_in")
        gain_in = sem("gain_in")
        raw_in = [sem(f"raw_in{r}") for r in range(RAW)]
        hi_ready = sem("hi_ready")
        lo_ready = sem("lo_ready")
        slot_used = sem("slot_used")
        h_ready = sem("h_ready")
        turned = sem("turned")
        turn_hi = sem("turn_hi")
        turn_lo = sem("turn_lo")
        rms_ready = sem("rms_ready")
        proj_out = sem("proj_out")
        add_done = sem("add_done")
        gk_logit = sem("gk_logit")
        gk_act = sem("gk_act")
        gk_vec = sem("gk_vec")
        gla_sc = sem("gla_sc")
        gla_sce = sem("gla_sce")
        gla_kv = sem("gla_kv")
        gla_st = sem("gla_st")
        gla_od = sem("gla_od")
        gla_oe = sem("gla_oe")
        head_sq = sem("head_sq")
        head_rms = sem("head_rms")
        roped = sem("roped")
        rope_turned = sem("rope_turned")
        rope_out = sem("rope_out")
        u_score = sem("u_score")
        u_max = sem("u_max")
        u_exp = sem("u_exp")
        u_prob = sem("u_prob")
        u_turned = sem("u_turned")
        u_pT = sem("u_pT")
        u_val = sem("u_val")
        u_out = sem("u_out")
        ff_silu = sem("ff_silu")
        ff_h = sem("ff_h")
        ff_hi = sem("ff_hi")
        ff_lo = sem("ff_lo")
        lam_v = sem("lam_v")
        lam_a = sem("lam_a")
        top_d = sem("top_d")
        top_e = sem("top_e")
        chosen = sem("chosen")
        ranks = sem("ranks")
        routed = sem("routed")
        oh_ready = sem("oh_ready")
        oh_turned = sem("oh_turned")
        ohT_ready = sem("ohT_ready")
        disp = sem("disp")
        xg_h = sem("xg_h")
        xg_l = sem("xg_l")
        e_silu = sem("e_silu")
        e_hr = sem("e_hr")
        e_tr = sem("e_tr")
        e_hi = sem("e_hi")
        e_lo = sem("e_lo")
        e_yo = sem("e_yo")
        e_comb = sem("e_comb")
        e_add = sem("e_add")
        cur_done = sem("cur_done")
        e_blank = sem("e_blank")
        dve_step = sem("dve_step")
        act_step = sem("act_step")
        out_ready = sem("out_ready")
        out_done = sem("out_done")

        def shaped(buf, i, kt, n):
            return buf[:, i, 0:kt * n].rearrange("p (k n) -> p k n", k=kt)

        def gate_end(j):
            return 2 if j == 0 else 6 * j

        def slot_shape(s):
            _, _, kt, _, n = slots[s]
            return kt, n

        units = [("mem", 0, h, t) for h in range(MEM_HEADS) for t in range(TT)]
        NU0 = len(units)
        units += [("mem", 1, h, t) for h in range(MEM_HEADS) for t in range(TT)]
        units += [("diff", 1, h, t) for h in range(DH) for t in range(TT)]
        U_BANK = {"score": (0, 6), "turn": (2, 3), "val": (4, 5)}

        def unit_parts(u):
            kind, _, _, t = units[u]
            return (1, S) if kind == "mem" else (2, P * (t + 1))

        block = ctx.enter_context(nc.Block())

        @block.sync
        def _(sp):
            sp.dma_start(H[:, :, :], mem[0].rearrange("(t p) d -> p t d", p=P)).then_inc(mem_in, 16)
            sp.dma_start(cst[:, :], consts).then_inc(const_in, 16)
            sp.dma_start(xres[:, :, :], x[0].rearrange("(t p) d -> p t d", p=P)).then_inc(x_in, 16)
            for s, (src, k0, kt, n0, n) in enumerate(slots):
                if s >= RAW:
                    sp.wait_ge(lo_ready, s - RAW + 1)
                with nc.allow_non_contiguous_dma(reason="router columns"):
                    sp.dma_start(shaped(raw, s % RAW, kt, n),
                                 src.rearrange("(k p) n -> p k n", p=P)[:, k0:k0 + kt, n0:n0 + n])\
                      .then_inc(raw_in[s % RAW], 16)

            def expert_loads(sweep):
                base = NPRE + sweep * NE * PER_EXPERT
                with sp.Fori(0, NE) as e:
                    u = 0
                    for j in range(STEPS + 1):
                        for wgt in ((w_exp_gate, w_exp_up) if j < STEPS else ()):
                            for half in range(2):
                                s = base + u
                                sp.wait_ge(lo_ready, e * PER_EXPERT + s - RAW + 1)
                                sp.dma_start(shaped(raw, s % RAW, 4, 512),
                                             wgt[0, e].rearrange("(k p) n -> p k n", p=P)
                                             [:, 4 * half:4 * half + 4, 512 * j:512 * j + 512])\
                                  .then_inc(raw_in[s % RAW], 16)
                                u += 1
                        for half in (range(2) if j > 0 else ()):
                            s = base + u
                            sp.wait_ge(lo_ready, e * PER_EXPERT + s - RAW + 1)
                            k0 = 4 * (j - 1) + 2 * half
                            sp.dma_start(shaped(raw, s % RAW, 2, D),
                                         w_exp_down[0, e].rearrange("(k p) n -> p k n", p=P)[:, k0:k0 + 2, :])\
                              .then_inc(raw_in[s % RAW], 16)
                            u += 1

            expert_loads(0)
            sp.wait_ge(routed, 1)
            over = sp.value_load(flag[0:1, 0:1], min_val=0, max_val=S)
            with sp.If(over > P):
                expert_loads(1)
            for t in range(TT):
                sp.wait_ge(out_ready, t + 1)
                sp.dma_start(out[0, P * t:P * t + P, :], H[:, t, :]).then_inc(out_done, 16)
            sp.wait_ge(out_done, 16 * TT)

        @block.gpsimd
        def _(pool):
            gains = [g_mix[0:1, :], g_ffn[0:1, :], g_kv.rearrange("(a d) -> a d", a=1), g_mix[1:2, :],
                     g_ffn[1:2, :], g_final.rearrange("(a d) -> a d", a=1)]
            pool.dma_start(gain[:, :], gains[0].to_broadcast([P, D])).then_inc(gain_in, 16)
            pool.dma_start(wgk, w_gk_up[0]).then_inc(small_in, 16)
            with nc.allow_non_contiguous_dma(reason="384 gate biases"):
                pool.dma_start(bgk[:, :], b_gk[0].rearrange("(h p) -> p h", p=GDK)).then_inc(small_in, 16)
            pool.dma_start(ggla[:, :], g_gla[0:1, :].to_broadcast([P, GDV])).then_inc(small_in, 16)
            pool.dma_start(gsub[:, :], g_subln[0:1, :].to_broadcast([P, DV])).then_inc(small_in, 16)
            for i, v in enumerate((lambda_q1, lambda_k1, lambda_q2, lambda_k2)):
                pool.dma_start(lam4[:, i, :], v[0:1, :].to_broadcast([P, HEAD_DIM])).then_inc(small_in, 16)
            for n, used in zip(range(1, len(gains)), (2, 6, 8, 10, 14)):
                pool.wait_ge(h_ready, used)
                pool.dma_start(gain[:, :], gains[n].to_broadcast([P, D])).then_inc(gain_in, 16)

        N_SMALL = 16 * 8

        @block.scalar
        def _(act):
            steps = [0]

            def link(ins):
                steps[0] += 1
                ins.then_inc(act_step, 1)
                act.wait_ge(act_step, steps[0])

            split = [0]

            def split_to(end):
                for s in range(split[0], end):
                    kt, n = slot_shape(s)
                    act.wait_ge(raw_in[s % RAW], 16 * (s // RAW + 1))
                    if s >= SPLIT:
                        act.wait_ge(slot_used, s - SPLIT + 1)
                    nc.scalar.activation(w_hi[:, s % SPLIT, 0:kt * n], raw[:, s % RAW, 0:kt * n], ACT.Copy)\
                      .then_inc(hi_ready, 1)
                split[0] = max(split[0], end)

            turns = [0]

            def turn():
                n = turns[0]
                for t in range(TT):
                    for half in range(2):
                        act.wait_ge(turned, 4 * n + 2 * t + half + 1)
                        nc.scalar.activation(
                            act_hi[:, 4 * half:4 * half + 4, P * t:P * t + P],
                            ps[:, 2 * t + half, :].rearrange("p (k n) -> p k n", k=4), ACT.Copy).then_inc(turn_hi, 1)
                turns[0] += 1

            def norm(ready, count):
                act.wait_ge(ready, count)
                for t in range(TT):
                    nc.scalar.activation(H[:, t, :], xres[:, t, :], ACT.Square, accum_out=ss[:, t:t + 1])\
                      .then_inc(act_step, 1)
                steps[0] += TT
                act.wait_ge(act_step, steps[0])
                nc.scalar.activation(rms, ss, ACT.Sqrt, bias=eps, scale=1.0 / D).then_inc(rms_ready, 1)

            def proj(after, dst, src, func=ACT.Copy):
                act.wait_ge(slot_used, after)
                nc.scalar.activation(dst, src, func).then_inc(proj_out, 1)

            def unit_exp(u):
                ns, nk = unit_parts(u)
                act.wait_ge(u_max, u + 1)
                for i in range(ns):
                    b = sc[:, u % 3, 256 * i:256 * i + nk]
                    c = 2 * (u % 3) + i
                    ins = nc.scalar.activation(b, b, ACT.Exp, bias=nbias[:, c:c + 1], scale=HEAD_DIM ** -0.5,
                                               accum_out=rsum[:, c:c + 1])
                ins.then_inc(u_exp, 1)

            def unit_copy(u):
                _, nk = unit_parts(u)
                act.wait_ge(u_turned, u + 1)
                nc.scalar.activation(pT[:, u % 2, 0:nk], ps[:, U_BANK["turn"][u % 2], 0:nk], ACT.Copy)\
                  .then_inc(u_pT, 1)

            def attention(u0, u1):
                for i in range(u0, u1 + 1):
                    if i < u1:
                        unit_exp(i)
                    if i > u0:
                        unit_copy(i - 1)

            act.wait_ge(const_in, 16)
            act.wait_ge(small_in, N_SMALL)
            act.wait_ge(mem_in, 16)
            split_to(3)
            turn()
            for l in range(2):
                split_to(2 * l + 2)
                proj(2 * l + 1, kmT[:, l, :, :], ps[:, 4 + 2 * l, :].rearrange("p (m s) -> p m s", m=2))
                proj(2 * l + 2, vm[:, l, :, :], ps[:, 5 + 2 * l, :].rearrange("p (t n) -> p t n", t=TT))
                split_to(2 * l + 4)
            norm(x_in, 16)
            split_to(4 + 3)
            turn()
            a = first["in_a"]
            proj(a + 1, gd[0:RANK, 0:S], ps[0:RANK, 4, 0:S])
            split_to(a + 4)
            proj(a + 2, qmT[:, :, :], ps[:, 5, :].rearrange("p (m s) -> p m s", m=2))
            act.wait_ge(gk_logit, 1)
            for h in range(GH):
                ins = nc.scalar.activation(ge[:, S * h:S * h + S], ps[0:GDK, 6 + h // 2, S * (h % 2):S * (h % 2) + S],
                                           ACT.Identity, bias=bgk[:, h:h + 1])
            ins.then_inc(gk_act, 1)
            act.wait_ge(gk_act, 1)
            nc.scalar.activation(gf, ge, ACT.Abs).then_inc(gk_act, 1)
            act.wait_ge(gk_act, 2)
            nc.scalar.activation(gf, gf, ACT.Exp, scale=-1.0).then_inc(gk_act, 1)
            act.wait_ge(gk_act, 3)
            nc.scalar.activation(gf, gf, ACT.Ln, bias=1.0).then_inc(gk_act, 1)
            split_to(a + 6)
            for i in range(4):
                dst = (gq, gk_)[i // 2][:, 512 * (i % 2):512 * (i % 2) + 512]
                proj(a + 3 + i, dst, ps[0:GDK, i, :])
            split_to(a + 9)
            for t in range(TT):
                proj(a + 8, v_tok[:, t, 0:512], ps[:, 4 + t, :])
            proj(a + 9, v_tok[:, :, 512:768], ps[:, 6, :].rearrange("p (t n) -> p t n", t=TT))
            split_to(a + 12)
            for t in range(TT):
                proj(a + 11, H[:, t, 0:512], ps[:, 7 * (1 - t), :], ACT.Silu)
            proj(a + 12, H[:, :, 512:768], ps[:, 1, :].rearrange("p (t n) -> p t n", t=TT), ACT.Silu)
            act.wait_ge(gk_vec, 2)
            nc.scalar.activation(ge, gd, ACT.Exp, scale=1.0 / 16).then_inc(gk_act, 1)
            nc.scalar.activation(gf, gd, ACT.Exp, scale=-1.0 / 16).then_inc(gk_act, 1)
            act.wait_ge(gk_vec, 3)
            nc.scalar.activation(ge, gb, ACT.Exp, scale=1.0 / 16).then_inc(gk_act, 1)
            act.wait_ge(gk_vec, 5)
            nc.scalar.activation(gf, gd, ACT.Exp, scale=1.0 / 16).then_inc(gk_act, 1)
            act.wait_ge(gk_act, 8)
            attention(0, NU0)
            split_to(a + 12 + 2)

            def head_norm(n, src, sq, width, m, ready, count):
                act.wait_ge(ready, count)
                nc.scalar.activation(sq, src, ACT.Square).then_inc(head_rms, 1)
                act.wait_ge(head_sq, n + 1)
                nc.scalar.activation(hrms[:, 0:m], hss[:, 0:m], ACT.Sqrt, bias=eps, scale=1.0 / width)\
                  .then_inc(head_rms, 1)

            head_norm(0, gla_o, T[:, 5:7, 0:MIX], GDV, TT * GH, gla_oe, GH)
            turn()
            split_to(first["dense"] + 1)
            norm(add_done, 4)
            split_to(first["dense"] + 2)
            turn()
            d = first["dense"]
            n_ff = F_DENSE // 256
            for i in range(n_ff + 1):
                base = d + 3 * i - (1 if i > 0 else 0)
                if i < n_ff:
                    split_to(base + 2)
                if i > 0:
                    act.wait_ge(ff_h, i)
                    if i > 1:
                        act.wait_ge(slot_used, base)
                    nc.scalar.activation(f_hi[:, :, :], f_h.rearrange("p (m s) -> p m s", m=2), ACT.Copy)\
                      .then_inc(ff_hi, 1)
                if i < n_ff:
                    act.wait_ge(slot_used, base + 1)
                    nc.scalar.activation(f_gate, ps[:, i % 2, :], ACT.Silu).then_inc(ff_silu, 1)
                if i > 0:
                    split_to(base + (3 if i < n_ff else 1))
            split_to(first["kv"] + 2)
            norm(add_done, 8)
            turn()
            k = first["kv"]
            split_to(k + 4)
            for t in range(TT):
                proj(k + 2, k_raw[:, t, 0:512], ps[:, 4 + t, :])
            split_to(k + 6)
            for t in range(TT):
                proj(k + 4, k_raw[:, t, 512:768], ps[:, 6 + t, 0:256])
                proj(k + 4, v_tok[:, t, 0:256], ps[:, 6 + t, 256:512])
            for t in range(TT):
                proj(k + 6, v_tok[:, t, 256:768], ps[:, t, :])
            b = first["in_b"]
            split_to(b + 2)
            turn()
            split_to(b + 4)
            for t in range(TT):
                proj(b + 2, q_raw[:, t, 0:512], ps[:, 4 + t, :])
            for t in range(TT):
                proj(b + 4, q_raw[:, t, 512:768], ps[:, 6 + t, 0:256])
                proj(b + 4, qm_tok[:, t, :], ps[:, 6 + t, 256:512])
            for r in range(4):
                dst, t = (kT, qT)[r // 2], r % 2
                act.wait_ge(rope_turned, r + 1)
                nc.scalar.activation(dst[:, 0:4, P * t:P * t + P],
                                     ps[:, 2 * (r % 2), :].rearrange("p (m n) -> p m n", m=4), ACT.Copy)
                if r >= 2:
                    nc.scalar.activation(qmT[:, :, P * t:P * t + P],
                                         ps[:, 2 * (r % 2) + 1, 256:512].rearrange("p (m n) -> p m n", m=2), ACT.Copy)
                nc.scalar.activation(dst[:, 4:6, P * t:P * t + P],
                                     ps[:, 2 * (r % 2) + 1, 0:256].rearrange("p (m n) -> p m n", m=2), ACT.Copy)\
                  .then_inc(rope_out, 1)
            act.wait_ge(lam_v, 1)
            nc.scalar.activation(lamc[:, 2:4], lamc[:, 0:2], ACT.Exp).then_inc(lam_a, 1)
            attention(NU0, len(units))
            split_to(first["out_b"] + 3)
            head_norm(1, diff_o, diff_sq, DV, TT * DH, u_out, len(units))
            turn()
            split_to(NPRE - 1)
            norm(add_done, 12)
            split_to(NPRE)
            turn()
            act.wait_ge(top_d, 1)
            nc.scalar.activation(rt[:, 2:4], rt[:, 0:2], ACT.Exp).then_inc(top_e, 1)

            def gathered(sweep, e, one):
                for half in range(2):
                    act.wait_ge(disp, sweep * 2 * (NE + 1) + 2 * e + half + 1 + one)
                    nc.scalar.activation(xg_hi[:, 4 * half:4 * half + 4, :],
                                         ps[:, 1 + 2 * half, :].rearrange("p (k n) -> p k n", k=4), ACT.Copy)\
                      .then_inc(xg_h, 1)

            def experts(sweep):
                gathered(sweep, 0, 0)
                done = sweep * NE
                base = NPRE + done * PER_EXPERT

                def evacuate_y(i):
                    act.wait_ge(slot_used, i * PER_EXPERT + base)
                    if sweep == 0:
                        act.wait_ge(e_blank, 1)
                    nc.scalar.activation(y_e[:, 0:512], ps[:, 5, :], ACT.Copy).then_inc(e_yo, 1)
                    nc.scalar.activation(y_e[:, 512:1024], ps[:, 6, :], ACT.Copy).then_inc(e_yo, 1)

                with act.Fori(0, NE) as e:
                    u = [0]

                    def split_next(n):
                        for _ in range(n):
                            s = base + u[0]
                            act.wait_ge(raw_in[s % RAW], e * (16 * PER_EXPERT // RAW) + 16 * (s // RAW + 1))
                            act.wait_ge(slot_used, e * PER_EXPERT + s - E_SPLIT + 1)
                            nc.scalar.activation(e_whi[:, (s - NPRE) % E_SPLIT, :], raw[:, s % RAW, :], ACT.Copy)\
                              .then_inc(hi_ready, 1)
                            u[0] += 1

                    def hidden(j):
                        act.wait_ge(e_tr, (e + done) * STEPS + j + 1)
                        nc.scalar.activation(h_hi, ps[:, 4, :].rearrange("p (m n) -> p m n", m=4), ACT.Copy)\
                          .then_inc(e_hi, 1)

                    split_next(2)
                    for j in range(STEPS):
                        split_next(2)
                        if j == 0:
                            evacuate_y(e)
                        if j == 1:
                            act.wait_ge(oh_turned, e + done + 1)
                            nc.scalar.activation(ohT[:, :], ps[:, 7, 0:256], ACT.Copy).then_inc(ohT_ready, 1)
                        if j > 0:
                            split_next(2)
                            hidden(j - 1)
                        act.wait_ge(slot_used, e * PER_EXPERT + base + gate_end(j))
                        nc.scalar.activation(e_h[:, :], ps[:, j % 2, :], ACT.Silu).then_inc(e_silu, 1)
                        split_next(2)
                    gathered(sweep, e, 2)
                    hidden(STEPS - 1)
                evacuate_y(NE)

            act.wait_ge(slot_used, NPRE)
            experts(0)
            act.wait_ge(routed, 1)
            over = act.value_load(flag[0:1, 0:1], min_val=0, max_val=S)
            with act.If(over > P):
                experts(1)
                act.wait_ge(e_add, 2 * 4 * (NE + 1))
            norm(e_add, 4 * (NE + 1))

        @block.vector
        def _(dve):
            steps = [0]

            def link(ins):
                steps[0] += 1
                ins.then_inc(dve_step, 1)
                dve.wait_ge(dve_step, steps[0])

            split = [0]

            def split_to(end):
                for s in range(split[0], end):
                    kt, n = slot_shape(s)
                    dve.wait_ge(hi_ready, s + 1)
                    nc.vector.tensor_tensor(w_lo[:, s % SPLIT, 0:kt * n], raw[:, s % RAW, 0:kt * n],
                                            w_hi[:, s % SPLIT, 0:kt * n].bitcast(F32), ALU.subtract)\
                      .then_inc(lo_ready, 1)
                split[0] = max(split[0], end)

            turns = [0]

            def turn():
                n = turns[0]
                for t in range(TT):
                    for half in range(2):
                        dve.wait_ge(turn_hi, 4 * n + 2 * t + half + 1)
                        ks = slice(4 * half, 4 * half + 4)
                        nc.vector.tensor_tensor(
                            act_lo[:, ks, P * t:P * t + P], ps[:, 2 * t + half, :].rearrange("p (k n) -> p k n", k=4),
                            act_hi[:, ks, P * t:P * t + P].bitcast(F32), ALU.subtract).then_inc(turn_lo, 1)
                turns[0] += 1

            norms = [0]

            def norm(signal, roots):
                n = norms[0]
                dve.wait_ge(rms_ready, roots)
                link(nc.vector.reciprocal(rs, rms))
                dve.wait_ge(gain_in, 16 * (n + 1))
                for t in range(TT):
                    nc.vector.scalar_tensor_tensor(out=H[:, t, :], in0=xres[:, t, :], scalar=rs[:, t:t + 1],
                                                   in1=gain[:, :], op0=ALU.mult, op1=ALU.mult).then_inc(signal, 1)
                norms[0] += 1

            adds = [0]

            def residual(banks, after):
                dve.wait_ge(slot_used, after)
                for i, b in enumerate(banks):
                    xs = xres[:, i // 2, 512 * (i % 2):512 * (i % 2) + 512]
                    nc.vector.tensor_tensor(xs, xs, ps[:, b, :], ALU.add).then_inc(add_done, 1)
                adds[0] += 1
                dve.wait_ge(add_done, 4 * adds[0])

            def unit_max(u):
                kind, _, _, t = units[u]
                ns, nk = unit_parts(u)
                c = 2 * (u % 3)
                bank = ps[:, U_BANK["score"][u % 2]:U_BANK["score"][u % 2] + 2, 0:S]
                buf = sc[:, u % 3, :].rearrange("p (i n) -> p i n", i=2)
                dve.wait_ge(u_score, u + 1)
                if kind == "mem":
                    link(nc.vector.tensor_copy(buf[:, 0, :], bank[:, 0, :]))
                else:
                    m = cst[:, C_CAUSAL + P - P * t:C_CAUSAL + 2 * P].rearrange("p (o n) -> p o n", o=1)
                    link(nc.vector.tensor_tensor(buf[:, :, 0:nk], bank[:, :, 0:nk], m.to_broadcast([P, 2, nk]),
                                                 ALU.add))
                link(nc.vector.tensor_reduce(nmax[:, c:c + ns], buf[:, 0:ns, 0:nk], AX.X, ALU.max, negate=True))
                nc.vector.tensor_scalar(nbias[:, c:c + ns], nmax[:, c:c + ns], HEAD_DIM ** -0.5, None, ALU.mult)\
                  .then_inc(u_max, 1)

            def unit_prob(u):
                kind, _, _, t = units[u]
                ns, nk = unit_parts(u)
                c = 2 * (u % 3)
                b0, b1 = sc[:, u % 3, 0:nk], sc[:, u % 3, 256:256 + nk]
                dve.wait_ge(u_exp, u + 1)
                link(nc.vector.reciprocal(rinv[:, c:c + ns], rsum[:, c:c + ns]))
                if kind == "mem":
                    nc.vector.tensor_scalar(b0, b0, rinv[:, c:c + 1], None, ALU.mult).then_inc(u_prob, 1)
                    return
                link(nc.vector.tensor_scalar(b1, b1, rinv[:, c + 1:c + 2], lamc[:, 5:6], ALU.mult, ALU.mult))
                nc.vector.scalar_tensor_tensor(out=b0, in0=b0, scalar=rinv[:, c:c + 1], in1=b1,
                                               op0=ALU.mult, op1=ALU.add).then_inc(u_prob, 1)

            def unit_out(u):
                kind, _, h, t = units[u]
                dst = H[:, t, MIX + HEAD_DIM * h:MIX + HEAD_DIM * (h + 1)] if kind == "mem" \
                    else diff_o[:, t, DV * h:DV * h + DV]
                dve.wait_ge(u_val, u + 1)
                nc.vector.tensor_copy(dst, ps[:, U_BANK["val"][u % 2], 0:dst.shape[1]]).then_inc(u_out, 1)

            def attention(u0, u1):
                for i in range(u0, u1 + 2):
                    if i < u1:
                        unit_max(i)
                    if u0 < i <= u1:
                        unit_prob(i - 1)
                    if i > u0 + 1:
                        unit_out(i - 2)

            def head_norm(sq, heads, sqrts):
                dve.wait_ge(head_rms, sqrts + 1)
                nc.vector.tensor_reduce(hss[:, 0:TT * heads], sq, AX.X, ALU.add).then_inc(head_sq, 1)
                dve.wait_ge(head_rms, sqrts + 2)
                link(nc.vector.reciprocal(hrs[:, 0:TT * heads], hrms[:, 0:TT * heads]))
                for t in range(TT):
                    for h in range(heads):
                        yield t, h, hrs[:, heads * t + h:heads * t + h + 1]

            dve.wait_ge(const_in, 16)
            dve.wait_ge(small_in, N_SMALL)
            link(nc.vector.memset(ones[:, :], 1.0))
            link(nc.vector.tensor_tensor(lam4[:, 0:3:2, :], lam4[:, 0:3:2, :], lam4[:, 1:4:2, :], ALU.mult))
            nc.vector.tensor_reduce(lamc[:, 0:2], lam4[:, 0:3:2, :], AX.X, ALU.add).then_inc(lam_v, 1)
            split_to(3)
            turn()
            split_to(4)
            dve.wait_ge(x_in, 16)
            norm(h_ready, 1)
            split_to(4 + 3)
            turn()
            a = first["in_a"]
            split_to(a + 4)
            dve.wait_ge(gk_act, 1)
            link(nc.vector.memset(ki, 1.0))
            link(nc.vector.memset(ki[:, 0:D:CHUNK], 0.0))
            dve.wait_ge(gk_act, 4)
            link(nc.vector.scalar_tensor_tensor(out=ge, in0=ge, scalar=0.0, in1=gf, op0=ALU.min, op1=ALU.subtract))
            nc.vector.tensor_tensor_scan(gb, ki, ge, 0.0, ALU.mult, ALU.add).then_inc(gk_vec, 1)
            dve.wait_ge(gk_vec, 1)
            split_to(a + 6)

            def chunks(buf):
                return buf.rearrange("p (c n) -> p c n", n=CHUNK)

            def at(col):
                return chunks(gb)[:, :, col:col + 1].to_broadcast([GDK, GH * NCH, CHUNK])

            dve.wait_ge(gk_logit, 1)
            nc.vector.tensor_tensor(chunks(gd), chunks(gb), at(CHUNK // 2 - 1), ALU.subtract).then_inc(gk_vec, 1)
            split_to(a + 12)
            dve.wait_ge(proj_out, 4 + 1 + 1 + 4)
            dve.wait_ge(gk_act, 5)
            nc.vector.scalar_tensor_tensor(out=qi, in0=gq, scalar=GDK ** -0.5, in1=ge, op0=ALU.mult, op1=ALU.mult)\
              .then_inc(gk_vec, 1)
            dve.wait_ge(gk_act, 6)
            nc.vector.tensor_tensor(ki, gk_, gf, ALU.mult).then_inc(gk_vec, 1)
            nc.vector.tensor_tensor(chunks(gd), at(CHUNK - 1), chunks(gb), ALU.subtract).then_inc(gk_vec, 1)
            dve.wait_ge(gk_act, 7)
            nc.vector.scalar_tensor_tensor(out=gq, in0=gq, scalar=GDK ** -0.5, in1=ge, op0=ALU.mult, op1=ALU.mult)\
              .then_inc(gk_vec, 1)
            dve.wait_ge(gk_act, 8)
            nc.vector.tensor_tensor(gk_, gk_, gf, ALU.mult).then_inc(gk_vec, 1)
            dve.wait_ge(gk_vec, 7)
            link(nc.vector.tensor_copy(small[0:GDK, 104:120], ge[:, CHUNK - 1:D:CHUNK]))
            decay = small[0:GDK, 104:120]
            link(nc.vector.memset(sT[:, :, :], 0.0))
            attention(0, NU0)
            split_to(a + 12 + 2)
            for h in range(GH):
                dve.wait_ge(gla_sc, h + 1)
                if h > 0:
                    dve.wait_ge(gla_od, h)
                for t in range(TT):
                    for c in range(2):
                        r = slice(CHUNK * c, CHUNK * c + CHUNK)
                        nc.vector.copy_predicated(sT[r, t, r], cst[r, C_GLA:C_GLA + CHUNK].bitcast(U32),
                                                  ps[r, h % 2, P * t + CHUNK * c:P * t + CHUNK * c + CHUNK])
                nc.vector.tensor_copy(kdT[:, :, :], ps[:, h % 2, 256:256 + 2 * GDK].rearrange("p (t n) -> p t n", t=TT))\
                  .then_inc(gla_sce, 1)
                dve.wait_ge(gla_kv, h + 1)
                link(nc.vector.tensor_copy(state[:, 0, :], ps[0:GDK, 2, 0:GDV]))
                link(nc.vector.scalar_tensor_tensor(out=state[:, 1, :], in0=state[:, 0, :],
                                                    scalar=decay[:, NCH * h + 1:NCH * h + 2],
                                                    in1=ps[0:GDK, 3, 0:GDV], op0=ALU.mult, op1=ALU.add))
                nc.vector.scalar_tensor_tensor(out=state[:, 2, :], in0=state[:, 1, :],
                                               scalar=decay[:, NCH * h + 2:NCH * h + 3],
                                               in1=ps[0:GDK, 2, 256:256 + GDV], op0=ALU.mult, op1=ALU.add).then_inc(gla_st, 1)
                dve.wait_ge(gla_od, h + 1)
                nc.vector.tensor_copy(gla_o[:, :, GDV * h:GDV * h + GDV],
                                      ps[:, 4 + h % 2, 0:2 * 256].rearrange("p (t n) -> p t n", t=TT)[:, :, 0:GDV])\
                  .then_inc(gla_oe, 1)
            sq = T[:, 5:7, 0:MIX].rearrange("p t (h n) -> p t h n", h=GH)
            for t, h, r in head_norm(sq, GH, 0):
                o = gla_o[:, t, GDV * h:GDV * h + GDV]
                ins = nc.vector.scalar_tensor_tensor(out=o, in0=o, scalar=r, in1=ggla[:, :], op0=ALU.mult, op1=ALU.mult)
            link(ins)
            for t in range(TT):
                nc.vector.tensor_tensor(H[:, t, 0:MIX], H[:, t, 0:MIX], gla_o[:, t, :], ALU.mult).then_inc(h_ready, 1)
            turn()
            split_to(first["dense"])
            residual((4, 6, 5, 7), first["dense"])
            split_to(first["dense"] + 1)
            norm(h_ready, 2)
            turn()
            d = first["dense"]
            n_ff = F_DENSE // 256
            for i in range(n_ff + 1):
                base = d + 3 * i - (1 if i > 0 else 0)
                if i < n_ff:
                    split_to(base + 2)
                if i > 0:
                    dve.wait_ge(ff_hi, i)
                    nc.vector.tensor_tensor(f_lo[:, :, :], f_h.rearrange("p (m s) -> p m s", m=2),
                                            f_hi[:, :, :].bitcast(F32), ALU.subtract).then_inc(ff_lo, 1)
                    split_to(base + (3 if i < n_ff else 1))
                if i < n_ff:
                    dve.wait_ge(ff_silu, i + 1)
                    dve.wait_ge(slot_used, base + 2)
                    if i > 0:
                        dve.wait_ge(ff_lo, i)
                    nc.vector.tensor_tensor(f_h, f_gate, ps[:, 2 + i % 2, :], ALU.mult).then_inc(ff_h, 1)
            residual((4, 5, 6, 7), first["kv"])
            norm(h_ready, 3)
            split_to(first["kv"] + 2)
            turn()
            split_to(first["kv"] + 6)
            norm(h_ready, 3)
            split_to(first["in_b"] + 1)
            turn()
            split_to(first["in_b"] + 4)

            ropes = [0]

            def rope(src, t, evacuated):
                dve.wait_ge(proj_out, evacuated)
                v = src[:, t, :].rearrange("p (h c d) -> p h c d", h=2 * DH, c=2)
                o = rot[:, t, :].rearrange("p (h c d) -> p h c d", h=2 * DH, c=2)
                cs, sn = (cos_sin[:, t, i:i + 1, :].to_broadcast([P, 2 * DH, HEAD_DIM // 2]) for i in range(2))
                tmp = [rope_t[:, i, :].rearrange("p (h d) -> p h d", h=2 * DH) for i in range(4)]
                if ropes[0] > 0:
                    dve.wait_ge(roped, ropes[0])
                for i, (a_, b_) in enumerate(((v[:, :, 0, :], cs), (v[:, :, 1, :], sn), (v[:, :, 0, :], sn),
                                              (v[:, :, 1, :], cs))):
                    ins = nc.vector.tensor_tensor(tmp[i], a_, b_, ALU.mult)
                link(ins)
                if ropes[0] >= 2:
                    dve.wait_ge(rope_turned, ropes[0] - 1)
                nc.vector.tensor_tensor(o[:, :, 0, :], tmp[0], tmp[1], ALU.subtract)
                nc.vector.tensor_tensor(o[:, :, 1, :], tmp[2], tmp[3], ALU.add).then_inc(roped, 1)
                ropes[0] += 1

            kv_out = 4 + 12 + 0 + 2 + 4 + 2
            rope(k_raw, 0, kv_out)
            rope(k_raw, 1, kv_out)
            rope(q_raw, 0, kv_out + 6)
            rope(q_raw, 1, kv_out + 6)
            dve.wait_ge(roped, 4)
            dve.wait_ge(lam_a, 1)
            link(nc.vector.tensor_tensor(lamc[:, 4:5], lamc[:, 3:4], lamc[:, 2:3], ALU.subtract))
            link(nc.vector.tensor_scalar(lamc[:, 5:6], lamc[:, 4:5], -LAMBDA_INIT, None, ALU.add))
            link(nc.vector.tensor_scalar(gsub[:, :], gsub[:, :], 1.0 - LAMBDA_INIT, None, ALU.mult))
            attention(NU0, len(units))
            split_to(first["out_b"] + 2)
            sq = diff_sq.rearrange("p t (h n) -> p t h n", h=DH)
            for t, h, r in head_norm(sq, DH, 2):
                nc.vector.scalar_tensor_tensor(out=H[:, t, DV * h:DV * h + DV], in0=diff_o[:, t, DV * h:DV * h + DV],
                                               scalar=r, in1=gsub[:, :], op0=ALU.mult, op1=ALU.mult)\
                  .then_inc(*((h_ready, 1) if h == DH - 1 else (dve_step, 1)))
                steps[0] += h != DH - 1
            turn()
            split_to(NPRE - 1)
            residual((4, 6, 5, 7), NPRE - 1)
            norm(h_ready, 4)
            turn()
            split_to(NPRE)

            dve.wait_ge(slot_used, NPRE)
            lg = rt[:, 8:24].rearrange("p (t e) -> p t e", t=TT)
            link(nc.vector.tensor_copy(lg, ps[:, 4, 0:TT * NE].rearrange("p (t e) -> p t e", t=TT)))
            for t in range(TT):
                link(nc.vector.max(top8[:, t, :], lg[:, t, :]))
                link(nc.vector.max_index(idx8[:, t, :], top8[:, t, :], lg[:, t, :]))
            link(nc.vector.tensor_copy(fidx, idx8[:, :, :]))
            nc.vector.tensor_tensor(rt[:, 0:2], top8[:, :, 1], top8[:, :, 0], ALU.subtract).then_inc(top_d, 1)
            link(nc.vector.memset(route_gate[:, :, :], 0.0))
            link(nc.vector.memset(route_rank[:, :, :], -1.0))
            iota8 = cst[:, C_IOTA:C_IOTA + NE]
            for t in range(TT):
                link(nc.vector.tensor_scalar(tmp8[:, t, :], iota8, fidx[:, t, 0:1], None, ALU.is_equal))
                link(nc.vector.tensor_scalar(msk[:, t, :], iota8, fidx[:, t, 1:2], None, ALU.is_equal))
                nc.vector.tensor_tensor(msk[:, t, :], msk[:, t, :], tmp8[:, t, :], ALU.add).then_inc(chosen, 1)
            dve.wait_ge(chosen, TT)
            dve.wait_ge(top_e, 1)
            link(nc.vector.tensor_scalar(rt[:, 4:6], rt[:, 2:4], 1.0, None, ALU.add))
            link(nc.vector.reciprocal(rt[:, 4:6], rt[:, 4:6]))
            link(nc.vector.tensor_tensor(rt[:, 6:8], rt[:, 2:4], rt[:, 4:6], ALU.mult))
            for t in range(TT):
                link(nc.vector.tensor_scalar(tmp8[:, t, :], iota8, fidx[:, t, 0:1], rt[:, 4 + t:5 + t],
                                             ALU.is_equal, ALU.mult))
                link(nc.vector.tensor_scalar(route_gate[:, t, 1:NE + 1], iota8, fidx[:, t, 1:2], rt[:, 6 + t:7 + t],
                                             ALU.is_equal, ALU.mult))
            link(nc.vector.tensor_tensor(route_gate[:, :, 1:NE + 1], route_gate[:, :, 1:NE + 1], tmp8, ALU.add))
            dve.wait_ge(ranks, 1)
            cnt = ps[:, 5, 0:TT * NE].rearrange("p (t e) -> p t e", t=TT)
            link(nc.vector.tensor_tensor(tmp8, msk, cnt, ALU.mult))
            link(nc.vector.tensor_scalar(msk, msk, -1.0, None, ALU.add))
            link(nc.vector.tensor_tensor(route_rank[:, :, 0:NE], tmp8, msk, ALU.add))
            link(nc.vector.tensor_reduce(rt[:, 24:25], ps[:, 5, 16:24], AX.X, ALU.max))
            link(nc.vector.memset(flag[:, :], 0))
            nc.vector.tensor_copy(flag[0:1, 0:1], rt[0:1, 24:25]).then_inc(routed, 1)

            def one_hot(sweep):
                for t in range(TT):
                    nc.vector.tensor_scalar(oh[:, t, :], cst[:, C_IOTA + P * sweep:C_IOTA + P * sweep + P],
                                            cur_rank[:, t:t + 1], None, ALU.is_equal).then_inc(oh_ready, 1)

            def gathered(sweep, e, more):
                for half in range(2):
                    dve.wait_ge(xg_h, sweep * 2 * (NE + 1) + 2 * e + half + 1 + more)
                    nc.vector.tensor_tensor(xg_lo[:, 4 * half:4 * half + 4, :],
                                            ps[:, 1 + 2 * half, :].rearrange("p (k n) -> p k n", k=4),
                                            xg_hi[:, 4 * half:4 * half + 4, :].bitcast(F32), ALU.subtract)\
                      .then_inc(xg_l, 1)

            def experts(sweep):
                done = sweep * NE
                cd = sweep * (2 * NE + 2)
                if sweep == 0:
                    nc.vector.memset(ohT[:, :], 0.0).then_inc(e_blank, 1)
                nc.vector.tensor_copy(cur_rank.rearrange("p (t o) -> p t o", o=1), route_rank[:, :, 0:1])\
                  .then_inc(cur_done, 1)
                dve.wait_ge(cur_done, cd + 1)
                one_hot(sweep)
                gathered(sweep, 0, 0)
                base = NPRE + done * PER_EXPERT

                def add_expert(i):
                    for n in range(4):
                        dve.wait_ge(e_comb, (i + sweep * (NE + 1)) * 4 + n + 1)
                        xs = xres[:, n // 2, 512 * (n % 2):512 * (n % 2) + 512]
                        nc.vector.scalar_tensor_tensor(out=xs, in0=ps[:, (1, 3, 4, 7)[n], :],
                                                       scalar=cur_gate[:, n // 2:n // 2 + 1], in1=xs,
                                                       op0=ALU.mult, op1=ALU.add).then_inc(e_add, 1)

                with dve.Fori(0, NE) as e:
                    u = [0]

                    def split_next(n):
                        for _ in range(n):
                            s = base + u[0]
                            dve.wait_ge(hi_ready, e * PER_EXPERT + s + 1)
                            r = (s - NPRE) % E_SPLIT
                            nc.vector.tensor_tensor(e_wlo[:, r, :], raw[:, s % RAW, :],
                                                    e_whi[:, r, :].bitcast(F32), ALU.subtract).then_inc(lo_ready, 1)
                            u[0] += 1

                    def hidden(j):
                        dve.wait_ge(e_hi, (e + done) * STEPS + j + 1)
                        nc.vector.tensor_tensor(h_lo, ps[:, 4, :].rearrange("p (m n) -> p m n", m=4),
                                                h_hi.bitcast(F32), ALU.subtract).then_inc(e_lo, 1)

                    split_next(2)
                    for j in range(STEPS):
                        split_next(2)
                        if j == 0:
                            nc.vector.tensor_copy(cur_gate.rearrange("p (t o) -> p t o", o=1),
                                                  route_gate[:, :, bass.ds(e, 1)]).then_inc(cur_done, 1)
                        if j == 3:
                            nc.vector.tensor_copy(cur_rank.rearrange("p (t o) -> p t o", o=1),
                                                  route_rank[:, :, bass.ds(e + 1, 1)]).then_inc(cur_done, 1)
                            dve.wait_ge(cur_done, 2 * e + cd + 3)
                            one_hot(sweep)
                        if j > 0:
                            split_next(2)
                            hidden(j - 1)
                        split_next(2)
                        if j == 0:
                            dve.wait_ge(cur_done, 2 * e + cd + 2)
                            add_expert(e)
                        dve.wait_ge(e_silu, (e + done) * STEPS + j + 1)
                        dve.wait_ge(slot_used, e * PER_EXPERT + base + gate_end(j) + 2)
                        nc.vector.tensor_tensor(e_h[:, :], e_h[:, :], ps[:, 2 + j % 2, :], ALU.mult).then_inc(e_hr, 1)
                    gathered(sweep, e, 2)
                    hidden(STEPS - 1)
                nc.vector.tensor_copy(cur_gate.rearrange("p (t o) -> p t o", o=1), route_gate[:, :, NE:NE + 1])\
                  .then_inc(cur_done, 1)
                dve.wait_ge(cur_done, cd + 2 * NE + 2)
                add_expert(NE)

            experts(0)
            dve.wait_ge(routed, 1)
            over = dve.value_load(flag[0:1, 0:1], min_val=0, max_val=S)
            with dve.If(over > P):
                experts(1)
                dve.wait_ge(e_add, 2 * 4 * (NE + 1))
            dve.wait_ge(e_add, 4 * (NE + 1))
            norm(out_ready, 5)

        @block.tensor
        def _(pe):
            def three(dst, l_hi, l_lo, r_hi, r_lo, start, stop):
                nc.tensor.matmul(dst, l_hi, r_hi, start=start, stop=False)
                nc.tensor.matmul(dst, l_lo, r_hi, start=False, stop=False)
                return nc.tensor.matmul(dst, l_hi, r_lo, start=False, stop=stop)

            used = [0]

            def take():
                s = used[0]
                used[0] += 1
                kt, n = slot_shape(s)
                pe.wait_ge(lo_ready, s + 1)
                return shaped(w_hi, s % SPLIT, kt, n), shaped(w_lo, s % SPLIT, kt, n)

            turns = [0]
            hs = [0]

            def turn(from_vector=True):
                for t in range(TT):
                    if from_vector:
                        hs[0] += 1
                        pe.wait_ge(h_ready, hs[0])
                    for half in range(2):
                        for k in range(4):
                            c = P * (4 * half + k)
                            ins = nc.tensor.transpose(ps[:, 2 * t + half, P * k:P * k + P], H[:, t, c:c + P], ident)
                        ins.then_inc(turned, 1)
                turns[0] += 1
                pe.wait_ge(turn_lo, 4 * turns[0])

            def token_major(banks, n_slots, cols=None):
                k = 0
                for i in range(n_slots):
                    hi, lo = take()
                    kt, n = hi.shape[1], hi.shape[2]
                    for kk in range(kt):
                        for t in range(TT):
                            ts = slice(P * t, P * t + P)
                            ins = three(banks[t][:, 0:n], act_hi[:, k, ts], act_lo[:, k, ts], hi[:, kk, :], lo[:, kk, :],
                                        k == 0, k == KT - 1)
                        k += 1
                    if i < n_slots - 1:
                        ins.then_inc(slot_used, 1)
                return ins

            def feature_major(regions, width):
                hi, lo = take()
                for m, reg in enumerate(regions):
                    for k in range(KT):
                        c = slice(width * m, width * m + width)
                        ins = three(reg, hi[:, k, c], lo[:, k, c], act_hi[:, k, :], act_lo[:, k, :], k == 0, k == KT - 1)
                return ins

            def mark(ins):
                ins.then_inc(slot_used, 1)

            def halves(b):
                return [ps[:, b, 0:256], ps[:, b, 256:512]]

            pe.wait_ge(const_in, 16)
            pe.wait_ge(small_in, N_SMALL)
            pe.wait_ge(mem_in, 16)
            turn(from_vector=False)
            for l in range(2):
                mark(feature_major(halves(4 + 2 * l), P))
                hi, lo = take()
                for t in range(TT):
                    for k in range(KT):
                        ts = slice(P * t, P * t + P)
                        ins = three(halves(5 + 2 * l)[t], act_hi[:, k, ts], act_lo[:, k, ts], hi[:, k, :], lo[:, k, :],
                                    k == 0, k == KT - 1)
                mark(ins)
            turn()
            pe.wait_ge(proj_out, 4)
            mark(feature_major([ps[0:RANK, 4, 0:S]], RANK))
            mark(feature_major(halves(5), P))
            pe.wait_ge(proj_out, 5)
            for h in range(GH):
                ins = nc.tensor.matmul(ps[0:GDK, 6 + h // 2, S * (h % 2):S * (h % 2) + S],
                                       wgk[:, GDK * h:GDK * h + GDK], gd[0:RANK, 0:S], start=True, stop=True)
            ins.then_inc(gk_logit, 1)
            for i in range(4):
                mark(feature_major([ps[0:GDK, i, 0:S], ps[0:GDK, i, S:2 * S]], GDK))

            def two_blocks(b512, b256):
                mark(token_major([ps[:, b512[0], :], ps[:, b512[1], :]], 2))
                hi, lo = take()
                for t in range(TT):
                    for k in range(KT):
                        ts = slice(P * t, P * t + P)
                        ins = three(halves(b256)[t], act_hi[:, k, ts], act_lo[:, k, ts], hi[:, k, :], lo[:, k, :],
                                    k == 0, k == KT - 1)
                mark(ins)

            pe.wait_ge(proj_out, 6)
            pe.wait_ge(gk_act, 1)
            two_blocks((4, 5), 6)
            pe.wait_ge(proj_out, 6 + 2)
            two_blocks((7, 0), 1)

            def unit_scores(u):
                kind, l, h, t = units[u]
                ns, nk = unit_parts(u)
                if u >= 2:
                    pe.wait_ge(u_max, u - 1)
                bank = U_BANK["score"][u % 2]
                ts = slice(P * t, P * t + P)
                if kind == "mem":
                    r, m = slice(HEAD_DIM * (h % 2), HEAD_DIM * (h % 2) + HEAD_DIM), h // 2
                    ins = nc.tensor.matmul(ps[:, bank, 0:S], qmT[r, m, ts], kmT[r, l, m, :], start=True, stop=True)
                else:
                    for i in range(2):
                        r = slice(HEAD_DIM * i, HEAD_DIM * i + HEAD_DIM)
                        ins = nc.tensor.matmul(ps[:, bank + i, 0:nk], qT[r, h, ts], kT[r, h, 0:nk],
                                               start=True, stop=True)
                ins.then_inc(u_score, 1)

            def unit_turn(u):
                _, nk = unit_parts(u)
                pe.wait_ge(u_prob, u + 1)
                if u >= 2:
                    pe.wait_ge(u_pT, u - 1)
                for k in range(nk // P):
                    ins = nc.tensor.transpose(ps[:, U_BANK["turn"][u % 2], P * k:P * k + P],
                                              sc[:, u % 3, P * k:P * k + P], ident)
                ins.then_inc(u_turned, 1)

            def unit_values(u):
                kind, l, h, _ = units[u]
                _, nk = unit_parts(u)
                pe.wait_ge(u_pT, u + 1)
                if u >= 2:
                    pe.wait_ge(u_out, u - 1)
                w = HEAD_DIM if kind == "mem" else DV
                for k in range(nk // P):
                    v = vm[:, l, k, w * h:w * h + w] if kind == "mem" else v_tok[:, k, w * h:w * h + w]
                    ins = nc.tensor.matmul(ps[:, U_BANK["val"][u % 2], 0:w], pT[:, u % 2, P * k:P * k + P], v,
                                           start=(k == 0), stop=(k == nk // P - 1))
                ins.then_inc(u_val, 1)

            def attention(u0, u1):
                for i in range(u0, u1 + 2):
                    if i < u1:
                        unit_scores(i)
                    if u0 < i <= u1:
                        unit_turn(i - 1)
                    if i > u0 + 1:
                        unit_values(i - 2)

            pe.wait_ge(proj_out, 16)
            attention(0, NU0)
            pe.wait_ge(gk_vec, 7)
            pe.wait_ge(u_out, NU0)
            for h in range(GH):
                hd = slice(S * h, S * h + S)
                q_in, k_in, q_st, k_st = qi[:, hd], ki[:, hd], gq[:, hd], gk_[:, hd]
                if h >= 2:
                    pe.wait_ge(gla_sce, h - 1)
                for n in range(NCH):
                    t, c = n // 2, n % 2
                    cs = slice(CHUNK * n, CHUNK * n + CHUNK)
                    nc.tensor.matmul(ps[CHUNK * c:CHUNK * c + CHUNK, h % 2, P * t + CHUNK * c:P * t + CHUNK * c + CHUNK],
                                     k_in[:, cs], q_in[:, cs], start=True, stop=True, skip_group_check=True)
                for t in range(TT):
                    ins = nc.tensor.transpose(ps[:, h % 2, 256 + GDK * t:256 + GDK * t + GDK],
                                              k_st[:, P * t:P * t + P], ident[0:GDK, 0:GDK])
                ins.then_inc(gla_sc, 1)
                pe.wait_ge(gla_sce, h + 1)
                for n in range(NCH - 1):
                    t, r = n // 2, slice(CHUNK * (n % 2), CHUNK * (n % 2) + CHUNK)
                    ins = nc.tensor.matmul(ps[0:GDK, 2 + n % 2, 256 * (n // 2):256 * (n // 2) + GDV], kdT[r, t, :],
                                           v_tok[r, t, GDV * h:GDV * h + GDV], start=True, stop=True)
                ins.then_inc(gla_kv, 1)
                pe.wait_ge(gla_st, h + 1)
                if h >= 2:
                    pe.wait_ge(gla_oe, h - 1)
                for t in range(TT):
                    o = ps[:, 4 + h % 2, 256 * t:256 * t + GDV]
                    nc.tensor.matmul(o, sT[:, t, :], v_tok[:, t, GDV * h:GDV * h + GDV], start=True, stop=False,
                                     skip_group_check=True)
                    for c in range(2):
                        n = 2 * t + c
                        if n == 0:
                            continue
                        r = slice(CHUNK * c, CHUNK * c + CHUNK)
                        ins = nc.tensor.matmul(o[r, :], q_st[:, CHUNK * n:CHUNK * n + CHUNK], state[:, n - 1, :],
                                               start=False, stop=True, skip_group_check=True)
                ins.then_inc(gla_od, 1)
            turn()

            pe.wait_ge(gla_oe, GH)

            def out_projection():
                token_major([ps[:, 4, :], ps[:, 5, :]], 2).then_inc(slot_used, 1)
                mark(token_major([ps[:, 6, :], ps[:, 7, :]], 2))

            out_projection()
            turn()
            pe.wait_ge(add_done, 4)
            n_ff = F_DENSE // 256
            for i in range(n_ff + 1):
                if i < n_ff:
                    if i >= 2:
                        pe.wait_ge(ff_silu, i - 1)
                        pe.wait_ge(ff_h, i - 1)
                    for j in range(2):
                        mark(feature_major(halves(2 * j + i % 2), P))
                if i > 0:
                    pe.wait_ge(ff_lo, i)
                    hi, lo = take()
                    for m in range(2):
                        for t in range(TT):
                            ts = slice(P * t, P * t + P)
                            for n in range(2):
                                ns = slice(512 * n, 512 * n + 512)
                                ins = three(ps[:, 4 + 2 * t + n, :], f_hi[:, m, ts], f_lo[:, m, ts],
                                            hi[:, m, ns], lo[:, m, ns], i == 1 and m == 0, i == n_ff and m == 1)
                    mark(ins)
            turn()
            pe.wait_ge(add_done, 8)
            mark(token_major([ps[:, 4, :], ps[:, 5, :]], 2))
            mark(token_major([ps[:, 6, :], ps[:, 7, :]], 2))
            mark(token_major([ps[:, 0, :], ps[:, 1, :]], 2))
            pe.wait_ge(proj_out, 16 + 8)
            turn()
            mark(token_major([ps[:, 4, :], ps[:, 5, :]], 2))
            mark(token_major([ps[:, 6, :], ps[:, 7, :]], 2))
            for r in range(4):
                t = r % 2
                pe.wait_ge(roped, r + 1)
                if r >= 2:
                    pe.wait_ge(rope_out, r - 1)
                for m in range(DH):
                    ins = nc.tensor.transpose(ps[:, 2 * t + m // 4, P * (m % 4):P * (m % 4) + P],
                                              rot[:, t, P * m:P * m + P], ident)
                if r >= 2:
                    for m in range(2):
                        ins = nc.tensor.transpose(ps[:, 2 * t + 1, 256 + P * m:256 + P * m + P],
                                                  qm_tok[:, t, P * m:P * m + P], ident)
                ins.then_inc(rope_turned, 1)
            pe.wait_ge(rope_out, 4)
            attention(NU0, len(units))
            turn()
            pe.wait_ge(u_out, len(units))
            out_projection()
            turn()
            pe.wait_ge(add_done, 12)
            hi, lo = take()
            for t in range(TT):
                for k in range(KT):
                    ts = slice(P * t, P * t + P)
                    ins = three(ps[:, 4, NE * t:NE * t + NE], act_hi[:, k, ts], act_lo[:, k, ts], hi[:, k, :],
                                lo[:, k, :], k == 0, k == KT - 1)
            mark(ins)
            strict = cst[:, C_STRICT:C_STRICT + P]
            pe.wait_ge(chosen, TT)
            nc.tensor.matmul(ps[:, 5, 0:NE], strict, msk[:, 0, :], start=True, stop=True)
            nc.tensor.matmul(ps[:, 5, NE:2 * NE], strict, msk[:, 1, :], start=True, stop=False)
            nc.tensor.matmul(ps[:, 5, NE:2 * NE], ones[:, :], msk[:, 0, :], start=False, stop=True)
            nc.tensor.matmul(ps[:, 5, 2 * NE:3 * NE], ones[:, :], msk[:, 0, :], start=True, stop=False)
            nc.tensor.matmul(ps[:, 5, 2 * NE:3 * NE], ones[:, :], msk[:, 1, :], start=False, stop=True)\
              .then_inc(ranks, 1)
            pe.wait_ge(routed, 1)

            def gather():
                for half in range(2):
                    for k in range(4):
                        c = P * (4 * half + k)
                        for t in range(TT):
                            ins = nc.tensor.matmul(ps[:, 1 + 2 * half, P * k:P * k + P], H[:, t, c:c + P], oh[:, t, :],
                                                   start=(t == 0), stop=(t == TT - 1))
                    ins.then_inc(disp, 1)

            def experts(sweep):
                done = sweep * NE
                base = NPRE + done * PER_EXPERT
                n_oh = sweep * 2 * (NE + 1)
                pe.wait_ge(oh_ready, n_oh + 2)
                if sweep:
                    pe.wait_ge(e_add, 4 * (NE + 1))
                gather()

                def scatter(i):
                    n_y = (i + sweep * (NE + 1)) * 2
                    for t in range(TT):
                        for n in range(2):
                            pe.wait_ge(e_yo, n_y + (2 if n + t else 1))
                            nc.tensor.matmul(ps[:, (1, 3, 4, 7)[2 * t + n], :], ohT[:, P * t:P * t + P],
                                             y_e[:, 512 * n:512 * n + 512], start=True, stop=True).then_inc(e_comb, 1)

                with pe.Fori(0, NE) as e:
                    u = [0]
                    pe.wait_ge(xg_l, 2 * e + n_oh + 2)

                    def expert_slot(kt, n):
                        s = base + u[0]
                        u[0] += 1
                        pe.wait_ge(lo_ready, e * PER_EXPERT + s + 1)
                        r = (s - NPRE) % E_SPLIT
                        return shaped(e_whi, r, kt, n), shaped(e_wlo, r, kt, n)

                    def product(bank):
                        for half in range(2):
                            hi, lo = expert_slot(4, 512)
                            for kk in range(4):
                                k = 4 * half + kk
                                ins = three(bank, xg_hi[:, k, :], xg_lo[:, k, :], hi[:, kk, :], lo[:, kk, :],
                                            k == 0, k == KT - 1)
                            ins.then_inc(slot_used, 1)

                    def turn_hidden(j):
                        pe.wait_ge(e_hr, (e + done) * STEPS + j + 1)
                        for m in range(4):
                            ins = nc.tensor.transpose(ps[:, 4, P * m:P * m + P], e_h[:, P * m:P * m + P], ident)
                        ins.then_inc(e_tr, 1)

                    def down(j):
                        pe.wait_ge(e_lo, (e + done) * STEPS + j + 1)
                        for half in range(2):
                            hi, lo = expert_slot(2, D)
                            for m in range(2):
                                f = 2 * half + m
                                for n in range(2):
                                    ns = slice(512 * n, 512 * n + 512)
                                    ins = three(ps[:, 5 + n, :], h_hi[:, f, :], h_lo[:, f, :], hi[:, m, ns],
                                                lo[:, m, ns], j == 0 and f == 0, j == STEPS - 1 and f == 3)
                            ins.then_inc(slot_used, 1)

                    for j in range(STEPS):
                        if j == 1:
                            pe.wait_ge(e_add, (e + sweep * (NE + 1)) * 4 + 4)
                        product(ps[:, j % 2, :])
                        if j > 0:
                            turn_hidden(j - 1)
                        if j == 1:
                            for t in range(TT):
                                ins = nc.tensor.transpose(ps[:, 7, P * t:P * t + P], oh[:, t, :], ident)
                            ins.then_inc(oh_turned, 1)
                        product(ps[:, 2 + j % 2, :])
                        if j == 0:
                            scatter(e)
                        if j > 0:
                            down(j - 1)
                    pe.wait_ge(oh_ready, 2 * e + n_oh + 4)
                    gather()
                    turn_hidden(STEPS - 1)
                    down(STEPS - 1)
                pe.wait_ge(xg_l, n_oh + 2 * NE + 2)
                scatter(NE)

            experts(0)
            over = pe.value_load(flag[0:1, 0:1], min_val=0, max_val=S)
            with pe.If(over > P):
                experts(1)


_INS = ["x", "mem", "g_mix", "g_ffn", "w_mem_kv", "w_out", "w_in_a", "w_gk_up", "b_gk", "g_gla", "g_kv", "w_kv",
        "w_in_b", "lambda_q1", "lambda_k1", "lambda_q2", "lambda_k2", "g_subln", "w_dense_gate", "w_dense_up",
        "w_dense_down", "w_router", "w_exp_gate", "w_exp_up", "w_exp_down", "g_final"]


def constants(np):
    p = np.arange(P)
    c = np.zeros((P, C_N), np.float32)
    c[:, C_ID:C_ID + P] = np.eye(P)
    c[:, C_IOTA:C_IOTA + S] = np.arange(S)
    c[:, C_STRICT:C_STRICT + P] = p[:, None] < p[None, :]
    c[:, C_CAUSAL + P:C_CAUSAL + 2 * P] = np.where(p[None, :] <= p[:, None], 0.0, NEG)
    c[:, C_GLA:C_GLA + CHUNK] = (p[:, None] % CHUNK) <= np.arange(CHUNK)[None, :]
    half = HEAD_DIM // 2
    inv = (np.float32(10000.0) ** (-np.arange(half, dtype=np.float32) / np.float32(half))).astype(np.float32)
    ang = np.arange(S, dtype=np.float32)[:, None] * inv[None, :]
    for t in range(TT):
        a = ang[P * t:P * t + P].astype(np.float64)
        c[:, C_ROPE + 64 * t:C_ROPE + 64 * t + 32] = np.cos(a)
        c[:, C_ROPE + 64 * t + 32:C_ROPE + 64 * t + 64] = np.sin(a)
    c[:, C_EPS] = EPS
    return c


def kernel(**inputs):
    import numpy as _np
    import concourse.bacc as _bacc
    from concourse import mybir as _mybir
    from concourse.bass_utils import run_bass_kernel_spmd as _run

    nc = _bacc.Bacc("TRN2", target_bir_lowering=False, num_devices=1)
    arrays, args = {}, []
    for name in _INS:
        a = _np.ascontiguousarray(inputs[name])
        arrays[f"in_{name}_dram"] = a
        args.append(nc.dram_tensor(f"in_{name}_dram", a.shape, _mybir.dt.from_np(a.dtype), kind="ExternalInput").ap())
    c = constants(_np)
    arrays["in_consts_dram"] = c
    args.append(nc.dram_tensor("in_consts_dram", c.shape, F32, kind="ExternalInput").ap())
    args.append(nc.dram_tensor("out_0_dram", (1, S, D), F32, kind="ExternalOutput").ap())
    trunk(nc, *args)
    r = _run(nc, [arrays], core_ids=[0])
    return r.results[0]["out_0_dram"]
```

```python
import math
from contextlib import ExitStack

import concourse.bass as bass
from concourse import mybir

F32 = mybir.dt.float32
F32R = mybir.dt.float32r
U32 = mybir.dt.uint32
I32 = mybir.dt.int32
ALU = mybir.AluOpType
ACT = mybir.ActivationFunctionType
AX = mybir.AxisListType

P = 128
D = 1024
S = 256
KT = D // P
TT = S // P
MEM_HEADS, HEAD_DIM = 4, 64
MEM_DIM = MEM_HEADS * HEAD_DIM
MIX = D - MEM_DIM
GH, GDV, GDK, RANK, CHUNK = 4, 192, 96, 16, 64
NCH = S // CHUNK
DH, DV = 6, 128
F_DENSE, F_EXP, NE = 2816, 3584, 8
EPS = 1e-6
LAMBDA_INIT = 0.8 - 0.6 * math.exp(-0.3)
NEG = -3.0e38

SLOT = 2048
RAW = 7
SPLIT = 3
E_SPLIT = 6

C_ID, C_IOTA, C_STRICT, C_CAUSAL, C_GLA, C_ROPE, C_EPS = 0, 128, 384, 512, 640, 704, 832
C_N = 833


def prefill_slots(w):
    slots, first = [], {}

    def add(stage, src, k0, kt, n0, n):
        first.setdefault(stage, len(slots))
        slots.append((src, k0, kt, n0, n))

    for l in range(2):
        add("mem_kv", w["w_mem_kv"][l], 0, 8, 0, 256)
        add("mem_kv", w["w_mem_kv"][l], 0, 8, 256, 256)
    add("in_a", w["w_in_a"][0], 0, 8, 2 * GH * GDK + 2 * MIX, RANK)
    add("in_a", w["w_in_a"][0], 0, 8, W_QMEM, MEM_DIM)
    for i in range(4):
        add("in_a", w["w_in_a"][0], 0, 8, 192 * i, 192)
    for base in (768, 1536):
        add("in_a", w["w_in_a"][0], 0, 4, base, 512)
        add("in_a", w["w_in_a"][0], 4, 4, base, 512)
        add("in_a", w["w_in_a"][0], 0, 8, base + 512, 256)

    def blocks(stage, src, nb):
        for b in range(nb):
            add(stage, src, 0, 4, 512 * b, 512)
            add(stage, src, 4, 4, 512 * b, 512)

    blocks("out_a", w["w_out"][0], 2)
    n = F_DENSE // 256
    for i in range(n + 1):
        if i < n:
            add("dense", w["w_dense_gate"][0], 0, 8, 256 * i, 256)
            add("dense", w["w_dense_up"][0], 0, 8, 256 * i, 256)
        if i > 0:
            add("dense", w["w_dense_down"][0], 2 * (i - 1), 2, 0, D)
    blocks("kv", w["w_kv"], 3)
    blocks("in_b", w["w_in_b"][0], 2)
    blocks("out_b", w["w_out"][1], 2)
    add("router", w["w_router"][0], 0, 8, 0, NE)
    first["experts"] = len(slots)
    return slots, first


W_QMEM = 2 * GH * GDK + 2 * MIX + RANK
STEPS = F_EXP // 512
PER_EXPERT = 6 * STEPS


def trunk(nc, x, mem, g_mix, g_ffn, w_mem_kv, w_out, w_in_a, w_gk_up, b_gk, g_gla, g_kv, w_kv, w_in_b,
          lambda_q1, lambda_k1, lambda_q2, lambda_k2, g_subln, w_dense_gate, w_dense_up, w_dense_down,
          w_router, w_exp_gate, w_exp_up, w_exp_down, g_final, consts, out):
    W = dict(w_mem_kv=w_mem_kv, w_out=w_out, w_in_a=w_in_a, w_kv=w_kv, w_in_b=w_in_b,
             w_dense_gate=w_dense_gate, w_dense_up=w_dense_up, w_dense_down=w_dense_down, w_router=w_router)
    slots, first = prefill_slots(W)
    NPRE = first["experts"]

    with ExitStack() as ctx:
        def sb(name, shape, dt=F32):
            return ctx.enter_context(nc.sbuf_tensor(name, shape, dt))

        def sem(name):
            return ctx.enter_context(nc.semaphore(name))

        raw = sb("raw", [P, RAW, SLOT])
        act_hi = sb("act_hi", [P, KT, S], F32R)
        act_lo = sb("act_lo", [P, KT, S], F32R)
        xres = sb("xres", [P, TT, D])
        H = sb("H", [P, TT, D])
        gain = sb("gain", [P, D])
        cst = sb("cst", [P, C_N])
        ones = sb("ones", [P, P])
        small = sb("small", [P, 136])
        rsc = sb("rsc", [P, 5, TT, NE])
        bgk = sb("bgk", [GDK, GH])
        idx8 = sb("idx8", [P, TT, 8], U32)
        route_gate = sb("route_gate", [P, TT, NE + 1])
        route_rank = sb("route_rank", [P, TT, NE + 1])
        flag = sb("flag", [1, 8], I32)

        ps = ctx.enter_context(nc.psum_tensor("ps", [P, 8, 512], F32))

        with ExitStack() as prefill:
            def sbp(name, shape, dt=F32):
                return prefill.enter_context(nc.sbuf_tensor(name, shape, dt))

            w_hi = sbp("w_hi", [P, SPLIT, SLOT], F32R)
            w_lo = sbp("w_lo", [P, SPLIT, SLOT], F32R)
            T = sbp("T", [P, 8, D])
            v_tok = sbp("v_tok", [P, TT, MIX])
            kmT = sbp("kmT", [P, 2, 2, S])
            vm = sbp("vm", [P, 2, TT, MEM_DIM])
            qmT = sbp("qmT", [P, 2, S])
            sc = sbp("sc", [P, 3, 512])
            ggla = sbp("ggla", [P, GDV])
            gsub = sbp("gsub", [P, DV])
            with nc.sbuf_tensor("pT", [P, 2, 512], F32) as pT:
                pass
            f_hi = sbp("f_hi", [P, 2, S], F32R)
            f_lo = sbp("f_lo", [P, 2, S], F32R)

        e_whi = sb("e_whi", [P, E_SPLIT, SLOT], F32R)
        e_wlo = sb("e_wlo", [P, E_SPLIT, SLOT], F32R)
        oh = sb("oh", [P, TT, P])
        ohT = sb("ohT", [P, S])
        e_h = sb("e_h", [P, 512])
        y_e = sb("y_e", [P, D])
        xg_hi, xg_lo = act_hi[:, :, 0:P], act_lo[:, :, 0:P]
        h_hi, h_lo = act_hi[:, 0:4, P:S], act_lo[:, 0:4, P:S]

        ident = cst[:, C_ID:C_ID + P]
        cos_sin = cst[:, C_ROPE:C_ROPE + 128].rearrange("p (t c d) -> p t c d", t=TT, c=2)
        eps = cst[:, C_EPS:C_EPS + 1]
        ss, rms, rs = small[:, 0:2], small[:, 2:4], small[:, 4:6]
        nmax, nbias, rsum = small[:, 8:14], small[:, 14:20], small[:, 20:26]
        rinv = small[:, 128:136]
        lamc = small[:, 32:40]
        hss, hrms, hrs = small[:, 40:52], small[:, 52:64], small[:, 64:76]
        blend = small[:, 120:123]
        cur_rank, cur_gate = small[:, 76:78], small[:, 78:80]
        rt = small[:, 80:120]

        gq, gk_, gb, gd = (T[0:GDK, i, :] for i in range(4))
        ge, gf, qi, ki = (T[0:GDK, i, :] for i in range(4, 8))
        state = [T[0:GDK, i, 0:3 * GDV].rearrange("p (n v) -> p n v", n=3) for i in (2, 5)]
        kdT = [T[:, i, 576:768].rearrange("p (t n) -> p t n", t=TT) for i in (2, 5)]
        sT = [T[:, i, 768:1024].rearrange("p (t n) -> p t n", t=TT) for i in (2, 5)]
        gla_sq = T[:, 3, 0:TT * GDV].rearrange("p (t n) -> p t n", t=TT)
        lam4 = sc[:, 0, 0:4 * HEAD_DIM].rearrange("p (i n) -> p i n", i=4)
        wgk = sc[0:RANK, 1, 0:GH * GDK]
        f_gate, f_h = T[:, 0, 0:512], T[:, 1, 0:512]
        flatT = T[:, :, :].rearrange("p a b -> p (a b)")
        k_raw = flatT[:, 0:1536].rearrange("p (t n) -> p t n", t=TT)
        q_raw = flatT[:, 1536:3072].rearrange("p (t n) -> p t n", t=TT)
        rot = flatT[:, 3072:4608].rearrange("p (t n) -> p t n", t=TT)
        kT = flatT[:, 4608:6144].rearrange("p (h s) -> p h s", h=DH)
        qT = flatT[:, 6144:7680].rearrange("p (h s) -> p h s", h=DH)
        qm_tok = flatT[:, 7680:8192].rearrange("p (t n) -> p t n", t=TT)
        rope_t = sc[:, :, :].rearrange("p a b -> p (a b)")[:, 0:1536].rearrange("p (a n) -> p a n", a=4)
        diff_o = flatT[:, 0:1536].rearrange("p (t n) -> p t n", t=TT)
        diff_sq = flatT[:, 1536:3072].rearrange("p (t n) -> p t n", t=TT)
        top8, fidx, msk, sel1, sel2 = (rsc[:, i, :, :] for i in range(5))
        logT = sc[0:NE, 2, 0:S]

        const_in = sem("const_in")
        small_in = sem("small_in")
        mem_in = sem("mem_in")
        x_in = sem("x_in")
        gain_in = sem("gain_in")
        raw_in = [sem(f"raw_in{r}") for r in range(RAW)]
        hi_ready = sem("hi_ready")
        lo_ready = sem("lo_ready")
        slot_used = sem("slot_used")
        h_ready = sem("h_ready")
        turned = sem("turned")
        turn_hi = sem("turn_hi")
        turn_lo = sem("turn_lo")
        rms_ready = sem("rms_ready")
        proj_out = sem("proj_out")
        add_done = sem("add_done")
        gk_logit = sem("gk_logit")
        gk_act = sem("gk_act")
        gk_vec = sem("gk_vec")
        gla_sc = sem("gla_sc")
        gla_sce = sem("gla_sce")
        gla_kv = sem("gla_kv")
        gla_st = sem("gla_st")
        gla_od = sem("gla_od")
        gla_oe = sem("gla_oe")
        gla_rms = sem("gla_rms")
        diff_sqs = sem("diff_sqs")
        diff_rms = sem("diff_rms")
        roped = sem("roped")
        rope_turned = sem("rope_turned")
        rope_out = sem("rope_out")
        u_score = sem("u_score")
        u_max = sem("u_max")
        u_exp = sem("u_exp")
        u_prob = sem("u_prob")
        u_turned = sem("u_turned")
        u_pT = sem("u_pT")
        u_val = sem("u_val")
        u_out = sem("u_out")
        ff_silu = sem("ff_silu")
        ff_h = sem("ff_h")
        ff_hi = sem("ff_hi")
        ff_lo = sem("ff_lo")
        lam_v = sem("lam_v")
        lam_a = sem("lam_a")
        logits_out = sem("logits_out")
        logits_turned = sem("logits_turned")
        top_d = sem("top_d")
        top_e = sem("top_e")
        chosen = sem("chosen")
        ranks = sem("ranks")
        routed = sem("routed")
        oh_ready = sem("oh_ready")
        oh_turned = sem("oh_turned")
        ohT_ready = sem("ohT_ready")
        disp = sem("disp")
        xg_h = sem("xg_h")
        xg_l = sem("xg_l")
        e_silu = sem("e_silu")
        e_hr = sem("e_hr")
        e_tr = sem("e_tr")
        e_hi = sem("e_hi")
        e_lo = sem("e_lo")
        e_yo = sem("e_yo")
        e_comb = sem("e_comb")
        e_add = sem("e_add")
        cur_done = sem("cur_done")
        dve_step = sem("dve_step")
        act_step = sem("act_step")
        out_ready = sem("out_ready")
        out_done = sem("out_done")

        def shaped(buf, i, kt, n):
            return buf[:, i, 0:kt * n].rearrange("p (k n) -> p k n", k=kt)

        def gate_end(j):
            return 2 if j == 0 else 6 * j

        def slot_shape(s):
            _, _, kt, _, n = slots[s]
            return kt, n

        units = [("mem", 0, m, t) for m in range(MEM_HEADS // 2) for t in range(TT)]
        NU0 = len(units)
        units += [("mem", 1, m, t) for m in range(MEM_HEADS // 2) for t in range(TT)]
        units += [("diff", 1, h, t) for h in range(DH) for t in range(TT)]
        U_BANK = {"score": (0, 6), "turn": (2, 3), "val": (4, 5)}

        def unit_keys(u):
            kind, _, _, t = units[u]
            return S if kind == "mem" else P * (t + 1)

        def unit_scores_bank(u):
            b = U_BANK["score"][u % 2]
            return ps[:, b:b + 2, 0:unit_keys(u)]

        block = ctx.enter_context(nc.Block())

        @block.sync
        def _(sp):
            sp.dma_start(cst[:, :], consts).then_inc(const_in, 16)
            for t in range(TT):
                sp.dma_start(H[:, t, :], mem[0, P * t:P * t + P, :]).then_inc(mem_in, 16)
            for s, (src, k0, kt, n0, n) in enumerate(slots):
                if s == 2:
                    sp.dma_start(xres[:, :, :], x[0].rearrange("(t p) d -> p t d", p=P)).then_inc(x_in, 16)
                if s >= RAW:
                    sp.wait_ge(lo_ready, s - RAW + 1)
                with nc.allow_non_contiguous_dma(reason="router columns"):
                    sp.dma_start(shaped(raw, s % RAW, kt, n),
                                 src.rearrange("(k p) n -> p k n", p=P)[:, k0:k0 + kt, n0:n0 + n])\
                      .then_inc(raw_in[s % RAW], 16)

            def expert_loads(sweep):
                base = NPRE + sweep * NE * PER_EXPERT
                with sp.Fori(0, NE) as e:
                    u = 0
                    for j in range(STEPS + 1):
                        for wgt in ((w_exp_gate, w_exp_up) if j < STEPS else ()):
                            for half in range(2):
                                s = base + u
                                sp.wait_ge(lo_ready, e * PER_EXPERT + s - RAW + 1)
                                sp.dma_start(shaped(raw, s % RAW, 4, 512),
                                             wgt[0, e].rearrange("(k p) n -> p k n", p=P)
                                             [:, 4 * half:4 * half + 4, 512 * j:512 * j + 512])\
                                  .then_inc(raw_in[s % RAW], 16)
                                u += 1
                        for half in (range(2) if j > 0 else ()):
                            s = base + u
                            sp.wait_ge(lo_ready, e * PER_EXPERT + s - RAW + 1)
                            k0 = 4 * (j - 1) + 2 * half
                            sp.dma_start(shaped(raw, s % RAW, 2, D),
                                         w_exp_down[0, e].rearrange("(k p) n -> p k n", p=P)[:, k0:k0 + 2, :])\
                              .then_inc(raw_in[s % RAW], 16)
                            u += 1

            expert_loads(0)
            sp.wait_ge(routed, 1)
            over = sp.value_load(flag[0:1, 0:1], min_val=0, max_val=S)
            with sp.If(over > P):
                expert_loads(1)
            for t in range(TT):
                sp.wait_ge(out_ready, t + 1)
                sp.dma_start(out[0, P * t:P * t + P, :], H[:, t, :]).then_inc(out_done, 16)
            sp.wait_ge(out_done, 16 * TT)

        @block.gpsimd
        def _(pool):
            gains = [g_mix[0:1, :], g_ffn[0:1, :], g_kv.rearrange("(a d) -> a d", a=1), g_mix[1:2, :],
                     g_ffn[1:2, :], g_final.rearrange("(a d) -> a d", a=1)]
            pool.dma_start(gain[:, :], gains[0].to_broadcast([P, D])).then_inc(gain_in, 16)
            pool.dma_start(wgk, w_gk_up[0]).then_inc(small_in, 16)
            with nc.allow_non_contiguous_dma(reason="384 gate biases"):
                pool.dma_start(bgk[:, :], b_gk[0].rearrange("(h p) -> p h", p=GDK)).then_inc(small_in, 16)
            pool.dma_start(ggla[:, :], g_gla[0:1, :].to_broadcast([P, GDV])).then_inc(small_in, 16)
            pool.dma_start(gsub[:, :], g_subln[0:1, :].to_broadcast([P, DV])).then_inc(small_in, 16)
            for i, v in enumerate((lambda_q1, lambda_k1, lambda_q2, lambda_k2)):
                pool.dma_start(lam4[:, i, :], v[0:1, :].to_broadcast([P, HEAD_DIM])).then_inc(small_in, 16)
            for n, used in zip(range(1, len(gains)), (2, 6, 8, 10, 14)):
                pool.wait_ge(h_ready, used)
                pool.dma_start(gain[:, :], gains[n].to_broadcast([P, D])).then_inc(gain_in, 16)

        N_IN_A = 4 + 12
        N_SMALL = 16 * 8

        @block.scalar
        def _(act):
            steps = [0]

            def link(ins):
                steps[0] += 1
                ins.then_inc(act_step, 1)
                act.wait_ge(act_step, steps[0])

            split = [0]

            def split_to(end):
                for s in range(split[0], end):
                    kt, n = slot_shape(s)
                    act.wait_ge(raw_in[s % RAW], 16 * (s // RAW + 1))
                    if s >= SPLIT:
                        act.wait_ge(slot_used, s - SPLIT + 1)
                    nc.scalar.activation(w_hi[:, s % SPLIT, 0:kt * n], raw[:, s % RAW, 0:kt * n], ACT.Copy)\
                      .then_inc(hi_ready, 1)
                split[0] = max(split[0], end)

            turns = [0]

            def turn():
                n = turns[0]
                for t in range(TT):
                    for half in range(2):
                        act.wait_ge(turned, 4 * n + 2 * t + half + 1)
                        nc.scalar.activation(
                            act_hi[:, 4 * half:4 * half + 4, P * t:P * t + P],
                            ps[:, 2 * t + half, :].rearrange("p (k n) -> p k n", k=4), ACT.Copy).then_inc(turn_hi, 1)
                turns[0] += 1

            def norm(ready, counts):
                for t in range(TT):
                    act.wait_ge(ready, counts[t])
                    link(nc.scalar.activation(H[:, t, :], xres[:, t, :], ACT.Square, accum_out=ss[:, t:t + 1]))
                    nc.scalar.activation(rms[:, t:t + 1], ss[:, t:t + 1], ACT.Sqrt, bias=eps, scale=1.0 / D)\
                      .then_inc(rms_ready, 1)

            def proj(after, dst, src, func=ACT.Copy):
                act.wait_ge(slot_used, after)
                nc.scalar.activation(dst, src, func).then_inc(proj_out, 1)

            def unit_exp(u):
                nk = unit_keys(u)
                act.wait_ge(u_max, u + 1)
                for i in range(2):
                    c = 2 * (u % 3) + i
                    ins = nc.scalar.activation(sc[:, u % 3, 256 * i:256 * i + nk], unit_scores_bank(u)[:, i, :],
                                               ACT.Exp, bias=nbias[:, c:c + 1], scale=HEAD_DIM ** -0.5,
                                               accum_out=rsum[:, c:c + 1])
                ins.then_inc(u_exp, 1)

            def unit_copy(u):
                n = 2 * S if units[u][0] == "mem" else unit_keys(u)
                act.wait_ge(u_turned, u + 1)
                nc.scalar.activation(pT[:, u % 2, 0:n], ps[:, U_BANK["turn"][u % 2], 0:n], ACT.Copy)\
                  .then_inc(u_pT, 1)

            def unit_square(u):
                kind, _, h, t = units[u]
                if kind == "diff":
                    act.wait_ge(u_out, u + 1)
                    hs = slice(DV * h, DV * h + DV)
                    nc.scalar.activation(diff_sq[:, t, hs], diff_o[:, t, hs], ACT.Square,
                                         accum_out=hss[:, DH * t + h:DH * t + h + 1]).then_inc(diff_sqs, 1)

            def attention(u0, u1):
                for i in range(u0, u1 + 4):
                    if i < u1:
                        unit_exp(i)
                    if u0 <= i - 2 < u1:
                        unit_copy(i - 2)
                    if u0 <= i - 4:
                        unit_square(i - 4)

            split_to(1)
            turn()
            for l in range(2):
                split_to(2 * l + 2)
                proj(2 * l + 1, kmT[:, l, :, :], ps[:, 4 + 2 * l, :].rearrange("p (m s) -> p m s", m=2))
                proj(2 * l + 2, vm[:, l, :, :], ps[:, 5 + 2 * l, :].rearrange("p (t n) -> p t n", t=TT))
                split_to(min(2 * l + 4, 4))
            norm(x_in, (16, 16))
            split_to(4 + 3)
            turn()
            a = first["in_a"]
            proj(a + 1, gd[0:RANK, 0:S], ps[0:RANK, 4, 0:S])
            split_to(a + 4)
            proj(a + 2, qmT[:, :, :], ps[:, 5, :].rearrange("p (m s) -> p m s", m=2))
            act.wait_ge(small_in, N_SMALL)
            act.wait_ge(gk_logit, 1)
            for h in range(GH):
                ins = nc.scalar.activation(ge[:, S * h:S * h + S], ps[0:GDK, 6 + h // 2, S * (h % 2):S * (h % 2) + S],
                                           ACT.Identity, bias=bgk[:, h:h + 1])
            ins.then_inc(gk_act, 1)
            act.wait_ge(gk_act, 1)
            nc.scalar.activation(gf, ge, ACT.Abs).then_inc(gk_act, 1)
            act.wait_ge(gk_act, 2)
            nc.scalar.activation(gf, gf, ACT.Exp, scale=-1.0).then_inc(gk_act, 1)
            act.wait_ge(gk_act, 3)
            nc.scalar.activation(gf, gf, ACT.Ln, bias=1.0).then_inc(gk_act, 1)
            split_to(a + 6)
            for i in range(4):
                dst = (gq, gk_)[i // 2][:, 512 * (i % 2):512 * (i % 2) + 512]
                proj(a + 3 + i, dst, ps[0:GDK, i, :])
            split_to(a + 9)
            for t in range(TT):
                proj(a + 8, v_tok[:, t, 0:512], ps[:, 4 + t, :])
            proj(a + 9, v_tok[:, :, 512:768], ps[:, 6, :].rearrange("p (t n) -> p t n", t=TT))
            split_to(a + 12)
            for t in range(TT):
                proj(a + 11, H[:, t, 0:512], ps[:, 7 * (1 - t), :], ACT.Silu)
            proj(a + 12, H[:, :, 512:768], ps[:, 1, :].rearrange("p (t n) -> p t n", t=TT), ACT.Silu)
            act.wait_ge(gk_vec, 2)
            nc.scalar.activation(ge, gd, ACT.Exp, scale=1.0 / 16).then_inc(gk_act, 1)
            nc.scalar.activation(gf, gd, ACT.Exp, scale=-1.0 / 16).then_inc(gk_act, 1)
            act.wait_ge(gk_vec, 3)
            nc.scalar.activation(ge, gb, ACT.Exp, scale=1.0 / 16).then_inc(gk_act, 1)
            act.wait_ge(gk_vec, 5)
            nc.scalar.activation(gf, gd, ACT.Exp, scale=1.0 / 16).then_inc(gk_act, 1)
            act.wait_ge(gk_act, 8)
            attention(0, NU0)
            split_to(a + 12 + 2)

            for h in range(GH):
                act.wait_ge(gla_od, h + 1)
                for t in range(TT):
                    ins = nc.scalar.activation(gla_sq[:, t, :], ps[:, 4 + h % 2, 256 * t:256 * t + GDV], ACT.Square,
                                               accum_out=hss[:, TT * h + t:TT * h + t + 1])
                link(ins)
                hs = slice(TT * h, TT * h + TT)
                nc.scalar.activation(hrms[:, hs], hss[:, hs], ACT.Sqrt, bias=eps, scale=1.0 / GDV).then_inc(gla_rms, 1)
            turn()
            split_to(first["dense"] + 1)
            norm(add_done, (2, 4))
            split_to(first["dense"] + 2)
            turn()
            d = first["dense"]
            n_ff = F_DENSE // 256
            for i in range(n_ff + 1):
                base = d + 3 * i - (1 if i > 0 else 0)
                if i < n_ff:
                    split_to(base + 2)
                if i > 0:
                    act.wait_ge(ff_h, i)
                    if i > 1:
                        act.wait_ge(slot_used, base)
                    nc.scalar.activation(f_hi[:, :, :], f_h.rearrange("p (m s) -> p m s", m=2), ACT.Copy)\
                      .then_inc(ff_hi, 1)
                if i < n_ff:
                    act.wait_ge(slot_used, base + 1)
                    nc.scalar.activation(f_gate, ps[:, i % 2, :], ACT.Silu).then_inc(ff_silu, 1)
                if i > 0:
                    split_to(base + (3 if i < n_ff else 1))
            split_to(first["kv"] + 2)
            norm(add_done, (6, 8))
            turn()
            k = first["kv"]
            split_to(k + 4)
            for t in range(TT):
                proj(k + 2, k_raw[:, t, 0:512], ps[:, 4 + t, :])
            split_to(k + 6)
            for t in range(TT):
                proj(k + 4, k_raw[:, t, 512:768], ps[:, 6 + t, 0:256])
                proj(k + 4, v_tok[:, t, 0:256], ps[:, 6 + t, 256:512])
            for t in range(TT):
                proj(k + 6, v_tok[:, t, 256:768], ps[:, t, :])
            b = first["in_b"]
            split_to(b + 2)
            turn()
            split_to(b + 4)
            for t in range(TT):
                proj(b + 2, q_raw[:, t, 0:512], ps[:, 4 + t, :])
            for t in range(TT):
                proj(b + 4, q_raw[:, t, 512:768], ps[:, 6 + t, 0:256])
                proj(b + 4, qm_tok[:, t, :], ps[:, 6 + t, 256:512])
            for r in range(4):
                dst, t = (kT, qT)[r // 2], r % 2
                act.wait_ge(rope_turned, r + 1)
                nc.scalar.activation(dst[:, 0:4, P * t:P * t + P],
                                     ps[:, 2 * (r % 2), :].rearrange("p (m n) -> p m n", m=4), ACT.Copy)
                if r >= 2:
                    nc.scalar.activation(qmT[:, :, P * t:P * t + P],
                                         ps[:, 2 * (r % 2) + 1, 256:512].rearrange("p (m n) -> p m n", m=2), ACT.Copy)
                nc.scalar.activation(dst[:, 4:6, P * t:P * t + P],
                                     ps[:, 2 * (r % 2) + 1, 0:256].rearrange("p (m n) -> p m n", m=2), ACT.Copy)\
                  .then_inc(rope_out, 1)
            act.wait_ge(lam_v, 1)
            nc.scalar.activation(lamc[:, 2:4], lamc[:, 0:2], ACT.Exp).then_inc(lam_a, 1)
            attention(NU0, len(units))
            act.wait_ge(diff_sqs, TT * DH)
            nc.scalar.activation(hrms, hss, ACT.Sqrt, bias=eps, scale=1.0 / DV).then_inc(diff_rms, 1)
            split_to(first["out_b"] + 3)
            turn()
            split_to(NPRE - 1)
            norm(add_done, (10, 12))
            split_to(NPRE)
            turn()
            act.wait_ge(top_d, 1)
            nc.scalar.activation(rt[:, 2:4], rt[:, 0:2], ACT.Exp).then_inc(top_e, 1)

            def gathered(sweep, e):
                for half in range(2):
                    act.wait_ge(disp, sweep * 2 * (NE + 1) + 2 * e + half + 1)
                    nc.scalar.activation(xg_hi[:, 4 * half:4 * half + 4, :],
                                         ps[:, 1 + 2 * half, :].rearrange("p (k n) -> p k n", k=4), ACT.Copy)\
                      .then_inc(xg_h, 1)

            def experts(sweep):
                done = sweep * NE
                base = NPRE + done * PER_EXPERT

                def evacuate_y(i):
                    act.wait_ge(slot_used, i * PER_EXPERT + base)
                    if sweep == 0:
                        act.wait_ge(routed, 1)
                    nc.scalar.activation(y_e[:, 0:512], ps[:, 5, :], ACT.Copy).then_inc(e_yo, 1)
                    nc.scalar.activation(y_e[:, 512:1024], ps[:, 6, :], ACT.Copy).then_inc(e_yo, 1)

                with act.Fori(0, NE) as e:
                    u = [0]

                    def split_next(n):
                        for _ in range(n):
                            s = base + u[0]
                            act.wait_ge(raw_in[s % RAW], e * (16 * PER_EXPERT // RAW) + 16 * (s // RAW + 1))
                            act.wait_ge(slot_used, e * PER_EXPERT + s - E_SPLIT + 1)
                            nc.scalar.activation(e_whi[:, (s - NPRE) % E_SPLIT, :], raw[:, s % RAW, :], ACT.Copy)\
                              .then_inc(hi_ready, 1)
                            u[0] += 1

                    def hidden(j):
                        act.wait_ge(e_tr, (e + done) * STEPS + j + 1)
                        nc.scalar.activation(h_hi, ps[:, 4, :].rearrange("p (m n) -> p m n", m=4), ACT.Copy)\
                          .then_inc(e_hi, 1)

                    split_next(2)
                    gathered(sweep, e)
                    for j in range(STEPS):
                        split_next(2)
                        if j == 0:
                            evacuate_y(e)
                        if j == 1:
                            act.wait_ge(oh_turned, e + done + 1)
                            nc.scalar.activation(ohT[:, :], ps[:, 7, 0:256], ACT.Copy).then_inc(ohT_ready, 1)
                        if j > 0:
                            split_next(2)
                            hidden(j - 1)
                        act.wait_ge(slot_used, e * PER_EXPERT + base + gate_end(j))
                        nc.scalar.activation(e_h[:, :], ps[:, j % 2, :], ACT.Silu).then_inc(e_silu, 1)
                        split_next(2)
                    hidden(STEPS - 1)
                evacuate_y(NE)

            act.wait_ge(slot_used, NPRE)
            experts(0)
            act.wait_ge(routed, 1)
            over = act.value_load(flag[0:1, 0:1], min_val=0, max_val=S)
            with act.If(over > P):
                experts(1)
                act.wait_ge(e_add, 2 * 4 * (NE + 1))
            norm(e_add, (4 * (NE + 1) - 2, 4 * (NE + 1)))

        @block.vector
        def _(dve):
            steps = [0]

            def link(ins):
                steps[0] += 1
                ins.then_inc(dve_step, 1)
                dve.wait_ge(dve_step, steps[0])

            split = [0]

            def split_to(end):
                for s in range(split[0], end):
                    kt, n = slot_shape(s)
                    dve.wait_ge(hi_ready, s + 1)
                    nc.vector.tensor_tensor(w_lo[:, s % SPLIT, 0:kt * n], raw[:, s % RAW, 0:kt * n],
                                            w_hi[:, s % SPLIT, 0:kt * n].bitcast(F32), ALU.subtract)\
                      .then_inc(lo_ready, 1)
                split[0] = max(split[0], end)

            turns = [0]

            def turn():
                n = turns[0]
                for t in range(TT):
                    for half in range(2):
                        dve.wait_ge(turn_hi, 4 * n + 2 * t + half + 1)
                        ks = slice(4 * half, 4 * half + 4)
                        nc.vector.tensor_tensor(
                            act_lo[:, ks, P * t:P * t + P], ps[:, 2 * t + half, :].rearrange("p (k n) -> p k n", k=4),
                            act_hi[:, ks, P * t:P * t + P].bitcast(F32), ALU.subtract).then_inc(turn_lo, 1)
                turns[0] += 1

            norms = [0]

            def norm(signal, streams, new=True):
                n = norms[0]
                dve.wait_ge(gain_in, 16 * (n + 1))
                for t in range(TT):
                    if new:
                        dve.wait_ge(rms_ready, TT * (streams - 1) + t + 1)
                        link(nc.vector.reciprocal(rs[:, t:t + 1], rms[:, t:t + 1]))
                    nc.vector.scalar_tensor_tensor(out=H[:, t, :], in0=xres[:, t, :], scalar=rs[:, t:t + 1],
                                                   in1=gain[:, :], op0=ALU.mult, op1=ALU.mult).then_inc(signal, 1)
                norms[0] += 1

            def residual(banks, after):
                dve.wait_ge(slot_used, after)
                for i, b in enumerate(banks):
                    xs = xres[:, i // 2, 512 * (i % 2):512 * (i % 2) + 512]
                    nc.vector.tensor_tensor(xs, xs, ps[:, b, :], ALU.add).then_inc(add_done, 1)

            def unit_max(u):
                c = 2 * (u % 3)
                scores = unit_scores_bank(u)
                dve.wait_ge(u_score, u + 1)
                if units[u][0] == "diff":
                    last = scores[:, :, unit_keys(u) - P:unit_keys(u)]
                    m = cst[:, C_CAUSAL:C_CAUSAL + P].rearrange("p (o n) -> p o n", o=1).to_broadcast([P, 2, P])
                    link(nc.vector.tensor_tensor(last, last, m, ALU.add))
                link(nc.vector.tensor_reduce(nmax[:, c:c + 2], scores, AX.X, ALU.max, negate=True))
                nc.vector.tensor_scalar(nbias[:, c:c + 2], nmax[:, c:c + 2], HEAD_DIM ** -0.5, None, ALU.mult)\
                  .then_inc(u_max, 1)

            def unit_prob(u):
                nk = unit_keys(u)
                c, r = 2 * (u % 3), 2 * (u % 4)
                b0, b1 = sc[:, u % 3, 0:nk], sc[:, u % 3, 256:256 + nk]
                w = blend[:, u % 3:u % 3 + 1]
                dve.wait_ge(u_exp, u + 1)
                if units[u][0] == "mem":
                    nc.vector.reciprocal(rinv[:, r:r + 2], rsum[:, c:c + 2]).then_inc(u_prob, 1)
                    return
                link(nc.vector.reciprocal(rinv[:, r:r + 2], rsum[:, c:c + 2]))
                link(nc.vector.tensor_scalar(w, rinv[:, r + 1:r + 2], rsum[:, c:c + 1], lamc[:, 5:6],
                                             ALU.mult, ALU.mult))
                nc.vector.scalar_tensor_tensor(out=b0, in0=b1, scalar=w, in1=b0, op0=ALU.mult, op1=ALU.add)\
                  .then_inc(u_prob, 1)

            def unit_out(u):
                kind, _, h, t = units[u]
                r = 2 * (u % 4)
                val = ps[:, U_BANK["val"][u % 2], 0:P]
                dve.wait_ge(u_val, u + 1)
                if kind == "diff":
                    nc.vector.tensor_scalar(diff_o[:, t, DV * h:DV * h + DV], val, rinv[:, r:r + 1], None, ALU.mult)\
                      .then_inc(u_out, 1)
                    return
                for i in range(2):
                    f = MIX + HEAD_DIM * (2 * h + i)
                    ins = nc.vector.tensor_scalar(H[:, t, f:f + HEAD_DIM], val[:, HEAD_DIM * i:HEAD_DIM * (i + 1)],
                                                  rinv[:, r + i:r + i + 1], None, ALU.mult)
                ins.then_inc(u_out, 1)

            def attention(u0, u1):
                for i in range(u0, u1 + 3):
                    if i < u1:
                        unit_max(i)
                    if u0 <= i - 1 < u1:
                        unit_prob(i - 1)
                    if u0 <= i - 3:
                        unit_out(i - 3)

            def head_roots(n):
                link(nc.vector.reciprocal(hrs[:, n], hrms[:, n]))

            link(nc.vector.memset(ones[:, :], 1.0))
            split_to(1)
            turn()
            split_to(4)
            norm(h_ready, 1)
            split_to(4 + 3)
            turn()
            a = first["in_a"]
            split_to(a + 4)
            dve.wait_ge(small_in, N_SMALL)
            link(nc.vector.tensor_tensor(lam4[:, 0:3:2, :], lam4[:, 0:3:2, :], lam4[:, 1:4:2, :], ALU.mult))
            nc.vector.tensor_reduce(lamc[:, 0:2], lam4[:, 0:3:2, :], AX.X, ALU.add).then_inc(lam_v, 1)
            dve.wait_ge(gk_act, 1)
            link(nc.vector.memset(ki, 1.0))
            link(nc.vector.memset(ki[:, 0:D:CHUNK], 0.0))
            dve.wait_ge(gk_act, 4)
            link(nc.vector.scalar_tensor_tensor(out=ge, in0=ge, scalar=0.0, in1=gf, op0=ALU.min, op1=ALU.subtract))
            nc.vector.tensor_tensor_scan(gb, ki, ge, 0.0, ALU.mult, ALU.add).then_inc(gk_vec, 1)
            dve.wait_ge(gk_vec, 1)
            split_to(a + 6)

            def chunks(buf):
                return buf.rearrange("p (c n) -> p c n", n=CHUNK)

            def at(col):
                return chunks(gb)[:, :, col:col + 1].to_broadcast([GDK, GH * NCH, CHUNK])

            dve.wait_ge(gk_logit, 1)
            nc.vector.tensor_tensor(chunks(gd), chunks(gb), at(CHUNK // 2 - 1), ALU.subtract).then_inc(gk_vec, 1)
            split_to(a + 12)
            dve.wait_ge(proj_out, 4 + 1 + 1 + 4)
            dve.wait_ge(gk_act, 5)
            nc.vector.scalar_tensor_tensor(out=qi, in0=gq, scalar=GDK ** -0.5, in1=ge, op0=ALU.mult, op1=ALU.mult)\
              .then_inc(gk_vec, 1)
            dve.wait_ge(gk_act, 6)
            nc.vector.tensor_tensor(ki, gk_, gf, ALU.mult).then_inc(gk_vec, 1)
            nc.vector.tensor_tensor(chunks(gd), at(CHUNK - 1), chunks(gb), ALU.subtract).then_inc(gk_vec, 1)
            dve.wait_ge(gk_act, 7)
            nc.vector.scalar_tensor_tensor(out=gq, in0=gq, scalar=GDK ** -0.5, in1=ge, op0=ALU.mult, op1=ALU.mult)\
              .then_inc(gk_vec, 1)
            dve.wait_ge(gk_act, 8)
            nc.vector.tensor_tensor(gk_, gk_, gf, ALU.mult).then_inc(gk_vec, 1)
            dve.wait_ge(gk_vec, 7)
            link(nc.vector.tensor_copy(small[0:GDK, 104:120], ge[:, CHUNK - 1:D:CHUNK]))
            decay = small[0:GDK, 104:120]
            for buf in sT:
                link(nc.vector.memset(buf, 0.0))
            attention(0, NU0)
            split_to(a + 12 + 2)
            dve.wait_ge(proj_out, N_IN_A)
            for t in range(TT):
                g_out = H[:, t, 0:MIX].rearrange("p (h n) -> p h n", h=GH)
                link(nc.vector.tensor_tensor(g_out, g_out, ggla.rearrange("p (o n) -> p o n", o=1)
                                             .to_broadcast([P, GH, GDV]), ALU.mult))

            def gla_scores(h):
                dve.wait_ge(gla_sc, h + 1)
                if h >= 2:
                    dve.wait_ge(gla_od, h - 1)
                for t in range(TT):
                    for c in range(2):
                        r = slice(CHUNK * c, CHUNK * c + CHUNK)
                        nc.vector.copy_predicated(sT[h % 2][r, t, r], cst[r, C_GLA:C_GLA + CHUNK].bitcast(U32),
                                                  ps[r, h % 2, P * t + CHUNK * c:P * t + CHUNK * c + CHUNK])
                nc.vector.tensor_copy(kdT[h % 2], ps[:, h % 2, 256:256 + 2 * GDK].rearrange("p (t n) -> p t n", t=TT))\
                  .then_inc(gla_sce, 1)

            def gla_states(h):
                kv, st = 2 + 4 * (h % 2), state[h % 2]
                dve.wait_ge(gla_kv, h + 1)
                link(nc.vector.tensor_copy(st[:, 0, :], ps[0:GDK, kv, 0:GDV]))
                link(nc.vector.scalar_tensor_tensor(out=st[:, 1, :], in0=st[:, 0, :],
                                                    scalar=decay[:, NCH * h + 1:NCH * h + 2],
                                                    in1=ps[0:GDK, kv + 1, 0:GDV], op0=ALU.mult, op1=ALU.add))
                nc.vector.scalar_tensor_tensor(out=st[:, 2, :], in0=st[:, 1, :],
                                               scalar=decay[:, NCH * h + 2:NCH * h + 3],
                                               in1=ps[0:GDK, kv, 256:256 + GDV], op0=ALU.mult, op1=ALU.add)\
                  .then_inc(gla_st, 1)

            def gla_outputs(h):
                dve.wait_ge(gla_rms, h + 1)
                head_roots(slice(TT * h, TT * h + TT))
                for t in range(TT):
                    g = H[:, t, GDV * h:GDV * h + GDV]
                    ins = nc.vector.scalar_tensor_tensor(out=g, in0=ps[:, 4 + h % 2, 256 * t:256 * t + GDV],
                                                         scalar=hrs[:, TT * h + t:TT * h + t + 1], in1=g,
                                                         op0=ALU.mult, op1=ALU.mult)
                    if h == GH - 1:
                        ins.then_inc(h_ready, 1)
                if h < GH - 1:
                    ins.then_inc(gla_oe, 1)

            for i in range(GH + 3):
                if i < GH:
                    gla_scores(i)
                if 0 <= i - 1 < GH:
                    gla_states(i - 1)
                if 0 <= i - 3:
                    gla_outputs(i - 3)
            turn()
            split_to(first["dense"])
            residual((4, 6, 5, 7), first["dense"])
            split_to(first["dense"] + 1)
            norm(h_ready, 2)
            turn()
            d = first["dense"]
            n_ff = F_DENSE // 256
            for i in range(n_ff + 1):
                base = d + 3 * i - (1 if i > 0 else 0)
                if i < n_ff:
                    split_to(base + 2)
                if i > 0:
                    dve.wait_ge(ff_hi, i)
                    nc.vector.tensor_tensor(f_lo[:, :, :], f_h.rearrange("p (m s) -> p m s", m=2),
                                            f_hi[:, :, :].bitcast(F32), ALU.subtract).then_inc(ff_lo, 1)
                    split_to(base + (3 if i < n_ff else 1))
                if i < n_ff:
                    dve.wait_ge(ff_silu, i + 1)
                    dve.wait_ge(slot_used, base + 2)
                    if i > 0:
                        dve.wait_ge(ff_lo, i)
                    nc.vector.tensor_tensor(f_h, f_gate, ps[:, 2 + i % 2, :], ALU.mult).then_inc(ff_h, 1)
            residual((4, 5, 6, 7), first["kv"])
            norm(h_ready, 3)
            split_to(first["kv"] + 2)
            turn()
            split_to(first["kv"] + 6)
            norm(h_ready, 3, new=False)
            split_to(first["in_b"] + 1)
            turn()
            split_to(first["in_b"] + 2)

            ropes = [0]

            def rope(src, t, evacuated):
                dve.wait_ge(proj_out, evacuated)
                v = src[:, t, :].rearrange("p (h c d) -> p h c d", h=2 * DH, c=2)
                o = rot[:, t, :].rearrange("p (h c d) -> p h c d", h=2 * DH, c=2)
                cs, sn = (cos_sin[:, t, i:i + 1, :].to_broadcast([P, 2 * DH, HEAD_DIM // 2]) for i in range(2))
                tmp = [rope_t[:, i, :].rearrange("p (h d) -> p h d", h=2 * DH) for i in range(4)]
                if ropes[0] > 0:
                    dve.wait_ge(roped, ropes[0])
                for i, (a_, b_) in enumerate(((v[:, :, 0, :], cs), (v[:, :, 1, :], sn), (v[:, :, 0, :], sn),
                                              (v[:, :, 1, :], cs))):
                    ins = nc.vector.tensor_tensor(tmp[i], a_, b_, ALU.mult)
                link(ins)
                if ropes[0] >= 2:
                    dve.wait_ge(rope_turned, ropes[0] - 1)
                nc.vector.tensor_tensor(o[:, :, 0, :], tmp[0], tmp[1], ALU.subtract)
                nc.vector.tensor_tensor(o[:, :, 1, :], tmp[2], tmp[3], ALU.add).then_inc(roped, 1)
                ropes[0] += 1

            kv_out = 4 + 12 + 0 + 2 + 4 + 2
            rope(k_raw, 0, kv_out)
            split_to(first["in_b"] + 3)
            rope(k_raw, 1, kv_out)
            split_to(first["in_b"] + 4)
            rope(q_raw, 0, kv_out + 6)
            rope(q_raw, 1, kv_out + 6)
            dve.wait_ge(roped, 4)
            dve.wait_ge(lam_a, 1)
            link(nc.vector.tensor_tensor(lamc[:, 4:5], lamc[:, 3:4], lamc[:, 2:3], ALU.subtract))
            link(nc.vector.tensor_scalar(lamc[:, 5:6], lamc[:, 4:5], -LAMBDA_INIT, None, ALU.add))
            link(nc.vector.tensor_scalar(gsub[:, :], gsub[:, :], 1.0 - LAMBDA_INIT, None, ALU.mult))
            attention(NU0, len(units))
            split_to(first["out_b"] + 2)
            dve.wait_ge(diff_rms, 1)
            head_roots(slice(0, TT * DH))
            for t in range(TT):
                for h in range(DH):
                    ins = nc.vector.scalar_tensor_tensor(out=H[:, t, DV * h:DV * h + DV],
                                                         in0=diff_o[:, t, DV * h:DV * h + DV],
                                                         scalar=hrs[:, DH * t + h:DH * t + h + 1],
                                                         in1=gsub[:, :], op0=ALU.mult, op1=ALU.mult)
                ins.then_inc(h_ready, 1)
            turn()
            split_to(NPRE - 1)
            residual((4, 6, 5, 7), NPRE - 1)
            norm(h_ready, 4)
            turn()
            split_to(NPRE)

            link(nc.vector.memset(route_gate[:, :, :], 0.0))
            link(nc.vector.memset(route_rank[:, :, :], -1.0))
            link(nc.vector.memset(flag[:, :], 0))
            dve.wait_ge(slot_used, NPRE)
            nc.vector.tensor_copy(logT, ps[0:NE, 4, 0:S]).then_inc(logits_out, 1)
            lg = rt[:, 8:24].rearrange("p (t e) -> p t e", t=TT)
            dve.wait_ge(logits_turned, 1)
            link(nc.vector.tensor_copy(lg, ps[:, 5, 0:TT * NE].rearrange("p (t e) -> p t e", t=TT)))
            for t in range(TT):
                ins = nc.vector.max(top8[:, t, :], lg[:, t, :])
            link(ins)
            for t in range(TT):
                ins = nc.vector.max_index(idx8[:, t, :], top8[:, t, :], lg[:, t, :])
            nc.vector.tensor_tensor(rt[:, 0:2], top8[:, :, 1], top8[:, :, 0], ALU.subtract).then_inc(top_d, 1)
            dve.wait_ge(top_d, 1)
            link(nc.vector.tensor_copy(fidx, idx8[:, :, :]))

            def per_token(column):
                return column.rearrange("p (t o) -> p t o", o=1).to_broadcast([P, TT, NE])

            iota8 = cst[:, C_IOTA:C_IOTA + NE].rearrange("p (o e) -> p o e", o=1).to_broadcast([P, TT, NE])
            nc.vector.tensor_tensor(sel1, iota8, fidx[:, :, 0:1].to_broadcast([P, TT, NE]), ALU.is_equal)
            link(nc.vector.tensor_tensor(sel2, iota8, fidx[:, :, 1:2].to_broadcast([P, TT, NE]), ALU.is_equal))
            nc.vector.tensor_tensor(msk, sel1, sel2, ALU.add).then_inc(chosen, 1)
            dve.wait_ge(top_e, 1)
            link(nc.vector.tensor_scalar(rt[:, 4:6], rt[:, 2:4], 1.0, None, ALU.add))
            link(nc.vector.reciprocal(rt[:, 4:6], rt[:, 4:6]))
            link(nc.vector.tensor_tensor(rt[:, 6:8], rt[:, 2:4], rt[:, 4:6], ALU.mult))
            nc.vector.tensor_tensor(sel1, sel1, per_token(rt[:, 4:6]), ALU.mult)
            link(nc.vector.tensor_tensor(sel2, sel2, per_token(rt[:, 6:8]), ALU.mult))
            link(nc.vector.tensor_tensor(route_gate[:, :, 1:NE + 1], sel1, sel2, ALU.add))
            dve.wait_ge(ranks, 1)
            cnt = ps[:, 6, 0:TT * NE].rearrange("p (t e) -> p t e", t=TT)
            link(nc.vector.scalar_tensor_tensor(out=msk, in0=cnt, scalar=1.0, in1=msk, op0=ALU.add, op1=ALU.mult))
            link(nc.vector.tensor_scalar(route_rank[:, :, 0:NE], msk, -1.0, None, ALU.add))

            def one_hot(sweep):
                for t in range(TT):
                    nc.vector.tensor_scalar(oh[:, t, :], cst[:, C_IOTA + P * sweep:C_IOTA + P * sweep + P],
                                            cur_rank[:, t:t + 1], None, ALU.is_equal).then_inc(oh_ready, 1)

            def gathered(sweep, e):
                for half in range(2):
                    dve.wait_ge(xg_h, sweep * 2 * NE + 2 * e + half + 1)
                    nc.vector.tensor_tensor(xg_lo[:, 4 * half:4 * half + 4, :],
                                            ps[:, 1 + 2 * half, :].rearrange("p (k n) -> p k n", k=4),
                                            xg_hi[:, 4 * half:4 * half + 4, :].bitcast(F32), ALU.subtract)\
                      .then_inc(xg_l, 1)

            def experts(sweep):
                done = sweep * NE
                cd = sweep * (2 * NE + 2)
                if sweep == 0:
                    nc.vector.memset(ohT[:, :], 0.0)
                nc.vector.tensor_copy(cur_rank.rearrange("p (t o) -> p t o", o=1), route_rank[:, :, 0:1])\
                  .then_inc(cur_done, 1)
                dve.wait_ge(cur_done, cd + 1)
                one_hot(sweep)
                if sweep == 0:
                    link(nc.vector.tensor_reduce(rt[:, 24:25], ps[:, 6, 2 * NE:3 * NE], AX.X, ALU.max))
                    nc.vector.tensor_copy(flag[0:1, 0:1], rt[0:1, 24:25]).then_inc(routed, 1)
                base = NPRE + done * PER_EXPERT

                def add_expert(i):
                    for n in range(4):
                        dve.wait_ge(e_comb, (i + sweep * (NE + 1)) * 4 + n + 1)
                        xs = xres[:, n // 2, 512 * (n % 2):512 * (n % 2) + 512]
                        nc.vector.scalar_tensor_tensor(out=xs, in0=ps[:, (1, 3, 4, 7)[n], :],
                                                       scalar=cur_gate[:, n // 2:n // 2 + 1], in1=xs,
                                                       op0=ALU.mult, op1=ALU.add).then_inc(e_add, 1)

                with dve.Fori(0, NE) as e:
                    u = [0]

                    def split_next(n):
                        for _ in range(n):
                            s = base + u[0]
                            dve.wait_ge(hi_ready, e * PER_EXPERT + s + 1)
                            r = (s - NPRE) % E_SPLIT
                            nc.vector.tensor_tensor(e_wlo[:, r, :], raw[:, s % RAW, :],
                                                    e_whi[:, r, :].bitcast(F32), ALU.subtract).then_inc(lo_ready, 1)
                            u[0] += 1

                    def hidden(j):
                        dve.wait_ge(e_hi, (e + done) * STEPS + j + 1)
                        nc.vector.tensor_tensor(h_lo, ps[:, 4, :].rearrange("p (m n) -> p m n", m=4),
                                                h_hi.bitcast(F32), ALU.subtract).then_inc(e_lo, 1)

                    split_next(2)
                    gathered(sweep, e)
                    for j in range(STEPS):
                        split_next(2)
                        if j == 0:
                            nc.vector.tensor_copy(cur_gate.rearrange("p (t o) -> p t o", o=1),
                                                  route_gate[:, :, bass.ds(e, 1)]).then_inc(cur_done, 1)
                        if j == 3:
                            nc.vector.tensor_copy(cur_rank.rearrange("p (t o) -> p t o", o=1),
                                                  route_rank[:, :, bass.ds(e + 1, 1)]).then_inc(cur_done, 1)
                            dve.wait_ge(cur_done, 2 * e + cd + 3)
                            one_hot(sweep)
                        if j > 0:
                            split_next(2)
                            hidden(j - 1)
                        split_next(2)
                        if j == 0:
                            dve.wait_ge(cur_done, 2 * e + cd + 2)
                            add_expert(e)
                        dve.wait_ge(e_silu, (e + done) * STEPS + j + 1)
                        dve.wait_ge(slot_used, e * PER_EXPERT + base + gate_end(j) + 2)
                        nc.vector.tensor_tensor(e_h[:, :], e_h[:, :], ps[:, 2 + j % 2, :], ALU.mult).then_inc(e_hr, 1)
                    hidden(STEPS - 1)
                nc.vector.tensor_copy(cur_gate.rearrange("p (t o) -> p t o", o=1), route_gate[:, :, NE:NE + 1])\
                  .then_inc(cur_done, 1)
                dve.wait_ge(cur_done, cd + 2 * NE + 2)
                add_expert(NE)

            experts(0)
            dve.wait_ge(routed, 1)
            over = dve.value_load(flag[0:1, 0:1], min_val=0, max_val=S)
            with dve.If(over > P):
                experts(1)
                dve.wait_ge(e_add, 2 * 4 * (NE + 1))
            dve.wait_ge(e_add, 4 * (NE + 1))
            norm(out_ready, 5)

        @block.tensor
        def _(pe):
            def three(dst, l_hi, l_lo, r_hi, r_lo, start, stop):
                nc.tensor.matmul(dst, l_hi, r_hi, start=start, stop=False)
                nc.tensor.matmul(dst, l_lo, r_hi, start=False, stop=False)
                return nc.tensor.matmul(dst, l_hi, r_lo, start=False, stop=stop)

            used = [0]

            def take():
                s = used[0]
                used[0] += 1
                kt, n = slot_shape(s)
                pe.wait_ge(lo_ready, s + 1)
                return shaped(w_hi, s % SPLIT, kt, n), shaped(w_lo, s % SPLIT, kt, n)

            turns = [0]

            def turn():
                for t in range(TT):
                    if turns[0] == 0:
                        pe.wait_ge(mem_in, 16 * TT)
                    else:
                        pe.wait_ge(h_ready, TT * (turns[0] - 1) + t + 1)
                    for half in range(2):
                        for k in range(4):
                            c = P * (4 * half + k)
                            ins = nc.tensor.transpose(ps[:, 2 * t + half, P * k:P * k + P], H[:, t, c:c + P], ident)
                        ins.then_inc(turned, 1)
                turns[0] += 1

            def await_turned(quarters):
                pe.wait_ge(turn_lo, 4 * (turns[0] - 1) + quarters)

            def token_major(banks, n_slots):
                k = 0
                await_turned(4)
                for i in range(n_slots):
                    hi, lo = take()
                    kt, n = hi.shape[1], hi.shape[2]
                    for kk in range(kt):
                        for t in range(TT):
                            ts = slice(P * t, P * t + P)
                            ins = three(banks[t][:, 0:n], act_hi[:, k, ts], act_lo[:, k, ts], hi[:, kk, :], lo[:, kk, :],
                                        k == 0, k == KT - 1)
                        k += 1
                    if i < n_slots - 1:
                        ins.then_inc(slot_used, 1)
                return ins

            def feature_major(regions, width):
                hi, lo = take()
                await_turned(4)
                for m, reg in enumerate(regions):
                    for k in range(KT):
                        c = slice(width * m, width * m + width)
                        ins = three(reg, hi[:, k, c], lo[:, k, c], act_hi[:, k, :], act_lo[:, k, :], k == 0, k == KT - 1)
                return ins

            def mark(ins):
                ins.then_inc(slot_used, 1)

            def halves(b):
                return [ps[:, b, 0:256], ps[:, b, 256:512]]

            pe.wait_ge(const_in, 16)
            turn()
            for l in range(2):
                mark(feature_major(halves(4 + 2 * l), P))
                hi, lo = take()
                for t in range(TT):
                    for k in range(KT):
                        ts = slice(P * t, P * t + P)
                        ins = three(halves(5 + 2 * l)[t], act_hi[:, k, ts], act_lo[:, k, ts], hi[:, k, :], lo[:, k, :],
                                    k == 0, k == KT - 1)
                mark(ins)
            turn()
            pe.wait_ge(proj_out, 4)
            mark(feature_major([ps[0:RANK, 4, 0:S]], RANK))
            mark(feature_major(halves(5), P))
            pe.wait_ge(proj_out, 5)
            pe.wait_ge(small_in, N_SMALL)
            for h in range(GH):
                ins = nc.tensor.matmul(ps[0:GDK, 6 + h // 2, S * (h % 2):S * (h % 2) + S],
                                       wgk[:, GDK * h:GDK * h + GDK], gd[0:RANK, 0:S], start=True, stop=True)
            ins.then_inc(gk_logit, 1)
            for i in range(4):
                mark(feature_major([ps[0:GDK, i, 0:S], ps[0:GDK, i, S:2 * S]], GDK))

            def two_blocks(b512, b256):
                mark(token_major([ps[:, b512[0], :], ps[:, b512[1], :]], 2))
                hi, lo = take()
                for t in range(TT):
                    for k in range(KT):
                        ts = slice(P * t, P * t + P)
                        ins = three(halves(b256)[t], act_hi[:, k, ts], act_lo[:, k, ts], hi[:, k, :], lo[:, k, :],
                                    k == 0, k == KT - 1)
                mark(ins)

            pe.wait_ge(proj_out, 6)
            pe.wait_ge(gk_act, 1)
            two_blocks((4, 5), 6)
            pe.wait_ge(proj_out, 6 + 2)
            two_blocks((7, 0), 1)

            def unit_scores(u):
                kind, l, h, t = units[u]
                if u >= 2:
                    pe.wait_ge(u_exp, u - 1)
                scores = unit_scores_bank(u)
                q, k = (qmT, kmT[:, l, :, :]) if kind == "mem" else (qT, kT)
                for i in range(2):
                    r = slice(HEAD_DIM * i, HEAD_DIM * i + HEAD_DIM)
                    ins = nc.tensor.matmul(scores[:, i, :], q[r, h, P * t:P * t + P], k[r, h, 0:unit_keys(u)],
                                           start=True, stop=True)
                ins.then_inc(u_score, 1)

            def unit_turn(u):
                pe.wait_ge(u_prob, u + 1)
                if u >= 2:
                    pe.wait_ge(u_pT, u - 1)
                for k in range((2 * S if units[u][0] == "mem" else unit_keys(u)) // P):
                    ins = nc.tensor.transpose(ps[:, U_BANK["turn"][u % 2], P * k:P * k + P],
                                              sc[:, u % 3, P * k:P * k + P], ident)
                ins.then_inc(u_turned, 1)

            def unit_values(u):
                kind, l, h, _ = units[u]
                nk = unit_keys(u)
                pe.wait_ge(u_pT, u + 1)
                if u >= 2:
                    pe.wait_ge(u_out, u - 1)
                if kind == "mem":
                    parts = [(vm[:, l], HEAD_DIM * (2 * h + i), HEAD_DIM, HEAD_DIM * i, S * i) for i in range(2)]
                else:
                    parts = [(v_tok, DV * h, DV, 0, 0)]
                for v, f, w, to, p0 in parts:
                    for k in range(nk // P):
                        ins = nc.tensor.matmul(ps[:, U_BANK["val"][u % 2], to:to + w],
                                               pT[:, u % 2, p0 + P * k:p0 + P * k + P], v[:, k, f:f + w],
                                               start=(k == 0), stop=(k == nk // P - 1))
                ins.then_inc(u_val, 1)

            def attention(u0, u1):
                for i in range(u0, u1 + 3):
                    if i < u1:
                        unit_scores(i)
                    if u0 <= i - 2 < u1:
                        unit_turn(i - 2)
                    if u0 <= i - 3:
                        unit_values(i - 3)

            pe.wait_ge(proj_out, N_IN_A)
            attention(0, NU0)
            pe.wait_ge(gk_vec, 7)
            pe.wait_ge(u_out, NU0)

            def gla_scores(h):
                hd = slice(S * h, S * h + S)
                if h >= 2:
                    pe.wait_ge(gla_sce, h - 1)
                for n in range(NCH):
                    t, c = n // 2, n % 2
                    cs = slice(CHUNK * n, CHUNK * n + CHUNK)
                    nc.tensor.matmul(ps[CHUNK * c:CHUNK * c + CHUNK, h % 2, P * t + CHUNK * c:P * t + CHUNK * c + CHUNK],
                                     ki[:, hd][:, cs], qi[:, hd][:, cs], start=True, stop=True, skip_group_check=True)
                for t in range(TT):
                    ins = nc.tensor.transpose(ps[:, h % 2, 256 + GDK * t:256 + GDK * t + GDK],
                                              gk_[:, hd][:, P * t:P * t + P], ident[0:GDK, 0:GDK])
                ins.then_inc(gla_sc, 1)

            def gla_chunk_kv(h):
                pe.wait_ge(gla_sce, h + 1)
                if h >= 2:
                    pe.wait_ge(gla_st, h - 1)
                for n in range(NCH - 1):
                    t, r = n // 2, slice(CHUNK * (n % 2), CHUNK * (n % 2) + CHUNK)
                    ins = nc.tensor.matmul(ps[0:GDK, 2 + 4 * (h % 2) + n % 2, 256 * (n // 2):256 * (n // 2) + GDV],
                                           kdT[h % 2][r, t, :], v_tok[r, t, GDV * h:GDV * h + GDV],
                                           start=True, stop=True)
                ins.then_inc(gla_kv, 1)

            def gla_outputs(h):
                pe.wait_ge(gla_st, h + 1)
                if h >= 2:
                    pe.wait_ge(gla_oe, h - 1)
                for t in range(TT):
                    o = ps[:, 4 + h % 2, 256 * t:256 * t + GDV]
                    nc.tensor.matmul(o, sT[h % 2][:, t, :], v_tok[:, t, GDV * h:GDV * h + GDV], start=True,
                                     stop=False, skip_group_check=True)
                    for c in range(2):
                        n = 2 * t + c
                        if n == 0:
                            continue
                        q_st = gq[:, S * h + CHUNK * n:S * h + CHUNK * n + CHUNK]
                        ins = nc.tensor.matmul(o[CHUNK * c:CHUNK * c + CHUNK, :], q_st, state[h % 2][:, n - 1, :],
                                               start=False, stop=True, skip_group_check=True)
                ins.then_inc(gla_od, 1)

            for i in range(GH + 2):
                if i < GH:
                    gla_scores(i)
                if 0 <= i - 1 < GH:
                    gla_chunk_kv(i - 1)
                if 0 <= i - 2:
                    gla_outputs(i - 2)
            turn()

            def out_projection():
                token_major([ps[:, 4, :], ps[:, 5, :]], 2).then_inc(slot_used, 1)
                mark(token_major([ps[:, 6, :], ps[:, 7, :]], 2))

            out_projection()
            turn()
            pe.wait_ge(add_done, 4)
            n_ff = F_DENSE // 256
            for i in range(n_ff + 1):
                if i < n_ff:
                    if i >= 2:
                        pe.wait_ge(ff_silu, i - 1)
                        pe.wait_ge(ff_h, i - 1)
                    for j in range(2):
                        mark(feature_major(halves(2 * j + i % 2), P))
                if i > 0:
                    pe.wait_ge(ff_lo, i)
                    hi, lo = take()
                    for m in range(2):
                        for t in range(TT):
                            ts = slice(P * t, P * t + P)
                            for n in range(2):
                                ns = slice(512 * n, 512 * n + 512)
                                ins = three(ps[:, 4 + 2 * t + n, :], f_hi[:, m, ts], f_lo[:, m, ts],
                                            hi[:, m, ns], lo[:, m, ns], i == 1 and m == 0, i == n_ff and m == 1)
                    mark(ins)
            turn()
            pe.wait_ge(add_done, 8)
            mark(token_major([ps[:, 4, :], ps[:, 5, :]], 2))
            mark(token_major([ps[:, 6, :], ps[:, 7, :]], 2))
            mark(token_major([ps[:, 0, :], ps[:, 1, :]], 2))
            pe.wait_ge(proj_out, 16 + 8)
            turn()
            mark(token_major([ps[:, 4, :], ps[:, 5, :]], 2))
            mark(token_major([ps[:, 6, :], ps[:, 7, :]], 2))
            for r in range(4):
                t = r % 2
                pe.wait_ge(roped, r + 1)
                if r >= 2:
                    pe.wait_ge(rope_out, r - 1)
                for m in range(DH):
                    ins = nc.tensor.transpose(ps[:, 2 * t + m // 4, P * (m % 4):P * (m % 4) + P],
                                              rot[:, t, P * m:P * m + P], ident)
                if r >= 2:
                    for m in range(2):
                        ins = nc.tensor.transpose(ps[:, 2 * t + 1, 256 + P * m:256 + P * m + P],
                                                  qm_tok[:, t, P * m:P * m + P], ident)
                ins.then_inc(rope_turned, 1)
            pe.wait_ge(rope_out, 4)
            attention(NU0, len(units))
            turn()
            pe.wait_ge(u_out, len(units))
            out_projection()
            turn()
            pe.wait_ge(add_done, 12)
            mark(feature_major([ps[0:NE, 4, 0:S]], NE))
            pe.wait_ge(logits_out, 1)
            for t in range(TT):
                ins = nc.tensor.transpose(ps[:, 5, NE * t:NE * t + NE], logT[:, P * t:P * t + P], ident[0:NE, 0:NE])
            ins.then_inc(logits_turned, 1)
            strict = cst[:, C_STRICT:C_STRICT + P]
            pe.wait_ge(chosen, 1)
            nc.tensor.matmul(ps[:, 6, 0:NE], strict, msk[:, 0, :], start=True, stop=True)
            nc.tensor.matmul(ps[:, 6, NE:2 * NE], strict, msk[:, 1, :], start=True, stop=False)
            nc.tensor.matmul(ps[:, 6, NE:2 * NE], ones[:, :], msk[:, 0, :], start=False, stop=True)
            nc.tensor.matmul(ps[:, 6, 2 * NE:3 * NE], ones[:, :], msk[:, 0, :], start=True, stop=False)
            nc.tensor.matmul(ps[:, 6, 2 * NE:3 * NE], ones[:, :], msk[:, 1, :], start=False, stop=True)\
              .then_inc(ranks, 1)

            def gather():
                for half in range(2):
                    for k in range(4):
                        c = P * (4 * half + k)
                        for t in range(TT):
                            ins = nc.tensor.matmul(ps[:, 1 + 2 * half, P * k:P * k + P], H[:, t, c:c + P], oh[:, t, :],
                                                   start=(t == 0), stop=(t == TT - 1))
                    ins.then_inc(disp, 1)

            def experts(sweep):
                done = sweep * NE
                base = NPRE + done * PER_EXPERT
                n_oh = sweep * 2 * (NE + 1)
                pe.wait_ge(oh_ready, n_oh + 2)
                if sweep:
                    pe.wait_ge(e_add, 4 * (NE + 1))
                gather()
                if sweep == 0:
                    pe.wait_ge(routed, 1)

                def scatter(i):
                    n_y = (i + sweep * (NE + 1)) * 2
                    for t in range(TT):
                        for n in range(2):
                            pe.wait_ge(e_yo, n_y + (2 if n + t else 1))
                            nc.tensor.matmul(ps[:, (1, 3, 4, 7)[2 * t + n], :], ohT[:, P * t:P * t + P],
                                             y_e[:, 512 * n:512 * n + 512], start=True, stop=True).then_inc(e_comb, 1)

                with pe.Fori(0, NE) as e:
                    u = [0]
                    pe.wait_ge(xg_l, 2 * (e + done) + 2)

                    def expert_slot(kt, n):
                        s = base + u[0]
                        u[0] += 1
                        pe.wait_ge(lo_ready, e * PER_EXPERT + s + 1)
                        r = (s - NPRE) % E_SPLIT
                        return shaped(e_whi, r, kt, n), shaped(e_wlo, r, kt, n)

                    def product(bank):
                        for half in range(2):
                            hi, lo = expert_slot(4, 512)
                            for kk in range(4):
                                k = 4 * half + kk
                                ins = three(bank, xg_hi[:, k, :], xg_lo[:, k, :], hi[:, kk, :], lo[:, kk, :],
                                            k == 0, k == KT - 1)
                            ins.then_inc(slot_used, 1)

                    def turn_hidden(j):
                        pe.wait_ge(e_hr, (e + done) * STEPS + j + 1)
                        for m in range(4):
                            ins = nc.tensor.transpose(ps[:, 4, P * m:P * m + P], e_h[:, P * m:P * m + P], ident)
                        ins.then_inc(e_tr, 1)

                    def down(j):
                        pe.wait_ge(e_lo, (e + done) * STEPS + j + 1)
                        for half in range(2):
                            hi, lo = expert_slot(2, D)
                            for m in range(2):
                                f = 2 * half + m
                                for n in range(2):
                                    ns = slice(512 * n, 512 * n + 512)
                                    ins = three(ps[:, 5 + n, :], h_hi[:, f, :], h_lo[:, f, :], hi[:, m, ns],
                                                lo[:, m, ns], j == 0 and f == 0, j == STEPS - 1 and f == 3)
                            ins.then_inc(slot_used, 1)

                    for j in range(STEPS):
                        if j == 1:
                            pe.wait_ge(e_add, (e + sweep * (NE + 1)) * 4 + 4)
                        product(ps[:, j % 2, :])
                        if j > 0:
                            turn_hidden(j - 1)
                        if j == 1:
                            for t in range(TT):
                                ins = nc.tensor.transpose(ps[:, 7, P * t:P * t + P], oh[:, t, :], ident)
                            ins.then_inc(oh_turned, 1)
                        product(ps[:, 2 + j % 2, :])
                        if j == 0:
                            scatter(e)
                        if j > 0:
                            down(j - 1)
                    pe.wait_ge(oh_ready, 2 * e + n_oh + 4)
                    gather()
                    turn_hidden(STEPS - 1)
                    down(STEPS - 1)
                scatter(NE)

            experts(0)
            over = pe.value_load(flag[0:1, 0:1], min_val=0, max_val=S)
            with pe.If(over > P):
                experts(1)


_INS = ["x", "mem", "g_mix", "g_ffn", "w_mem_kv", "w_out", "w_in_a", "w_gk_up", "b_gk", "g_gla", "g_kv", "w_kv",
        "w_in_b", "lambda_q1", "lambda_k1", "lambda_q2", "lambda_k2", "g_subln", "w_dense_gate", "w_dense_up",
        "w_dense_down", "w_router", "w_exp_gate", "w_exp_up", "w_exp_down", "g_final"]


def constants(np):
    p = np.arange(P)
    c = np.zeros((P, C_N), np.float32)
    c[:, C_ID:C_ID + P] = np.eye(P)
    c[:, C_IOTA:C_IOTA + S] = np.arange(S)
    c[:, C_STRICT:C_STRICT + P] = p[:, None] < p[None, :]
    c[:, C_CAUSAL:C_CAUSAL + P] = np.where(p[None, :] <= p[:, None], 0.0, NEG)
    c[:, C_GLA:C_GLA + CHUNK] = (p[:, None] % CHUNK) <= np.arange(CHUNK)[None, :]
    half = HEAD_DIM // 2
    inv = (np.float32(10000.0) ** (-np.arange(half, dtype=np.float32) / np.float32(half))).astype(np.float32)
    ang = np.arange(S, dtype=np.float32)[:, None] * inv[None, :]
    for t in range(TT):
        a = ang[P * t:P * t + P].astype(np.float64)
        c[:, C_ROPE + 64 * t:C_ROPE + 64 * t + 32] = np.cos(a)
        c[:, C_ROPE + 64 * t + 32:C_ROPE + 64 * t + 64] = np.sin(a)
    c[:, C_EPS] = EPS
    return c


def kernel(**inputs):
    import numpy as _np
    import concourse.bacc as _bacc
    from concourse import mybir as _mybir
    from concourse.bass_utils import run_bass_kernel_spmd as _run

    nc = _bacc.Bacc("TRN2", target_bir_lowering=False, num_devices=1)
    arrays, args = {}, []
    for name in _INS:
        a = _np.ascontiguousarray(inputs[name])
        arrays[f"in_{name}_dram"] = a
        args.append(nc.dram_tensor(f"in_{name}_dram", a.shape, _mybir.dt.from_np(a.dtype), kind="ExternalInput").ap())
    c = constants(_np)
    arrays["in_consts_dram"] = c
    args.append(nc.dram_tensor("in_consts_dram", c.shape, F32, kind="ExternalInput").ap())
    args.append(nc.dram_tensor("out_0_dram", (1, S, D), F32, kind="ExternalOutput").ap())
    trunk(nc, *args)
    r = _run(nc, [arrays], core_ids=[0])
    return r.results[0]["out_0_dram"]
```

```python
import math
from contextlib import ExitStack

import concourse.bass as bass
from concourse import mybir

F32 = mybir.dt.float32
F32R = mybir.dt.float32r
U32 = mybir.dt.uint32
I32 = mybir.dt.int32
ALU = mybir.AluOpType
ACT = mybir.ActivationFunctionType
AX = mybir.AxisListType

P = 128
D = 1024
S = 256
KT = D // P
TT = S // P
MEM_HEADS, HEAD_DIM = 4, 64
MEM_DIM = MEM_HEADS * HEAD_DIM
MIX = D - MEM_DIM
GH, GDV, GDK, RANK, CHUNK = 4, 192, 96, 16, 64
NCH = S // CHUNK
DH, DV = 6, 128
F_DENSE, F_EXP, NE = 2816, 3584, 8
EPS = 1e-6
LAMBDA_INIT = 0.8 - 0.6 * math.exp(-0.3)
NEG = -3.0e38

SLOT = 2048
RAW = 7
SPLIT = 3
E_SPLIT = 6

C_ID, C_IOTA, C_STRICT, C_CAUSAL, C_GLA, C_ROPE, C_EPS = 0, 128, 384, 512, 640, 704, 832
C_N = 833


def prefill_slots(w):
    slots, first = [], {}

    def add(stage, src, k0, kt, n0, n):
        first.setdefault(stage, len(slots))
        slots.append((src, k0, kt, n0, n))

    for l in range(2):
        add("mem_kv", w["w_mem_kv"][l], 0, 8, 0, 256)
        add("mem_kv", w["w_mem_kv"][l], 0, 8, 256, 256)
    add("in_a", w["w_in_a"][0], 0, 8, 2 * GH * GDK + 2 * MIX, RANK)
    add("in_a", w["w_in_a"][0], 0, 8, W_QMEM, MEM_DIM)
    for i in range(4):
        add("in_a", w["w_in_a"][0], 0, 8, 192 * i, 192)
    for base in (768, 1536):
        add("in_a", w["w_in_a"][0], 0, 4, base, 512)
        add("in_a", w["w_in_a"][0], 4, 4, base, 512)
        add("in_a", w["w_in_a"][0], 0, 8, base + 512, 256)

    def blocks(stage, src, nb):
        for b in range(nb):
            add(stage, src, 0, 4, 512 * b, 512)
            add(stage, src, 4, 4, 512 * b, 512)

    blocks("out_a", w["w_out"][0], 2)
    n = F_DENSE // 256
    for i in range(n + 1):
        if i < n:
            add("dense", w["w_dense_gate"][0], 0, 8, 256 * i, 256)
            add("dense", w["w_dense_up"][0], 0, 8, 256 * i, 256)
        if i > 0:
            add("dense", w["w_dense_down"][0], 2 * (i - 1), 2, 0, D)
    blocks("kv", w["w_kv"], 3)
    blocks("in_b", w["w_in_b"][0], 2)
    blocks("out_b", w["w_out"][1], 2)
    add("router", w["w_router"][0], 0, 8, 0, NE)
    first["experts"] = len(slots)
    return slots, first


W_QMEM = 2 * GH * GDK + 2 * MIX + RANK
STEPS = F_EXP // 512
PER_EXPERT = 6 * STEPS


def trunk(nc, x, mem, g_mix, g_ffn, w_mem_kv, w_out, w_in_a, w_gk_up, b_gk, g_gla, g_kv, w_kv, w_in_b,
          lambda_q1, lambda_k1, lambda_q2, lambda_k2, g_subln, w_dense_gate, w_dense_up, w_dense_down,
          w_router, w_exp_gate, w_exp_up, w_exp_down, g_final, consts, out):
    W = dict(w_mem_kv=w_mem_kv, w_out=w_out, w_in_a=w_in_a, w_kv=w_kv, w_in_b=w_in_b,
             w_dense_gate=w_dense_gate, w_dense_up=w_dense_up, w_dense_down=w_dense_down, w_router=w_router)
    slots, first = prefill_slots(W)
    NPRE = first["experts"]

    with ExitStack() as ctx:
        def sb(name, shape, dt=F32):
            return ctx.enter_context(nc.sbuf_tensor(name, shape, dt))

        def sem(name):
            return ctx.enter_context(nc.semaphore(name))

        raw = sb("raw", [P, RAW, SLOT])
        act_hi = sb("act_hi", [P, KT, S], F32R)
        act_lo = sb("act_lo", [P, KT, S], F32R)
        xres = sb("xres", [P, TT, D])
        H = sb("H", [P, TT, D])
        gain = sb("gain", [P, D])
        cst = sb("cst", [P, C_N])
        ones = sb("ones", [P, P])
        small = sb("small", [P, 136])
        rsc = sb("rsc", [P, 5, TT, NE])
        bgk = sb("bgk", [GDK, GH])
        idx8 = sb("idx8", [P, TT, 8], U32)
        route_gate = sb("route_gate", [P, TT, NE + 1])
        route_rank = sb("route_rank", [P, TT, NE])
        flag = sb("flag", [1, 8], I32)
        SCATTER_BANKS = (3, 7, 0, 7)

        ps = ctx.enter_context(nc.psum_tensor("ps", [P, 8, 512], F32))

        with ExitStack() as prefill:
            def sbp(name, shape, dt=F32):
                return prefill.enter_context(nc.sbuf_tensor(name, shape, dt))

            w_hi = sbp("w_hi", [P, SPLIT, SLOT], F32R)
            w_lo = sbp("w_lo", [P, SPLIT, SLOT], F32R)
            T = sbp("T", [P, 8, D])
            v_tok = sbp("v_tok", [P, TT, MIX])
            kmT = sbp("kmT", [P, 2, 2, S])
            vm = sbp("vm", [P, 2, TT, MEM_DIM])
            qmT = sbp("qmT", [P, 2, S])
            ggla = sbp("ggla", [P, GDV])
            gsub = sbp("gsub", [P, DV])
            with nc.sbuf_tensor("sc", [P, 3, 512], F32) as sc, nc.sbuf_tensor("pT", [P, 2, 512], F32) as pT:
                pass
            f_hi = sbp("f_hi", [P, 2, 2, S], F32R)
            f_lo = sbp("f_lo", [P, 2, 2, S], F32R)

        e_whi = sb("e_whi", [P, E_SPLIT, SLOT], F32R)
        e_wlo = sb("e_wlo", [P, E_SPLIT, SLOT], F32R)
        oh = sb("oh", [P, TT, P])
        ohT = sb("ohT", [P, S])
        e_h = sb("e_h", [P, 512])
        y_e = sb("y_e", [P, D])
        xg_hi, xg_lo = act_hi[:, :, 0:P], act_lo[:, :, 0:P]
        h_hi, h_lo = act_hi[:, 0:4, P:S], act_lo[:, 0:4, P:S]

        ident = cst[:, C_ID:C_ID + P]
        cos_sin = cst[:, C_ROPE:C_ROPE + 128].rearrange("p (t c d) -> p t c d", t=TT, c=2)
        eps = cst[:, C_EPS:C_EPS + 1]
        ss, rms, rs = small[:, 0:2], small[:, 2:4], small[:, 4:6]
        nmax, nbias, rsum = small[:, 8:14], small[:, 14:20], small[:, 20:26]
        rinv = small[:, 128:136]
        lamc = small[:, 32:40]
        hss, hrms, hrs = small[:, 40:52], small[:, 52:64], small[:, 64:76]
        blend = small[:, 120:123]
        cur_rank, cur_gate = small[:, 76:78], small[:, 78:80]
        rt = small[:, 80:120]

        gq, gk_, gb, gd = (T[0:GDK, i, :] for i in range(4))
        ge, gf, qi, ki = (T[0:GDK, i, :] for i in range(4, 8))
        state = [T[0:GDK, i, 0:3 * GDV].rearrange("p (n v) -> p n v", n=3) for i in (2, 5)]
        kdT = [T[:, i, 576:768].rearrange("p (t n) -> p t n", t=TT) for i in (2, 5)]
        sT = [T[:, i, 768:1024].rearrange("p (t n) -> p t n", t=TT) for i in (2, 5)]
        gla_sq = T[:, 3, 0:TT * GDV].rearrange("p (t n) -> p t n", t=TT)
        lam4 = sc[:, 0, 0:4 * HEAD_DIM].rearrange("p (i n) -> p i n", i=4)
        wgk = sc[0:RANK, 1, 0:GH * GDK]
        f_gate, f_h = T[:, 0, 0:512], T[:, 1, 0:512]
        flatT = T[:, :, :].rearrange("p a b -> p (a b)")
        k_raw = flatT[:, 0:1536].rearrange("p (t n) -> p t n", t=TT)
        q_raw = flatT[:, 1536:3072].rearrange("p (t n) -> p t n", t=TT)
        rot = flatT[:, 3072:4608].rearrange("p (t n) -> p t n", t=TT)
        kT = flatT[:, 4608:6144].rearrange("p (h s) -> p h s", h=DH)
        qT = flatT[:, 6144:7680].rearrange("p (h s) -> p h s", h=DH)
        qm_tok = flatT[:, 7680:8192].rearrange("p (t n) -> p t n", t=TT)
        rope_t = sc[:, :, :].rearrange("p a b -> p (a b)")[:, 0:1536].rearrange("p (a n) -> p a n", a=4)
        diff_o = flatT[:, 0:1536].rearrange("p (t n) -> p t n", t=TT)
        diff_sq = flatT[:, 1536:3072].rearrange("p (t n) -> p t n", t=TT)
        top8, fidx, msk, sel1, sel2 = (rsc[:, i, :, :] for i in range(5))
        logT = sc[0:NE, 2, 0:S]

        const_in = sem("const_in")
        small_in = sem("small_in")
        mem_in = sem("mem_in")
        x_in = sem("x_in")
        gain_in = sem("gain_in")
        raw_in = [sem(f"raw_in{r}") for r in range(RAW)]
        hi_ready = sem("hi_ready")
        lo_ready = sem("lo_ready")
        slot_used = sem("slot_used")
        h_ready = sem("h_ready")
        turned = sem("turned")
        turn_hi = sem("turn_hi")
        turn_lo = sem("turn_lo")
        rms_ready = sem("rms_ready")
        proj_out = sem("proj_out")
        tile0_done = sem("tile0_done")
        add_done = sem("add_done")
        gk_logit = sem("gk_logit")
        gk_act = sem("gk_act")
        gk_vec = sem("gk_vec")
        gla_sc = sem("gla_sc")
        gla_sce = sem("gla_sce")
        gla_kv = sem("gla_kv")
        gla_st = sem("gla_st")
        gla_od = sem("gla_od")
        gla_oe = sem("gla_oe")
        gla_rms = sem("gla_rms")
        diff_sqs = sem("diff_sqs")
        diff_rms = sem("diff_rms")
        roped = sem("roped")
        rope_turned = sem("rope_turned")
        rope_out = sem("rope_out")
        u_score = sem("u_score")
        u_max = sem("u_max")
        u_exp = sem("u_exp")
        u_prob = sem("u_prob")
        u_turned = sem("u_turned")
        u_pT = sem("u_pT")
        u_val = sem("u_val")
        u_out = sem("u_out")
        ff_silu = sem("ff_silu")
        ff_h = sem("ff_h")
        ff_hi = sem("ff_hi")
        ff_lo = sem("ff_lo")
        lam_v = sem("lam_v")
        lam_a = sem("lam_a")
        logits_out = sem("logits_out")
        logits_turned = sem("logits_turned")
        top_d = sem("top_d")
        top_e = sem("top_e")
        chosen = sem("chosen")
        ranks = sem("ranks")
        routed = sem("routed")
        oh_ready = sem("oh_ready")
        oh_turned = sem("oh_turned")
        ohT_ready = sem("ohT_ready")
        disp = sem("disp")
        xg_h = sem("xg_h")
        xg_l = sem("xg_l")
        e_silu = sem("e_silu")
        e_hr = sem("e_hr")
        e_tr = sem("e_tr")
        e_hi = sem("e_hi")
        e_lo = sem("e_lo")
        e_yo = sem("e_yo")
        e_comb = sem("e_comb")
        e_add = sem("e_add")
        cur_done = sem("cur_done")
        dve_step = sem("dve_step")
        act_step = sem("act_step")
        out_ready = sem("out_ready")
        out_done = sem("out_done")

        def shaped(buf, i, kt, n):
            return buf[:, i, 0:kt * n].rearrange("p (k n) -> p k n", k=kt)

        def gate_end(j):
            return 2 if j == 0 else 6 * j

        def slot_shape(s):
            _, _, kt, _, n = slots[s]
            return kt, n

        units = [("mem", 0, m, t) for m in range(MEM_HEADS // 2) for t in range(TT)]
        NU0 = len(units)
        units += [("mem", 1, m, t) for m in range(MEM_HEADS // 2) for t in range(TT)]
        units += [("diff", 1, h, t) for h in range(DH) for t in range(TT)]
        U_BANK = {"score": (0, 6), "turn": (2, 3), "val": (4, 5)}

        def unit_keys(u):
            kind, _, _, t = units[u]
            return S if kind == "mem" else P * (t + 1)

        def unit_scores_bank(u):
            b = U_BANK["score"][u % 2]
            return ps[:, b:b + 2, 0:unit_keys(u)]

        block = ctx.enter_context(nc.Block())

        @block.sync
        def _(sp):
            sp.dma_start(cst[:, :], consts).then_inc(const_in, 16)
            for t in range(TT):
                sp.dma_start(H[:, t, :], mem[0, P * t:P * t + P, :]).then_inc(mem_in, 16)
            for s, (src, k0, kt, n0, n) in enumerate(slots):
                if s == 2:
                    sp.dma_start(xres[:, :, :], x[0].rearrange("(t p) d -> p t d", p=P)).then_inc(x_in, 16)
                if s >= RAW:
                    sp.wait_ge(lo_ready, s - RAW + 1)
                with nc.allow_non_contiguous_dma(reason="router columns"):
                    sp.dma_start(shaped(raw, s % RAW, kt, n),
                                 src.rearrange("(k p) n -> p k n", p=P)[:, k0:k0 + kt, n0:n0 + n])\
                      .then_inc(raw_in[s % RAW], 16)

            def expert_loads(sweep):
                base = NPRE + sweep * NE * PER_EXPERT
                with sp.Fori(0, NE) as e:
                    u = 0
                    for j in range(STEPS + 1):
                        for wgt in ((w_exp_gate, w_exp_up) if j < STEPS else ()):
                            for half in range(2):
                                s = base + u
                                sp.wait_ge(lo_ready, e * PER_EXPERT + s - RAW + 1)
                                sp.dma_start(shaped(raw, s % RAW, 4, 512),
                                             wgt[0, e].rearrange("(k p) n -> p k n", p=P)
                                             [:, 4 * half:4 * half + 4, 512 * j:512 * j + 512])\
                                  .then_inc(raw_in[s % RAW], 16)
                                u += 1
                        for half in (range(2) if j > 0 else ()):
                            s = base + u
                            sp.wait_ge(lo_ready, e * PER_EXPERT + s - RAW + 1)
                            k0 = 4 * (j - 1) + 2 * half
                            sp.dma_start(shaped(raw, s % RAW, 2, D),
                                         w_exp_down[0, e].rearrange("(k p) n -> p k n", p=P)[:, k0:k0 + 2, :])\
                              .then_inc(raw_in[s % RAW], 16)
                            u += 1

            expert_loads(0)
            sp.wait_ge(routed, 1)
            over = sp.value_load(flag[0:1, 0:1], min_val=0, max_val=S)
            with sp.If(over > P):
                expert_loads(1)
            for t in range(TT):
                sp.wait_ge(out_ready, t + 1)
                sp.dma_start(out[0, P * t:P * t + P, :], H[:, t, :]).then_inc(out_done, 16)
            sp.wait_ge(out_done, 16 * TT)

        @block.gpsimd
        def _(pool):
            gains = [g_mix[0:1, :], g_ffn[0:1, :], g_kv.rearrange("(a d) -> a d", a=1), g_mix[1:2, :],
                     g_ffn[1:2, :], g_final.rearrange("(a d) -> a d", a=1)]
            pool.dma_start(gain[:, :], gains[0].to_broadcast([P, D])).then_inc(gain_in, 16)
            pool.dma_start(wgk, w_gk_up[0]).then_inc(small_in, 16)
            with nc.allow_non_contiguous_dma(reason="384 gate biases"):
                pool.dma_start(bgk[:, :], b_gk[0].rearrange("(h p) -> p h", p=GDK)).then_inc(small_in, 16)
            pool.dma_start(ggla[:, :], g_gla[0:1, :].to_broadcast([P, GDV])).then_inc(small_in, 16)
            pool.dma_start(gsub[:, :], g_subln[0:1, :].to_broadcast([P, DV])).then_inc(small_in, 16)
            for i, v in enumerate((lambda_q1, lambda_k1, lambda_q2, lambda_k2)):
                pool.dma_start(lam4[:, i, :], v[0:1, :].to_broadcast([P, HEAD_DIM])).then_inc(small_in, 16)
            for n, used in zip(range(1, len(gains)), (2, 6, 8, 10, 14)):
                pool.wait_ge(h_ready, used)
                pool.dma_start(gain[:, :], gains[n].to_broadcast([P, D])).then_inc(gain_in, 16)

        N_IN_A = 4 + 12
        N_SMALL = 16 * 8

        @block.scalar
        def _(act):
            steps = [0]

            def link(ins):
                steps[0] += 1
                ins.then_inc(act_step, 1)
                act.wait_ge(act_step, steps[0])

            split = [0]

            def split_to(end):
                for s in range(split[0], end):
                    kt, n = slot_shape(s)
                    act.wait_ge(raw_in[s % RAW], 16 * (s // RAW + 1))
                    if s >= SPLIT:
                        act.wait_ge(slot_used, s - SPLIT + 1)
                    nc.scalar.activation(w_hi[:, s % SPLIT, 0:kt * n], raw[:, s % RAW, 0:kt * n], ACT.Copy)\
                      .then_inc(hi_ready, 1)
                split[0] = max(split[0], end)

            turns = [0]

            def turn():
                n = turns[0]
                for t in range(TT):
                    for half in range(2):
                        act.wait_ge(turned, 4 * n + 2 * t + half + 1)
                        nc.scalar.activation(
                            act_hi[:, 4 * half:4 * half + 4, P * t:P * t + P],
                            ps[:, 2 * t + half, :].rearrange("p (k n) -> p k n", k=4), ACT.Copy).then_inc(turn_hi, 1)
                turns[0] += 1

            def norm(ready, counts):
                for t in range(TT):
                    act.wait_ge(ready, counts[t])
                    link(nc.scalar.activation(H[:, t, :], xres[:, t, :], ACT.Square, accum_out=ss[:, t:t + 1]))
                    nc.scalar.activation(rms[:, t:t + 1], ss[:, t:t + 1], ACT.Sqrt, bias=eps, scale=1.0 / D)\
                      .then_inc(rms_ready, 1)

            def proj(after, dst, src, func=ACT.Copy, ahead=3):
                split_to(after + ahead)
                act.wait_ge(slot_used, after)
                nc.scalar.activation(dst, src, func).then_inc(proj_out, 1)

            def unit_exp(u):
                nk = unit_keys(u)
                act.wait_ge(u_max, u + 1)
                for i in range(2):
                    c = 2 * (u % 3) + i
                    ins = nc.scalar.activation(sc[:, u % 3, 256 * i:256 * i + nk], unit_scores_bank(u)[:, i, :],
                                               ACT.Exp, bias=nbias[:, c:c + 1], scale=HEAD_DIM ** -0.5,
                                               accum_out=rsum[:, c:c + 1])
                ins.then_inc(u_exp, 1)

            def unit_copy(u):
                n = 2 * S if units[u][0] == "mem" else unit_keys(u)
                act.wait_ge(u_turned, u + 1)
                nc.scalar.activation(pT[:, u % 2, 0:n], ps[:, U_BANK["turn"][u % 2], 0:n], ACT.Copy)\
                  .then_inc(u_pT, 1)

            def unit_square(u):
                kind, _, h, t = units[u]
                if kind == "diff":
                    act.wait_ge(u_out, u + 1)
                    hs = slice(DV * h, DV * h + DV)
                    nc.scalar.activation(diff_sq[:, t, hs], diff_o[:, t, hs], ACT.Square,
                                         accum_out=hss[:, DH * t + h:DH * t + h + 1]).then_inc(diff_sqs, 1)

            def attention(u0, u1, slots_end):
                for i in range(u0, u1 + 4):
                    if i < u1:
                        unit_exp(i)
                    if (i - u0) % 3 == 2:
                        split_to(min(split[0] + 1, slots_end))
                    if u0 <= i - 2 < u1:
                        unit_copy(i - 2)
                    if u0 <= i - 4:
                        unit_square(i - 4)

            split_to(1)
            turn()
            split_to(2)
            norm(x_in, (16, 16))
            for l in range(2):
                proj(2 * l + 1, kmT[:, l, :, :], ps[:, 4 + 2 * l, :].rearrange("p (m s) -> p m s", m=2))
                proj(2 * l + 2, vm[:, l, :, :], ps[:, 5 + 2 * l, :].rearrange("p (t n) -> p t n", t=TT),
                     ahead=3 - l)
            turn()
            split_to(4 + 3)
            a = first["in_a"]
            proj(a + 1, gd[0:RANK, 0:S], ps[0:RANK, 4, 0:S])
            proj(a + 2, qmT[:, :, :], ps[:, 5, :].rearrange("p (m s) -> p m s", m=2))
            act.wait_ge(small_in, N_SMALL)
            act.wait_ge(gk_logit, 1)
            for h in range(GH):
                ins = nc.scalar.activation(ge[:, S * h:S * h + S], ps[0:GDK, 6 + h // 2, S * (h % 2):S * (h % 2) + S],
                                           ACT.Identity, bias=bgk[:, h:h + 1])
            ins.then_inc(gk_act, 1)
            act.wait_ge(gk_act, 1)
            nc.scalar.activation(gf, ge, ACT.Abs).then_inc(gk_act, 1)
            act.wait_ge(gk_act, 2)
            nc.scalar.activation(gf, gf, ACT.Exp, scale=-1.0).then_inc(gk_act, 1)
            act.wait_ge(gk_act, 3)
            nc.scalar.activation(gf, gf, ACT.Ln, bias=1.0).then_inc(gk_act, 1)

            def gates(i):
                proj(a + 3 + i, (gq, gk_)[i // 2][:, 512 * (i % 2):512 * (i % 2) + 512], ps[0:GDK, i, :])

            gates(0)
            gates(1)
            act.wait_ge(gk_vec, 2)
            nc.scalar.activation(ge, gd, ACT.Exp, scale=1.0 / 16).then_inc(gk_act, 1)
            nc.scalar.activation(gf, gd, ACT.Exp, scale=-1.0 / 16).then_inc(gk_act, 1)
            gates(2)
            gates(3)
            act.wait_ge(gk_vec, 3)
            nc.scalar.activation(ge, gb, ACT.Exp, scale=1.0 / 16).then_inc(gk_act, 1)
            act.wait_ge(gk_vec, 5)
            nc.scalar.activation(gf, gd, ACT.Exp, scale=1.0 / 16).then_inc(gk_act, 1)
            split_to(a + 10)
            for t in range(TT):
                proj(a + 8, v_tok[:, t, 0:512], ps[:, 4 + t, :])
            proj(a + 9, v_tok[:, :, 512:768], ps[:, 6, :].rearrange("p (t n) -> p t n", t=TT))
            split_to(a + 13)
            for t in range(TT):
                proj(a + 11, H[:, t, 0:512], ps[:, 7 * (1 - t), :], ACT.Silu)
            proj(a + 12, H[:, :, 512:768], ps[:, 1, :].rearrange("p (t n) -> p t n", t=TT), ACT.Silu, ahead=2)
            act.wait_ge(gk_act, 8)
            attention(0, NU0, a + 12 + 3)
            split_to(a + 12 + 3)

            for h in range(GH):
                act.wait_ge(gla_od, h + 1)
                for t in range(TT):
                    ins = nc.scalar.activation(gla_sq[:, t, :], ps[:, 4 + h % 2, 256 * t:256 * t + GDV], ACT.Square,
                                               accum_out=hss[:, TT * h + t:TT * h + t + 1])
                link(ins)
                hs = slice(TT * h, TT * h + TT)
                nc.scalar.activation(hrms[:, hs], hss[:, hs], ACT.Sqrt, bias=eps, scale=1.0 / GDV).then_inc(gla_rms, 1)
            turn()
            split_to(first["dense"] + 2)
            norm(add_done, (3, 4))
            turn()
            split_to(first["dense"] + 3)
            d = first["dense"]
            n_ff = F_DENSE // 256
            for i in range(n_ff + 1):
                base = d + 3 * i - (1 if i > 0 else 0)
                if i < n_ff:
                    split_to(base + 2)
                if i > 0:
                    act.wait_ge(ff_h, i)
                    if i > 2:
                        act.wait_ge(slot_used, base - 3)
                    nc.scalar.activation(f_hi[:, (i - 1) % 2, :, :], f_h.rearrange("p (m s) -> p m s", m=2), ACT.Copy)\
                      .then_inc(ff_hi, 1)
                if i < n_ff:
                    act.wait_ge(slot_used, base + 1)
                    nc.scalar.activation(f_gate, ps[:, i % 2, :], ACT.Silu).then_inc(ff_silu, 1)
                if i > 0:
                    split_to(base + (3 if i < n_ff else 1))
            split_to(first["kv"] + 2)
            norm(add_done, (6, 8))
            turn()
            k = first["kv"]
            split_to(k + 3)
            for t in range(TT):
                proj(k + 2, k_raw[:, t, 0:512], ps[:, 4 + t, :])
            split_to(k + 6)
            for t in range(TT):
                proj(k + 4, k_raw[:, t, 512:768], ps[:, 6 + t, 0:256])
                proj(k + 4, v_tok[:, t, 0:256], ps[:, 6 + t, 256:512])
            split_to(k + 8)
            for t in range(TT):
                proj(k + 6, v_tok[:, t, 256:768], ps[:, t, :], ahead=2)
            b = first["in_b"]
            turn()
            split_to(b + 3)
            for t in range(TT):
                proj(b + 2, q_raw[:, t, 0:512], ps[:, 4 + t, :], ahead=2)
            for t in range(TT):
                proj(b + 4, q_raw[:, t, 512:768], ps[:, 6 + t, 0:256], ahead=1)
                proj(b + 4, qm_tok[:, t, :], ps[:, 6 + t, 256:512], ahead=1)
            for r in range(4):
                dst, t = (kT, qT)[r // 2], r % 2
                act.wait_ge(rope_turned, r + 1)
                nc.scalar.activation(dst[:, 0:4, P * t:P * t + P],
                                     ps[:, 2 * (r % 2), :].rearrange("p (m n) -> p m n", m=4), ACT.Copy)
                if r >= 2:
                    nc.scalar.activation(qmT[:, :, P * t:P * t + P],
                                         ps[:, 2 * (r % 2) + 1, 256:512].rearrange("p (m n) -> p m n", m=2), ACT.Copy)
                nc.scalar.activation(dst[:, 4:6, P * t:P * t + P],
                                     ps[:, 2 * (r % 2) + 1, 0:256].rearrange("p (m n) -> p m n", m=2), ACT.Copy)\
                  .then_inc(rope_out, 1)
            act.wait_ge(lam_v, 1)
            nc.scalar.activation(lamc[:, 2:4], lamc[:, 0:2], ACT.Exp).then_inc(lam_a, 1)
            attention(NU0, len(units), first["out_b"] + 3)
            act.wait_ge(diff_sqs, TT * DH)
            nc.scalar.activation(hrms, hss, ACT.Sqrt, bias=eps, scale=1.0 / DV).then_inc(diff_rms, 1)
            turn()
            split_to(NPRE)
            norm(add_done, (11, 12))
            turn()
            act.wait_ge(top_d, 1)
            nc.scalar.activation(rt[:, 2:4], rt[:, 0:2], ACT.Exp).then_inc(top_e, 1)

            def gathered(sweep, e):
                for half in range(2):
                    act.wait_ge(disp, sweep * 2 * NE + 2 * e + half + 1)
                    nc.scalar.activation(xg_hi[:, 4 * half:4 * half + 4, :],
                                         ps[:, 1 + 2 * half, :].rearrange("p (k n) -> p k n", k=4), ACT.Copy)\
                      .then_inc(xg_h, 1)

            def experts(sweep):
                done = sweep * NE
                base = NPRE + done * PER_EXPERT

                def evacuate_y(i):
                    act.wait_ge(slot_used, i * PER_EXPERT + base)
                    if sweep == 0:
                        act.wait_ge(routed, 1)
                    nc.scalar.activation(y_e[:, 0:512], ps[:, 5, :], ACT.Copy).then_inc(e_yo, 1)
                    nc.scalar.activation(y_e[:, 512:1024], ps[:, 6, :], ACT.Copy).then_inc(e_yo, 1)

                def split_slots(e, u0, n):
                    for s in range(base + u0, base + u0 + n):
                        act.wait_ge(raw_in[s % RAW], e * (16 * PER_EXPERT // RAW) + 16 * (s // RAW + 1))
                        act.wait_ge(slot_used, e * PER_EXPERT + s - E_SPLIT + 1)
                        nc.scalar.activation(e_whi[:, (s - NPRE) % E_SPLIT, :], raw[:, s % RAW, :], ACT.Copy)\
                          .then_inc(hi_ready, 1)

                def hidden(e, j):
                    act.wait_ge(e_tr, (e + done) * STEPS + j + 1)
                    nc.scalar.activation(h_hi, ps[:, 4, :].rearrange("p (m n) -> p m n", m=4), ACT.Copy)\
                      .then_inc(e_hi, 1)

                def expert(e, last):
                    for j in range(STEPS):
                        split_slots(e, gate_end(j), 2)
                        if j == 0:
                            evacuate_y(e)
                        else:
                            split_slots(e, gate_end(j) + 2, 2)
                            hidden(e, j - 1)
                        if j == 2:
                            act.wait_ge(oh_turned, e + done + 1)
                            nc.scalar.activation(ohT[:, :], ps[:, 7, 0:256], ACT.Copy).then_inc(ohT_ready, 1)
                        act.wait_ge(slot_used, e * PER_EXPERT + base + gate_end(j))
                        nc.scalar.activation(e_h[:, :], ps[:, j % 2, :], ACT.Silu).then_inc(e_silu, 1)
                        split_slots(e, gate_end(j + 1) - 2, 2)
                    if not last:
                        split_slots(e, PER_EXPERT, 2)
                    hidden(e, STEPS - 1)
                    if not last:
                        gathered(sweep, e + 1)

                split_slots(0, 0, 2)
                gathered(sweep, 0)
                with act.Fori(0, NE - 1) as e:
                    expert(e, False)
                expert(NE - 1, True)
                evacuate_y(NE)

            act.wait_ge(slot_used, NPRE)
            experts(0)
            act.wait_ge(routed, 1)
            over = act.value_load(flag[0:1, 0:1], min_val=0, max_val=S)
            with act.If(over > P):
                experts(1)
                act.wait_ge(e_add, 2 * 4 * (NE + 1))
            norm(e_add, (4 * (NE + 1) - 2, 4 * (NE + 1)))

        @block.vector
        def _(dve):
            steps = [0]

            def link(ins):
                steps[0] += 1
                ins.then_inc(dve_step, 1)
                dve.wait_ge(dve_step, steps[0])

            split = [0]

            def split_to(end):
                for s in range(split[0], end):
                    kt, n = slot_shape(s)
                    dve.wait_ge(hi_ready, s + 1)
                    nc.vector.tensor_tensor(w_lo[:, s % SPLIT, 0:kt * n], raw[:, s % RAW, 0:kt * n],
                                            w_hi[:, s % SPLIT, 0:kt * n].bitcast(F32), ALU.subtract)\
                      .then_inc(lo_ready, 1)
                split[0] = max(split[0], end)

            turns = [0]

            def turn():
                n = turns[0]
                for t in range(TT):
                    for half in range(2):
                        dve.wait_ge(turn_hi, 4 * n + 2 * t + half + 1)
                        ks = slice(4 * half, 4 * half + 4)
                        nc.vector.tensor_tensor(
                            act_lo[:, ks, P * t:P * t + P], ps[:, 2 * t + half, :].rearrange("p (k n) -> p k n", k=4),
                            act_hi[:, ks, P * t:P * t + P].bitcast(F32), ALU.subtract).then_inc(turn_lo, 1)
                turns[0] += 1

            norms = [0]

            def norm(signal, streams, new=True):
                n = norms[0]
                dve.wait_ge(gain_in, 16 * (n + 1))
                for t in range(TT):
                    if new:
                        dve.wait_ge(rms_ready, TT * (streams - 1) + t + 1)
                        link(nc.vector.reciprocal(rs[:, t:t + 1], rms[:, t:t + 1]))
                    nc.vector.scalar_tensor_tensor(out=H[:, t, :], in0=xres[:, t, :], scalar=rs[:, t:t + 1],
                                                   in1=gain[:, :], op0=ALU.mult, op1=ALU.mult).then_inc(signal, 1)
                norms[0] += 1

            def residual(t, half, bank):
                xs = xres[:, t, 512 * half:512 * half + 512]
                nc.vector.tensor_tensor(xs, xs, ps[:, bank, :], ALU.add).then_inc(add_done, 1)

            def out_residual(n, end):
                dve.wait_ge(slot_used, end - 2)
                for t in range(TT):
                    residual(t, 0, 4 + t)
                split_to(min(end + 2, NPRE))
                dve.wait_ge(tile0_done, 2 * n + 1)
                residual(0, 1, 6)
                dve.wait_ge(slot_used, end)
                residual(1, 1, 7)

            def unit_max(u):
                c = 2 * (u % 3)
                scores = unit_scores_bank(u)
                dve.wait_ge(u_score, u + 1)
                if units[u][0] == "diff":
                    last = scores[:, :, unit_keys(u) - P:unit_keys(u)]
                    m = cst[:, C_CAUSAL:C_CAUSAL + P].rearrange("p (o n) -> p o n", o=1).to_broadcast([P, 2, P])
                    link(nc.vector.tensor_tensor(last, last, m, ALU.add))
                link(nc.vector.tensor_reduce(nmax[:, c:c + 2], scores, AX.X, ALU.max, negate=True))
                nc.vector.tensor_scalar(nbias[:, c:c + 2], nmax[:, c:c + 2], HEAD_DIM ** -0.5, None, ALU.mult)\
                  .then_inc(u_max, 1)

            def unit_prob(u):
                nk = unit_keys(u)
                c, r = 2 * (u % 3), 2 * (u % 4)
                b0, b1 = sc[:, u % 3, 0:nk], sc[:, u % 3, 256:256 + nk]
                w = blend[:, u % 3:u % 3 + 1]
                dve.wait_ge(u_exp, u + 1)
                if units[u][0] == "mem":
                    nc.vector.reciprocal(rinv[:, r:r + 2], rsum[:, c:c + 2]).then_inc(u_prob, 1)
                    return
                link(nc.vector.reciprocal(rinv[:, r:r + 2], rsum[:, c:c + 2]))
                link(nc.vector.tensor_scalar(w, rinv[:, r + 1:r + 2], rsum[:, c:c + 1], lamc[:, 5:6],
                                             ALU.mult, ALU.mult))
                nc.vector.scalar_tensor_tensor(out=b0, in0=b1, scalar=w, in1=b0, op0=ALU.mult, op1=ALU.add)\
                  .then_inc(u_prob, 1)

            def unit_out(u):
                kind, _, h, t = units[u]
                r = 2 * (u % 4)
                val = ps[:, U_BANK["val"][u % 2], 0:P]
                dve.wait_ge(u_val, u + 1)
                if kind == "diff":
                    nc.vector.tensor_scalar(diff_o[:, t, DV * h:DV * h + DV], val, rinv[:, r:r + 1], None, ALU.mult)\
                      .then_inc(u_out, 1)
                    return
                for i in range(2):
                    f = MIX + HEAD_DIM * (2 * h + i)
                    ins = nc.vector.tensor_scalar(H[:, t, f:f + HEAD_DIM], val[:, HEAD_DIM * i:HEAD_DIM * (i + 1)],
                                                  rinv[:, r + i:r + i + 1], None, ALU.mult)
                ins.then_inc(u_out, 1)

            def attention(u0, u1, slots_end):
                for i in range(u0, u1 + 3):
                    if i < u1:
                        unit_max(i)
                    if (i - u0) % 3 == 2:
                        split_to(min(split[0] + 1, slots_end))
                    if u0 <= i - 1 < u1:
                        unit_prob(i - 1)
                    if u0 <= i - 3:
                        unit_out(i - 3)

            def head_roots(n):
                link(nc.vector.reciprocal(hrs[:, n], hrms[:, n]))

            link(nc.vector.memset(ones[:, :], 1.0))
            link(nc.vector.memset(ki, 1.0))
            link(nc.vector.memset(ki[:, 0:D:CHUNK], 0.0))
            split_to(1)
            turn()
            split_to(2)
            norm(h_ready, 1)
            split_to(4 + 2)
            turn()
            split_to(4 + 3)
            a = first["in_a"]
            split_to(a + 5)
            dve.wait_ge(small_in, N_SMALL)
            link(nc.vector.tensor_tensor(lam4[:, 0:3:2, :], lam4[:, 0:3:2, :], lam4[:, 1:4:2, :], ALU.mult))
            nc.vector.tensor_reduce(lamc[:, 0:2], lam4[:, 0:3:2, :], AX.X, ALU.add).then_inc(lam_v, 1)
            dve.wait_ge(gk_act, 4)
            link(nc.vector.scalar_tensor_tensor(out=ge, in0=ge, scalar=0.0, in1=gf, op0=ALU.min, op1=ALU.subtract))
            nc.vector.tensor_tensor_scan(gb, ki, ge, 0.0, ALU.mult, ALU.add).then_inc(gk_vec, 1)
            dve.wait_ge(gk_vec, 1)
            split_to(a + 6)

            def chunks(buf):
                return buf.rearrange("p (c n) -> p c n", n=CHUNK)

            def at(col):
                return chunks(gb)[:, :, col:col + 1].to_broadcast([GDK, GH * NCH, CHUNK])

            dve.wait_ge(gk_logit, 1)
            nc.vector.tensor_tensor(chunks(gd), chunks(gb), at(CHUNK // 2 - 1), ALU.subtract).then_inc(gk_vec, 1)
            split_to(a + 7)
            dve.wait_ge(proj_out, 4 + 1 + 1 + 2)
            dve.wait_ge(gk_act, 5)
            nc.vector.scalar_tensor_tensor(out=qi, in0=gq, scalar=GDK ** -0.5, in1=ge, op0=ALU.mult, op1=ALU.mult)\
              .then_inc(gk_vec, 1)
            split_to(a + 9)
            dve.wait_ge(proj_out, 4 + 1 + 1 + 4)
            dve.wait_ge(gk_act, 6)
            nc.vector.tensor_tensor(ki, gk_, gf, ALU.mult).then_inc(gk_vec, 1)
            nc.vector.tensor_tensor(chunks(gd), at(CHUNK - 1), chunks(gb), ALU.subtract).then_inc(gk_vec, 1)
            dve.wait_ge(gk_act, 7)
            nc.vector.scalar_tensor_tensor(out=gq, in0=gq, scalar=GDK ** -0.5, in1=ge, op0=ALU.mult, op1=ALU.mult)\
              .then_inc(gk_vec, 1)
            dve.wait_ge(gk_act, 8)
            nc.vector.tensor_tensor(gk_, gk_, gf, ALU.mult).then_inc(gk_vec, 1)
            dve.wait_ge(gk_vec, 7)
            link(nc.vector.tensor_copy(small[0:GDK, 104:120], ge[:, CHUNK - 1:D:CHUNK]))
            decay = small[0:GDK, 104:120]
            for buf in sT:
                link(nc.vector.memset(buf, 0.0))
            split_to(a + 14)
            attention(0, NU0, a + 12 + 3)
            split_to(a + 12 + 2)
            def gla_scores(h):
                dve.wait_ge(gla_sc, h + 1)
                if h >= 2:
                    dve.wait_ge(gla_od, h - 1)
                for t in range(TT):
                    for c in range(2):
                        r = slice(CHUNK * c, CHUNK * c + CHUNK)
                        nc.vector.copy_predicated(sT[h % 2][r, t, r], cst[r, C_GLA:C_GLA + CHUNK].bitcast(U32),
                                                  ps[r, h % 2, P * t + CHUNK * c:P * t + CHUNK * c + CHUNK])
                nc.vector.tensor_copy(kdT[h % 2], ps[:, h % 2, 256:256 + 2 * GDK].rearrange("p (t n) -> p t n", t=TT))\
                  .then_inc(gla_sce, 1)

            def gla_states(h):
                kv, st = 2 + 4 * (h % 2), state[h % 2]
                dve.wait_ge(gla_kv, h + 1)
                link(nc.vector.tensor_copy(st[:, 0, :], ps[0:GDK, kv, 0:GDV]))
                link(nc.vector.scalar_tensor_tensor(out=st[:, 1, :], in0=st[:, 0, :],
                                                    scalar=decay[:, NCH * h + 1:NCH * h + 2],
                                                    in1=ps[0:GDK, kv + 1, 0:GDV], op0=ALU.mult, op1=ALU.add))
                nc.vector.scalar_tensor_tensor(out=st[:, 2, :], in0=st[:, 1, :],
                                               scalar=decay[:, NCH * h + 2:NCH * h + 3],
                                               in1=ps[0:GDK, kv, 256:256 + GDV], op0=ALU.mult, op1=ALU.add)\
                  .then_inc(gla_st, 1)

            def gla_outputs(h):
                dve.wait_ge(gla_rms, h + 1)
                head_roots(slice(TT * h, TT * h + TT))
                for t in range(TT):
                    g = H[:, t, GDV * h:GDV * h + GDV]
                    ins = nc.vector.scalar_tensor_tensor(out=g, in0=ps[:, 4 + h % 2, 256 * t:256 * t + GDV],
                                                         scalar=hrs[:, TT * h + t:TT * h + t + 1], in1=g,
                                                         op0=ALU.mult, op1=ALU.mult)
                    if h == GH - 1:
                        ins.then_inc(h_ready, 1)
                if h < GH - 1:
                    ins.then_inc(gla_oe, 1)

            for i in range(GH + 3):
                if i < GH:
                    gla_scores(i)
                if 0 <= i - 1 < GH:
                    gla_states(i - 1)
                if i == 2:
                    dve.wait_ge(proj_out, N_IN_A)
                    for t in range(TT):
                        g_out = H[:, t, 0:MIX].rearrange("p (h n) -> p h n", h=GH)
                        link(nc.vector.tensor_tensor(g_out, g_out, ggla.rearrange("p (o n) -> p o n", o=1)
                                                     .to_broadcast([P, GH, GDV]), ALU.mult))
                if 0 <= i - 3:
                    gla_outputs(i - 3)
            turn()
            split_to(first["dense"] + 1)
            out_residual(0, first["dense"])
            norm(h_ready, 2)
            turn()
            split_to(first["dense"] + 3)
            d = first["dense"]
            n_ff = F_DENSE // 256
            for i in range(n_ff + 1):
                base = d + 3 * i - (1 if i > 0 else 0)
                if i < n_ff:
                    split_to(base + 2)
                if i > 0:
                    dve.wait_ge(ff_hi, i)
                    nc.vector.tensor_tensor(f_lo[:, (i - 1) % 2, :, :], f_h.rearrange("p (m s) -> p m s", m=2),
                                            f_hi[:, (i - 1) % 2, :, :].bitcast(F32), ALU.subtract).then_inc(ff_lo, 1)
                    split_to(base + (3 if i < n_ff else 1))
                if i < n_ff:
                    dve.wait_ge(ff_silu, i + 1)
                    dve.wait_ge(slot_used, base + 2)
                    if i > 0:
                        dve.wait_ge(ff_lo, i)
                    nc.vector.tensor_tensor(f_h, f_gate, ps[:, 2 + i % 2, :], ALU.mult).then_inc(ff_h, 1)
            split_to(first["kv"] + 2)
            dve.wait_ge(tile0_done, 2)
            for half in range(2):
                residual(0, half, 4 + half)
            dve.wait_ge(slot_used, first["kv"])
            for half in range(2):
                residual(1, half, 6 + half)
            norm(h_ready, 3)
            turn()
            split_to(first["kv"] + 3)
            norm(h_ready, 3, new=False)
            split_to(first["in_b"] + 2)
            turn()
            split_to(first["in_b"] + 3)

            ropes = [0]

            def rope(src, t, evacuated):
                dve.wait_ge(proj_out, evacuated)
                v = src[:, t, :].rearrange("p (h c d) -> p h c d", h=2 * DH, c=2)
                o = rot[:, t, :].rearrange("p (h c d) -> p h c d", h=2 * DH, c=2)
                cs, sn = (cos_sin[:, t, i:i + 1, :].to_broadcast([P, 2 * DH, HEAD_DIM // 2]) for i in range(2))
                tmp = [rope_t[:, i, :].rearrange("p (h d) -> p h d", h=2 * DH) for i in range(4)]
                if ropes[0] > 0:
                    dve.wait_ge(roped, ropes[0])
                for i, (a_, b_) in enumerate(((v[:, :, 0, :], cs), (v[:, :, 1, :], sn), (v[:, :, 0, :], sn),
                                              (v[:, :, 1, :], cs))):
                    ins = nc.vector.tensor_tensor(tmp[i], a_, b_, ALU.mult)
                link(ins)
                if ropes[0] >= 2:
                    dve.wait_ge(rope_turned, ropes[0] - 1)
                nc.vector.tensor_tensor(o[:, :, 0, :], tmp[0], tmp[1], ALU.subtract)
                nc.vector.tensor_tensor(o[:, :, 1, :], tmp[2], tmp[3], ALU.add).then_inc(roped, 1)
                ropes[0] += 1

            kv_out = 4 + 12 + 0 + 2 + 4 + 2
            rope(k_raw, 0, kv_out)
            rope(k_raw, 1, kv_out)
            split_to(first["in_b"] + 4)
            rope(q_raw, 0, kv_out + 6)
            rope(q_raw, 1, kv_out + 6)
            dve.wait_ge(roped, 4)
            dve.wait_ge(lam_a, 1)
            link(nc.vector.tensor_tensor(lamc[:, 4:5], lamc[:, 3:4], lamc[:, 2:3], ALU.subtract))
            link(nc.vector.tensor_scalar(lamc[:, 5:6], lamc[:, 4:5], -LAMBDA_INIT, None, ALU.add))
            link(nc.vector.tensor_scalar(gsub[:, :], gsub[:, :], 1.0 - LAMBDA_INIT, None, ALU.mult))
            attention(NU0, len(units), first["out_b"] + 3)
            dve.wait_ge(diff_rms, 1)
            head_roots(slice(0, TT * DH))
            for t in range(TT):
                for h in range(DH):
                    ins = nc.vector.scalar_tensor_tensor(out=H[:, t, DV * h:DV * h + DV],
                                                         in0=diff_o[:, t, DV * h:DV * h + DV],
                                                         scalar=hrs[:, DH * t + h:DH * t + h + 1],
                                                         in1=gsub[:, :], op0=ALU.mult, op1=ALU.mult)
                ins.then_inc(h_ready, 1)
            turn()
            out_residual(1, NPRE - 1)
            norm(h_ready, 4)
            turn()

            link(nc.vector.memset(route_gate[:, :, :], 0.0))
            link(nc.vector.memset(flag[:, :], 0))
            dve.wait_ge(slot_used, NPRE)
            nc.vector.tensor_copy(logT, ps[0:NE, 4, 0:S]).then_inc(logits_out, 1)
            lg = rt[:, 8:24].rearrange("p (t e) -> p t e", t=TT)
            dve.wait_ge(logits_turned, 1)
            link(nc.vector.tensor_copy(lg, ps[:, 5, 0:TT * NE].rearrange("p (t e) -> p t e", t=TT)))
            for t in range(TT):
                ins = nc.vector.max(top8[:, t, :], lg[:, t, :])
            link(ins)
            for t in range(TT):
                ins = nc.vector.max_index(idx8[:, t, :], top8[:, t, :], lg[:, t, :])
            nc.vector.tensor_tensor(rt[:, 0:2], top8[:, :, 1], top8[:, :, 0], ALU.subtract).then_inc(top_d, 1)
            dve.wait_ge(top_d, 1)
            link(nc.vector.tensor_copy(fidx, idx8[:, :, :]))

            def per_token(column):
                return column.rearrange("p (t o) -> p t o", o=1).to_broadcast([P, TT, NE])

            iota8 = cst[:, C_IOTA:C_IOTA + NE].rearrange("p (o e) -> p o e", o=1).to_broadcast([P, TT, NE])
            nc.vector.tensor_tensor(sel1, iota8, fidx[:, :, 0:1].to_broadcast([P, TT, NE]), ALU.is_equal)
            link(nc.vector.tensor_tensor(sel2, iota8, fidx[:, :, 1:2].to_broadcast([P, TT, NE]), ALU.is_equal))
            nc.vector.tensor_tensor(msk, sel1, sel2, ALU.add).then_inc(chosen, 1)
            dve.wait_ge(top_e, 1)
            link(nc.vector.tensor_scalar(rt[:, 4:6], rt[:, 2:4], 1.0, None, ALU.add))
            link(nc.vector.reciprocal(rt[:, 4:6], rt[:, 4:6]))
            link(nc.vector.tensor_tensor(rt[:, 6:8], rt[:, 2:4], rt[:, 4:6], ALU.mult))
            nc.vector.tensor_tensor(sel1, sel1, per_token(rt[:, 4:6]), ALU.mult)
            link(nc.vector.tensor_tensor(sel2, sel2, per_token(rt[:, 6:8]), ALU.mult))
            link(nc.vector.tensor_tensor(route_gate[:, :, 1:NE + 1], sel1, sel2, ALU.add))
            dve.wait_ge(ranks, 1)
            cnt = ps[:, 6, 0:TT * NE].rearrange("p (t e) -> p t e", t=TT)
            link(nc.vector.scalar_tensor_tensor(out=msk, in0=cnt, scalar=1.0, in1=msk, op0=ALU.add, op1=ALU.mult))
            link(nc.vector.tensor_scalar(route_rank[:, :, :], msk, -1.0, None, ALU.add))

            def one_hot(sweep):
                for t in range(TT):
                    nc.vector.tensor_scalar(oh[:, t, :], cst[:, C_IOTA + P * sweep:C_IOTA + P * sweep + P],
                                            cur_rank[:, t:t + 1], None, ALU.is_equal).then_inc(oh_ready, 1)

            def gathered(sweep, e):
                for half in range(2):
                    dve.wait_ge(xg_h, sweep * 2 * NE + 2 * e + half + 1)
                    nc.vector.tensor_tensor(xg_lo[:, 4 * half:4 * half + 4, :],
                                            ps[:, 1 + 2 * half, :].rearrange("p (k n) -> p k n", k=4),
                                            xg_hi[:, 4 * half:4 * half + 4, :].bitcast(F32), ALU.subtract)\
                      .then_inc(xg_l, 1)

            def experts(sweep):
                done = sweep * NE
                cd = sweep * (2 * NE + 1)
                if sweep == 0:
                    nc.vector.memset(ohT[:, :], 0.0)
                nc.vector.tensor_copy(cur_rank.rearrange("p (t o) -> p t o", o=1), route_rank[:, :, 0:1])\
                  .then_inc(cur_done, 1)
                dve.wait_ge(cur_done, cd + 1)
                one_hot(sweep)
                if sweep == 0:
                    link(nc.vector.tensor_reduce(rt[:, 24:25], ps[:, 6, 2 * NE:3 * NE], AX.X, ALU.max))
                    nc.vector.tensor_copy(flag[0:1, 0:1], rt[0:1, 24:25]).then_inc(routed, 1)
                base = NPRE + done * PER_EXPERT

                def add_tile(i, t):
                    for n in (2 * t, 2 * t + 1):
                        dve.wait_ge(e_comb, (i + sweep * (NE + 1)) * 4 + n + 1)
                        xs = xres[:, t, 512 * (n % 2):512 * (n % 2) + 512]
                        nc.vector.scalar_tensor_tensor(out=xs, in0=ps[:, SCATTER_BANKS[n], :],
                                                       scalar=cur_gate[:, t:t + 1], in1=xs,
                                                       op0=ALU.mult, op1=ALU.add).then_inc(e_add, 1)

                def split_slots(e, u0, n):
                    for s in range(base + u0, base + u0 + n):
                        dve.wait_ge(hi_ready, e * PER_EXPERT + s + 1)
                        r = (s - NPRE) % E_SPLIT
                        nc.vector.tensor_tensor(e_wlo[:, r, :], raw[:, s % RAW, :],
                                                e_whi[:, r, :].bitcast(F32), ALU.subtract).then_inc(lo_ready, 1)

                def hidden(e, j):
                    dve.wait_ge(e_hi, (e + done) * STEPS + j + 1)
                    nc.vector.tensor_tensor(h_lo, ps[:, 4, :].rearrange("p (m n) -> p m n", m=4),
                                            h_hi.bitcast(F32), ALU.subtract).then_inc(e_lo, 1)

                def column(table, e):
                    return table[:, :, e:e + 1] if isinstance(e, int) else table[:, :, bass.ds(e, 1)]

                def expert(e, last):
                    for j in range(STEPS):
                        split_slots(e, gate_end(j), 2)
                        if j == 0:
                            nc.vector.tensor_copy(cur_gate.rearrange("p (t o) -> p t o", o=1),
                                                  column(route_gate, e)).then_inc(cur_done, 1)
                        if j == 3 and not last:
                            nc.vector.tensor_copy(cur_rank.rearrange("p (t o) -> p t o", o=1),
                                                  column(route_rank, e + 1)).then_inc(cur_done, 1)
                            dve.wait_ge(cur_done, 2 * e + cd + 3)
                            one_hot(sweep)
                        if j > 0:
                            split_slots(e, gate_end(j) + 2, 2)
                            hidden(e, j - 1)
                        if j == 1:
                            add_tile(e, 1)
                        split_slots(e, gate_end(j + 1) - 2, 2)
                        dve.wait_ge(e_silu, (e + done) * STEPS + j + 1)
                        dve.wait_ge(slot_used, e * PER_EXPERT + base + gate_end(j) + 2)
                        nc.vector.tensor_tensor(e_h[:, :], e_h[:, :], ps[:, 2 + j % 2, :], ALU.mult).then_inc(e_hr, 1)
                        if j == 0:
                            dve.wait_ge(cur_done, 2 * e + cd + 2)
                            add_tile(e, 0)
                    if not last:
                        split_slots(e, PER_EXPERT, 2)
                    hidden(e, STEPS - 1)
                    if not last:
                        gathered(sweep, e + 1)

                split_slots(0, 0, 2)
                gathered(sweep, 0)
                with dve.Fori(0, NE - 1) as e:
                    expert(e, False)
                expert(NE - 1, True)
                nc.vector.tensor_copy(cur_gate.rearrange("p (t o) -> p t o", o=1), route_gate[:, :, NE:NE + 1])\
                  .then_inc(cur_done, 1)
                dve.wait_ge(cur_done, cd + 2 * NE + 1)
                for t in range(TT):
                    add_tile(NE, t)

            experts(0)
            dve.wait_ge(routed, 1)
            over = dve.value_load(flag[0:1, 0:1], min_val=0, max_val=S)
            with dve.If(over > P):
                experts(1)
                dve.wait_ge(e_add, 2 * 4 * (NE + 1))
            dve.wait_ge(e_add, 4 * (NE + 1))
            norm(out_ready, 5)

        @block.tensor
        def _(pe):
            def three(dst, l_hi, l_lo, r_hi, r_lo, start, stop):
                nc.tensor.matmul(dst, l_hi, r_hi, start=start, stop=False)
                nc.tensor.matmul(dst, l_lo, r_hi, start=False, stop=False)
                return nc.tensor.matmul(dst, l_hi, r_lo, start=False, stop=stop)

            used = [0]

            def take():
                s = used[0]
                used[0] += 1
                kt, n = slot_shape(s)
                pe.wait_ge(lo_ready, s + 1)
                return shaped(w_hi, s % SPLIT, kt, n), shaped(w_lo, s % SPLIT, kt, n)

            turns = [0]

            def turn():
                for t in range(TT):
                    if turns[0] == 0:
                        pe.wait_ge(mem_in, 16 * TT)
                    else:
                        pe.wait_ge(h_ready, TT * (turns[0] - 1) + t + 1)
                    for half in range(2):
                        for k in range(4):
                            c = P * (4 * half + k)
                            ins = nc.tensor.transpose(ps[:, 2 * t + half, P * k:P * k + P], H[:, t, c:c + P], ident)
                        ins.then_inc(turned, 1)
                turns[0] += 1

            def await_turned(quarters):
                pe.wait_ge(turn_lo, 4 * (turns[0] - 1) + quarters)

            def token_major(banks, tile0=False):
                for i in range(2):
                    hi, lo = take()
                    for t in range(TT):
                        await_turned(1 + 2 * t if i == 0 else 4)
                        ts = slice(P * t, P * t + P)
                        for kk in range(KT // 2):
                            k = KT // 2 * i + kk
                            ins = three(banks[t], act_hi[:, k, ts], act_lo[:, k, ts], hi[:, kk, :], lo[:, kk, :],
                                        k == 0, k == KT - 1)
                        if tile0 and i == 1 and t == 0:
                            ins.then_inc(tile0_done, 1)
                    if i == 0:
                        ins.then_inc(slot_used, 1)
                return ins

            def feature_major(regions, width):
                hi, lo = take()
                for m, reg in enumerate(regions):
                    for k in range(KT):
                        if m == 0 and k % (KT // 2) == 0:
                            await_turned(3 if k == 0 else 4)
                        c = slice(width * m, width * m + width)
                        ins = three(reg, hi[:, k, c], lo[:, k, c], act_hi[:, k, :], act_lo[:, k, :], k == 0, k == KT - 1)
                return ins

            def mark(ins):
                ins.then_inc(slot_used, 1)

            def halves(b):
                return [ps[:, b, 0:256], ps[:, b, 256:512]]

            pe.wait_ge(const_in, 16)
            turn()
            for l in range(2):
                mark(feature_major(halves(4 + 2 * l), P))
                hi, lo = take()
                for t in range(TT):
                    for k in range(KT):
                        ts = slice(P * t, P * t + P)
                        ins = three(halves(5 + 2 * l)[t], act_hi[:, k, ts], act_lo[:, k, ts], hi[:, k, :], lo[:, k, :],
                                    k == 0, k == KT - 1)
                mark(ins)
            turn()
            pe.wait_ge(proj_out, 4)
            mark(feature_major([ps[0:RANK, 4, 0:S]], RANK))
            mark(feature_major(halves(5), P))
            pe.wait_ge(proj_out, 5)
            pe.wait_ge(small_in, N_SMALL)
            for h in range(GH):
                ins = nc.tensor.matmul(ps[0:GDK, 6 + h // 2, S * (h % 2):S * (h % 2) + S],
                                       wgk[:, GDK * h:GDK * h + GDK], gd[0:RANK, 0:S], start=True, stop=True)
            ins.then_inc(gk_logit, 1)
            for i in range(4):
                mark(feature_major([ps[0:GDK, i, 0:S], ps[0:GDK, i, S:2 * S]], GDK))

            def two_blocks(b512, b256):
                mark(token_major([ps[:, b512[0], :], ps[:, b512[1], :]]))
                hi, lo = take()
                for t in range(TT):
                    for k in range(KT):
                        ts = slice(P * t, P * t + P)
                        ins = three(halves(b256)[t], act_hi[:, k, ts], act_lo[:, k, ts], hi[:, k, :], lo[:, k, :],
                                    k == 0, k == KT - 1)
                mark(ins)

            pe.wait_ge(proj_out, 6)
            pe.wait_ge(gk_act, 1)
            two_blocks((4, 5), 6)
            pe.wait_ge(proj_out, 6 + 2)
            two_blocks((7, 0), 1)

            def unit_scores(u):
                kind, l, h, t = units[u]
                if u >= 2:
                    pe.wait_ge(u_exp, u - 1)
                scores = unit_scores_bank(u)
                q, k = (qmT, kmT[:, l, :, :]) if kind == "mem" else (qT, kT)
                for i in range(2):
                    r = slice(HEAD_DIM * i, HEAD_DIM * i + HEAD_DIM)
                    ins = nc.tensor.matmul(scores[:, i, :], q[r, h, P * t:P * t + P], k[r, h, 0:unit_keys(u)],
                                           start=True, stop=True)
                ins.then_inc(u_score, 1)

            def unit_turn(u):
                pe.wait_ge(u_prob, u + 1)
                if u >= 2:
                    pe.wait_ge(u_pT, u - 1)
                for k in range((2 * S if units[u][0] == "mem" else unit_keys(u)) // P):
                    ins = nc.tensor.transpose(ps[:, U_BANK["turn"][u % 2], P * k:P * k + P],
                                              sc[:, u % 3, P * k:P * k + P], ident)
                ins.then_inc(u_turned, 1)

            def unit_values(u):
                kind, l, h, _ = units[u]
                nk = unit_keys(u)
                pe.wait_ge(u_pT, u + 1)
                if u >= 2:
                    pe.wait_ge(u_out, u - 1)
                if kind == "mem":
                    parts = [(vm[:, l], HEAD_DIM * (2 * h + i), HEAD_DIM, HEAD_DIM * i, S * i) for i in range(2)]
                else:
                    parts = [(v_tok, DV * h, DV, 0, 0)]
                for v, f, w, to, p0 in parts:
                    for k in range(nk // P):
                        ins = nc.tensor.matmul(ps[:, U_BANK["val"][u % 2], to:to + w],
                                               pT[:, u % 2, p0 + P * k:p0 + P * k + P], v[:, k, f:f + w],
                                               start=(k == 0), stop=(k == nk // P - 1))
                ins.then_inc(u_val, 1)

            def attention(u0, u1):
                for i in range(u0, u1 + 3):
                    if i < u1:
                        unit_scores(i)
                    if u0 <= i - 2 < u1:
                        unit_turn(i - 2)
                    if u0 <= i - 3:
                        unit_values(i - 3)

            pe.wait_ge(proj_out, N_IN_A)
            attention(0, NU0)
            pe.wait_ge(gk_vec, 7)
            pe.wait_ge(u_out, NU0)

            def gla_scores(h):
                hd = slice(S * h, S * h + S)
                if h >= 2:
                    pe.wait_ge(gla_sce, h - 1)
                for n in range(NCH):
                    t, c = n // 2, n % 2
                    cs = slice(CHUNK * n, CHUNK * n + CHUNK)
                    nc.tensor.matmul(ps[CHUNK * c:CHUNK * c + CHUNK, h % 2, P * t + CHUNK * c:P * t + CHUNK * c + CHUNK],
                                     ki[:, hd][:, cs], qi[:, hd][:, cs], start=True, stop=True, skip_group_check=True)
                for t in range(TT):
                    ins = nc.tensor.transpose(ps[:, h % 2, 256 + GDK * t:256 + GDK * t + GDK],
                                              gk_[:, hd][:, P * t:P * t + P], ident[0:GDK, 0:GDK])
                ins.then_inc(gla_sc, 1)

            def gla_chunk_kv(h):
                pe.wait_ge(gla_sce, h + 1)
                if h >= 2:
                    pe.wait_ge(gla_st, h - 1)
                for n in range(NCH - 1):
                    t, r = n // 2, slice(CHUNK * (n % 2), CHUNK * (n % 2) + CHUNK)
                    ins = nc.tensor.matmul(ps[0:GDK, 2 + 4 * (h % 2) + n % 2, 256 * (n // 2):256 * (n // 2) + GDV],
                                           kdT[h % 2][r, t, :], v_tok[r, t, GDV * h:GDV * h + GDV],
                                           start=True, stop=True)
                ins.then_inc(gla_kv, 1)

            def gla_outputs(h):
                pe.wait_ge(gla_st, h + 1)
                if h >= 2:
                    pe.wait_ge(gla_oe, h - 1)
                for t in range(TT):
                    o = ps[:, 4 + h % 2, 256 * t:256 * t + GDV]
                    nc.tensor.matmul(o, sT[h % 2][:, t, :], v_tok[:, t, GDV * h:GDV * h + GDV], start=True,
                                     stop=False, skip_group_check=True)
                    for c in range(2):
                        n = 2 * t + c
                        if n == 0:
                            continue
                        q_st = gq[:, S * h + CHUNK * n:S * h + CHUNK * n + CHUNK]
                        ins = nc.tensor.matmul(o[CHUNK * c:CHUNK * c + CHUNK, :], q_st, state[h % 2][:, n - 1, :],
                                               start=False, stop=True, skip_group_check=True)
                ins.then_inc(gla_od, 1)

            for i in range(GH + 2):
                if i < GH:
                    gla_scores(i)
                if 0 <= i - 1 < GH:
                    gla_chunk_kv(i - 1)
                if 0 <= i - 2:
                    gla_outputs(i - 2)
            turn()

            def out_projection():
                mark(token_major([ps[:, 4, :], ps[:, 5, :]]))
                mark(token_major([ps[:, 6, :], ps[:, 7, :]], tile0=True))

            out_projection()
            turn()
            pe.wait_ge(add_done, 4)
            n_ff = F_DENSE // 256
            for i in range(n_ff + 1):
                if i < n_ff:
                    if i >= 2:
                        pe.wait_ge(ff_silu, i - 1)
                        pe.wait_ge(ff_h, i - 1)
                    for j in range(2):
                        mark(feature_major(halves(2 * j + i % 2), P))
                if i > 0:
                    pe.wait_ge(ff_lo, i)
                    hi, lo = take()
                    c = (i - 1) % 2
                    for t in range(TT):
                        ts = slice(P * t, P * t + P)
                        for m in range(2):
                            for n in range(2):
                                ns = slice(512 * n, 512 * n + 512)
                                ins = three(ps[:, 4 + 2 * t + n, :], f_hi[:, c, m, ts], f_lo[:, c, m, ts],
                                            hi[:, m, ns], lo[:, m, ns], i == 1 and m == 0, i == n_ff and m == 1)
                        if i == n_ff and t == 0:
                            ins.then_inc(tile0_done, 1)
                    mark(ins)
            turn()
            pe.wait_ge(add_done, 8)
            mark(token_major([ps[:, 4, :], ps[:, 5, :]]))
            mark(token_major([ps[:, 6, :], ps[:, 7, :]]))
            mark(token_major([ps[:, 0, :], ps[:, 1, :]]))
            pe.wait_ge(proj_out, 16 + 8)
            turn()
            mark(token_major([ps[:, 4, :], ps[:, 5, :]]))
            mark(token_major([ps[:, 6, :], ps[:, 7, :]]))
            for r in range(4):
                t = r % 2
                pe.wait_ge(roped, r + 1)
                if r >= 2:
                    pe.wait_ge(rope_out, r - 1)
                for m in range(DH):
                    ins = nc.tensor.transpose(ps[:, 2 * t + m // 4, P * (m % 4):P * (m % 4) + P],
                                              rot[:, t, P * m:P * m + P], ident)
                if r >= 2:
                    for m in range(2):
                        ins = nc.tensor.transpose(ps[:, 2 * t + 1, 256 + P * m:256 + P * m + P],
                                                  qm_tok[:, t, P * m:P * m + P], ident)
                ins.then_inc(rope_turned, 1)
            pe.wait_ge(rope_out, 4)
            attention(NU0, len(units))
            turn()
            pe.wait_ge(u_out, len(units))
            out_projection()
            turn()
            pe.wait_ge(add_done, 12)
            mark(feature_major([ps[0:NE, 4, 0:S]], NE))
            pe.wait_ge(logits_out, 1)
            for t in range(TT):
                ins = nc.tensor.transpose(ps[:, 5, NE * t:NE * t + NE], logT[:, P * t:P * t + P], ident[0:NE, 0:NE])
            ins.then_inc(logits_turned, 1)
            strict = cst[:, C_STRICT:C_STRICT + P]
            pe.wait_ge(chosen, 1)
            nc.tensor.matmul(ps[:, 6, 0:NE], strict, msk[:, 0, :], start=True, stop=True)
            nc.tensor.matmul(ps[:, 6, NE:2 * NE], strict, msk[:, 1, :], start=True, stop=False)
            nc.tensor.matmul(ps[:, 6, NE:2 * NE], ones[:, :], msk[:, 0, :], start=False, stop=True)
            nc.tensor.matmul(ps[:, 6, 2 * NE:3 * NE], ones[:, :], msk[:, 0, :], start=True, stop=False)
            nc.tensor.matmul(ps[:, 6, 2 * NE:3 * NE], ones[:, :], msk[:, 1, :], start=False, stop=True)\
              .then_inc(ranks, 1)

            def gather():
                for half in range(2):
                    for k in range(4):
                        c = P * (4 * half + k)
                        for t in range(TT):
                            ins = nc.tensor.matmul(ps[:, 1 + 2 * half, P * k:P * k + P], H[:, t, c:c + P], oh[:, t, :],
                                                   start=(t == 0), stop=(t == TT - 1))
                    ins.then_inc(disp, 1)

            def experts(sweep):
                done = sweep * NE
                base = NPRE + done * PER_EXPERT
                n_oh = sweep * 2 * NE
                pe.wait_ge(oh_ready, n_oh + 2)
                if sweep:
                    pe.wait_ge(e_add, 4 * (NE + 1))
                gather()
                if sweep == 0:
                    pe.wait_ge(routed, 1)

                def scatter(i, t):
                    for n in range(2):
                        if t == 0:
                            pe.wait_ge(e_yo, 2 * (i + sweep * (NE + 1)) + n + 1)
                        elif n == 1:
                            pe.wait_ge(e_add, 4 * (i + sweep * (NE + 1)) + 2)
                        nc.tensor.matmul(ps[:, SCATTER_BANKS[2 * t + n], :], ohT[:, P * t:P * t + P],
                                         y_e[:, 512 * n:512 * n + 512], start=True, stop=True).then_inc(e_comb, 1)

                def slot(e, u, kt, n):
                    pe.wait_ge(lo_ready, e * PER_EXPERT + base + u + 1)
                    return shaped(e_whi, u % E_SPLIT, kt, n), shaped(e_wlo, u % E_SPLIT, kt, n)

                def product(e, u0, bank):
                    for half in range(2):
                        hi, lo = slot(e, u0 + half, 4, 512)
                        for kk in range(4):
                            k = 4 * half + kk
                            ins = three(bank, xg_hi[:, k, :], xg_lo[:, k, :], hi[:, kk, :], lo[:, kk, :],
                                        k == 0, k == KT - 1)
                        ins.then_inc(slot_used, 1)

                def turn_hidden(e, j):
                    pe.wait_ge(e_hr, (e + done) * STEPS + j + 1)
                    for m in range(4):
                        ins = nc.tensor.transpose(ps[:, 4, P * m:P * m + P], e_h[:, P * m:P * m + P], ident)
                    ins.then_inc(e_tr, 1)

                def down(e, j, u0):
                    pe.wait_ge(e_lo, (e + done) * STEPS + j + 1)
                    for half in range(2):
                        hi, lo = slot(e, u0 + half, 2, D)
                        for m in range(2):
                            f = 2 * half + m
                            for n in range(2):
                                ns = slice(512 * n, 512 * n + 512)
                                ins = three(ps[:, 5 + n, :], h_hi[:, f, :], h_lo[:, f, :], hi[:, m, ns],
                                            lo[:, m, ns], j == 0 and f == 0, j == STEPS - 1 and f == 3)
                        ins.then_inc(slot_used, 1)

                def expert(e, last):
                    pe.wait_ge(xg_l, 2 * (e + done) + 2)
                    for j in range(STEPS):
                        if j == 2:
                            pe.wait_ge(e_add, (e + sweep * (NE + 1)) * 4 + 4)
                        product(e, gate_end(j) - 2, ps[:, j % 2, :])
                        if j > 0:
                            turn_hidden(e, j - 1)
                        if j == 1:
                            scatter(e, 1)
                        if j == 2:
                            for t in range(TT):
                                ins = nc.tensor.transpose(ps[:, 7, P * t:P * t + P], oh[:, t, :], ident)
                            ins.then_inc(oh_turned, 1)
                        product(e, gate_end(j), ps[:, 2 + j % 2, :])
                        if j == 0:
                            scatter(e, 0)
                        else:
                            down(e, j - 1, gate_end(j) + 2)
                    turn_hidden(e, STEPS - 1)
                    if not last:
                        pe.wait_ge(oh_ready, 2 * e + n_oh + 4)
                        gather()
                    down(e, STEPS - 1, PER_EXPERT - 2)

                with pe.Fori(0, NE - 1) as e:
                    expert(e, False)
                expert(NE - 1, True)
                for t in range(TT):
                    scatter(NE, t)

            experts(0)
            over = pe.value_load(flag[0:1, 0:1], min_val=0, max_val=S)
            with pe.If(over > P):
                experts(1)


_INS = ["x", "mem", "g_mix", "g_ffn", "w_mem_kv", "w_out", "w_in_a", "w_gk_up", "b_gk", "g_gla", "g_kv", "w_kv",
        "w_in_b", "lambda_q1", "lambda_k1", "lambda_q2", "lambda_k2", "g_subln", "w_dense_gate", "w_dense_up",
        "w_dense_down", "w_router", "w_exp_gate", "w_exp_up", "w_exp_down", "g_final"]


def constants(np):
    p = np.arange(P)
    c = np.zeros((P, C_N), np.float32)
    c[:, C_ID:C_ID + P] = np.eye(P)
    c[:, C_IOTA:C_IOTA + S] = np.arange(S)
    c[:, C_STRICT:C_STRICT + P] = p[:, None] < p[None, :]
    c[:, C_CAUSAL:C_CAUSAL + P] = np.where(p[None, :] <= p[:, None], 0.0, NEG)
    c[:, C_GLA:C_GLA + CHUNK] = (p[:, None] % CHUNK) <= np.arange(CHUNK)[None, :]
    half = HEAD_DIM // 2
    inv = (np.float32(10000.0) ** (-np.arange(half, dtype=np.float32) / np.float32(half))).astype(np.float32)
    ang = np.arange(S, dtype=np.float32)[:, None] * inv[None, :]
    for t in range(TT):
        a = ang[P * t:P * t + P].astype(np.float64)
        c[:, C_ROPE + 64 * t:C_ROPE + 64 * t + 32] = np.cos(a)
        c[:, C_ROPE + 64 * t + 32:C_ROPE + 64 * t + 64] = np.sin(a)
    c[:, C_EPS] = EPS
    return c


def kernel(**inputs):
    import numpy as _np
    import concourse.bacc as _bacc
    from concourse import mybir as _mybir
    from concourse.bass_utils import run_bass_kernel_spmd as _run

    nc = _bacc.Bacc("TRN2", target_bir_lowering=False, num_devices=1)
    arrays, args = {}, []
    for name in _INS:
        a = _np.ascontiguousarray(inputs[name])
        arrays[f"in_{name}_dram"] = a
        args.append(nc.dram_tensor(f"in_{name}_dram", a.shape, _mybir.dt.from_np(a.dtype), kind="ExternalInput").ap())
    c = constants(_np)
    arrays["in_consts_dram"] = c
    args.append(nc.dram_tensor("in_consts_dram", c.shape, F32, kind="ExternalInput").ap())
    args.append(nc.dram_tensor("out_0_dram", (1, S, D), F32, kind="ExternalOutput").ap())
    trunk(nc, *args)
    r = _run(nc, [arrays], core_ids=[0])
    return r.results[0]["out_0_dram"]
```
